# Optimizing a Trainium2 kernel written in Bass

```python
import math
import jax
import jax.numpy as jnp
from jax import lax
import numpy as np
import math, functools
import jax, jax.numpy as jnp

D_MODEL = 1024
BATCH = 1
SEQ = 512
DEPTH = 2

GRID_W = 64
CTX_LEN = 256
N_MIXERS = 4
HEAD_DIM = 64
ROPE_THETA = 10000.0
Q_BLOCK = 128
NORM_EPS = 1e-6
NEG_INF = -1e30

DA_HEADS = D_MODEL // (2 * HEAD_DIM)
DA_V_DIM = 2 * HEAD_DIM
SWA_HEADS = D_MODEL // HEAD_DIM
SWA_KV_HEADS = 4
SWA_WINDOW = 128
GA_HEADS = D_MODEL // HEAD_DIM
GA_KV_HEADS = 4
NA_HEADS = D_MODEL // HEAD_DIM
NA_ROWS = 8
NA_COLS = 16
N_GROUPS = 4
EXPERTS_PER_GROUP = 8
N_EXPERTS = N_GROUPS * EXPERTS_PER_GROUP
TOP_K = 2
D_EXPERT = D_MODEL // 2
MOE_BLOCK = 128


def _rmsnorm(x, g):
    xf = x.astype(jnp.float32)
    y = xf * lax.rsqrt(jnp.mean(xf * xf, axis=-1, keepdims=True) + NORM_EPS)
    return (y * g.astype(jnp.float32)).astype(x.dtype)

def _modulate(h, shift, scale):
    return h * (1 + scale) + shift

def _axial_rope_tables(n):
    t = jnp.arange(n, dtype=jnp.int32)
    pos = jnp.stack([t // GRID_W, t % GRID_W], axis=-1).astype(jnp.float32)
    quarter = HEAD_DIM // 4
    inv_freq = 1.0 / (ROPE_THETA ** (jnp.arange(quarter, dtype=jnp.float32) / quarter))
    ang = pos[:, :, None] * inv_freq
    return jnp.cos(ang), jnp.sin(ang)

def _rope(x, cos, sin):
    b, n, hh, d = x.shape
    xr = x.astype(jnp.float32).reshape(b, n, hh, 2, 2, d // 4)
    x1, x2 = xr[..., 0, :], xr[..., 1, :]
    cs, sn = cos[None, :, None], sin[None, :, None]
    out = jnp.stack([x1 * cs - x2 * sn, x2 * cs + x1 * sn], axis=-2)
    return out.reshape(b, n, hh, d).astype(x.dtype)

def _project(t, w, splits):
    b, n, _ = t.shape
    y = t @ w
    outs, off = [], 0
    for nh, dh in splits:
        outs.append(y[..., off:off + nh * dh].reshape(b, n, nh, dh))
        off += nh * dh
    return outs

def _sweep_queries(fn, q):
    b, s = q.shape[:2]
    nb = s // Q_BLOCK
    qb = jnp.swapaxes(q.reshape((b, nb, Q_BLOCK) + q.shape[2:]), 0, 1)
    ob = lax.map(fn, qb)
    return jnp.swapaxes(ob, 0, 1).reshape((b, s) + ob.shape[3:])

def _gqa_attend(q, k, v, sink=None, mask=None):
    b, nq, hq, d = q.shape
    hkv = k.shape[2]
    grp = hq // hkv
    qg = q.reshape(b, nq, hkv, grp, d)
    s = jnp.einsum('bqhgd,bkhd->bhgqk', qg, k).astype(jnp.float32) / math.sqrt(d)
    if mask is not None:
        s = jnp.where(mask, s, NEG_INF)
    if sink is None:
        p = jax.nn.softmax(s, axis=-1)
    else:
        sk = jnp.broadcast_to(sink.astype(jnp.float32).reshape(1, hkv, grp, 1, 1), s.shape[:-1] + (1,))
        p = jax.nn.softmax(jnp.concatenate([s, sk], axis=-1), axis=-1)[..., :-1]
    o = jnp.einsum('bhgqk,bkhd->bqhgd', p.astype(v.dtype), v)
    return o.reshape(b, nq, hq, v.shape[-1])

def _diff_attend(q, k, v, lam):
    s = jnp.einsum('bqhmd,bkhmd->bhmqk', q, k).astype(jnp.float32) / math.sqrt(q.shape[-1])
    p = jax.nn.softmax(s, axis=-1)
    a = p[:, :, 0] - lam * p[:, :, 1]
    return jnp.einsum('bhqk,bkhd->bqhd', a.astype(v.dtype), v)

def _diff_mixer(h, hc, w_qkv, w_o, lam_vecs, subln_g, lam_init, cos, sin, need_ctx):
    b, s, _ = h.shape
    lv = lam_vecs.astype(jnp.float32)
    lam = jnp.exp(jnp.sum(lv[0] * lv[1])) - jnp.exp(jnp.sum(lv[2] * lv[3])) + lam_init
    splits = [(2 * DA_HEADS, HEAD_DIM), (2 * DA_HEADS, HEAD_DIM), (DA_HEADS, DA_V_DIM)]
    q, k, v = _project(h, w_qkv, splits)
    qc, kc, vc = _project(hc, w_qkv, splits)
    q = _rope(q, cos, sin).reshape(b, s, DA_HEADS, 2, HEAD_DIM)
    k = _rope(k, cos, sin).reshape(b, s, DA_HEADS, 2, HEAD_DIM)
    kc = kc.reshape(b, -1, DA_HEADS, 2, HEAD_DIM)
    k_all = jnp.concatenate([kc, k], axis=1)
    v_all = jnp.concatenate([vc, v], axis=1)

    def out_proj(o):
        o = _rmsnorm(o, subln_g) * (1.0 - lam_init)
        return o.reshape(o.shape[0], o.shape[1], -1) @ w_o

    y = out_proj(_sweep_queries(lambda qb: _diff_attend(qb, k_all, v_all, lam), q))
    if not need_ctx:
        return y, None
    qc = qc.reshape(b, -1, DA_HEADS, 2, HEAD_DIM)
    return y, out_proj(_diff_attend(qc, kc, vc, lam))

def _swa_mixer(h, hc, w_qkv, w_o, sink, cos, sin, need_ctx):
    b, s, _ = h.shape
    n_ctx = hc.shape[1]
    nb = s // Q_BLOCK
    splits = [(SWA_HEADS, HEAD_DIM), (SWA_KV_HEADS, HEAD_DIM), (SWA_KV_HEADS, HEAD_DIM)]
    q, k, v = _project(h, w_qkv, splits)
    qc, kc, vc = _project(hc, w_qkv, splits)
    q, k = _rope(q, cos, sin), _rope(k, cos, sin)

    def band(t):
        tb = t.reshape((b, nb, Q_BLOCK) + t.shape[2:])
        tp = jnp.pad(tb, [(0, 0), (1, 1)] + [(0, 0)] * (tb.ndim - 2))
        tband = jnp.concatenate([tp[:, :-2], tp[:, 1:-1], tp[:, 2:]], axis=2)
        return jnp.swapaxes(tband, 0, 1)

    kb, vb = band(k), band(v)
    qb = jnp.swapaxes(q.reshape(b, nb, Q_BLOCK, SWA_HEADS, HEAD_DIM), 0, 1)
    qi = jnp.arange(Q_BLOCK)[:, None]
    kj = jnp.arange(3 * Q_BLOCK)[None, :]
    in_window = jnp.abs(kj - Q_BLOCK - qi) <= SWA_WINDOW
    ctx_ok = jnp.ones((Q_BLOCK, n_ctx), dtype=bool)

    def block(args):
        q_blk, k_blk, v_blk, bi = args
        kpos = bi * Q_BLOCK - Q_BLOCK + kj
        valid = in_window & (kpos >= 0) & (kpos < s)
        mask = jnp.concatenate([ctx_ok, valid], axis=-1)
        k_all = jnp.concatenate([kc, k_blk], axis=1)
        v_all = jnp.concatenate([vc, v_blk], axis=1)
        return _gqa_attend(q_blk, k_all, v_all, sink, mask)

    o = lax.map(block, (qb, kb, vb, jnp.arange(nb)))
    y = jnp.swapaxes(o, 0, 1).reshape(b, s, -1) @ w_o
    if not need_ctx:
        return y, None
    return y, _gqa_attend(qc, kc, vc, sink).reshape(b, n_ctx, -1) @ w_o

def _axial_gqa_mixer(h, hc, w_qkv, w_o, qk_g, cos, sin, need_ctx):
    b, s, _ = h.shape
    n_ctx = hc.shape[1]
    splits = [(GA_HEADS, HEAD_DIM), (GA_KV_HEADS, HEAD_DIM), (GA_KV_HEADS, HEAD_DIM)]
    q, k, v = _project(h, w_qkv, splits)
    qc, kc, vc = _project(hc, w_qkv, splits)
    q, k = _rmsnorm(q, qk_g[0]), _rmsnorm(k, qk_g[1])
    qc, kc = _rmsnorm(qc, qk_g[0]), _rmsnorm(kc, qk_g[1])
    q, k = _rope(q, cos, sin), _rope(k, cos, sin)
    k_all = jnp.concatenate([kc, k], axis=1)
    v_all = jnp.concatenate([vc, v], axis=1)
    o = _sweep_queries(lambda qb: _gqa_attend(qb, k_all, v_all), q)
    y = o.reshape(b, s, -1) @ w_o
    if not need_ctx:
        return y, None
    return y, _gqa_attend(qc, kc, vc).reshape(b, n_ctx, -1) @ w_o

def _na_mixer(h, hc, w_qkv, w_o, rpb, need_ctx):
    b, s, _ = h.shape
    n_ctx = hc.shape[1]
    rows = s // GRID_W
    kh = min(NA_ROWS, rows)
    splits = [(NA_HEADS, HEAD_DIM)] * 3
    q, k, v = _project(h, w_qkv, splits)
    qc, kc, vc = _project(hc, w_qkv, splits)
    q_g = q.reshape(b, rows, GRID_W, NA_HEADS, HEAD_DIM)
    k_g = k.reshape(b, rows, GRID_W, NA_HEADS, HEAD_DIM)
    v_g = v.reshape(b, rows, GRID_W, NA_HEADS, HEAD_DIM)
    cols = np.arange(GRID_W)
    col_idx = np.clip(cols - NA_COLS // 2, 0, GRID_W - NA_COLS)[:, None] + np.arange(NA_COLS)[None, :]
    dc_idx = col_idx - cols[:, None] + (NA_COLS - 1)
    bias_c = rpb.astype(jnp.float32)[:, :, dc_idx]
    scale = 1.0 / math.sqrt(HEAD_DIM)
    n_nb = kh * NA_COLS

    def row_step(args):
        q_r, r = args
        r0 = jnp.clip(r - kh // 2, 0, rows - kh)
        k_r = lax.dynamic_slice_in_dim(k_g, r0, kh, axis=1)[:, :, col_idx]
        v_r = lax.dynamic_slice_in_dim(v_g, r0, kh, axis=1)[:, :, col_idx]
        dr_idx = r0 + jnp.arange(kh) - r + (NA_ROWS - 1)
        bias = jnp.take(bias_c, dr_idx, axis=1).transpose(0, 2, 1, 3)
        s_nb = jnp.einsum('bchd,bkcwhd->bhckw', q_r, k_r).astype(jnp.float32) * scale + bias[None]
        s_cx = jnp.einsum('bchd,bnhd->bhcn', q_r, kc).astype(jnp.float32) * scale
        logits = jnp.concatenate([s_nb.reshape(b, NA_HEADS, GRID_W, n_nb), s_cx], axis=-1)
        p = jax.nn.softmax(logits, axis=-1).astype(v.dtype)
        p_nb = p[..., :n_nb].reshape(b, NA_HEADS, GRID_W, kh, NA_COLS)
        return (jnp.einsum('bhckw,bkcwhd->bchd', p_nb, v_r)
                + jnp.einsum('bhcn,bnhd->bchd', p[..., n_nb:], vc))

    o = lax.map(row_step, (jnp.swapaxes(q_g, 0, 1), jnp.arange(rows)))
    y = jnp.swapaxes(o, 0, 1).reshape(b, s, -1) @ w_o
    if not need_ctx:
        return y, None
    return y, _gqa_attend(qc, kc, vc).reshape(b, n_ctx, -1) @ w_o

def _hier_moe(t, wr_g, br_g, wr_e, br_e, w_gate, w_up, w_down):
    n_tok, d = t.shape
    lg = (t @ wr_g).astype(jnp.float32) + br_g.astype(jnp.float32)
    pg = jax.nn.softmax(lg, axis=-1)
    g = jnp.argmax(lg, axis=-1)
    gate_g = jnp.take_along_axis(pg, g[:, None], axis=1)
    le = ((t @ wr_e).astype(jnp.float32) + br_e.astype(jnp.float32)).reshape(n_tok, N_GROUPS, EXPERTS_PER_GROUP)
    le_g = jnp.take_along_axis(le, g[:, None, None], axis=1)[:, 0]
    top_v, top_i = lax.top_k(le_g, TOP_K)
    weights = (gate_g * jax.nn.softmax(top_v, axis=-1)).reshape(-1)
    expert = (g[:, None] * EXPERTS_PER_GROUP + top_i).reshape(-1)
    tok = jnp.repeat(jnp.arange(n_tok, dtype=jnp.int32), TOP_K)
    n_assign = n_tok * TOP_K
    order = jnp.argsort(expert, stable=True)
    e_sorted = expert[order]
    counts = jax.ops.segment_sum(jnp.ones_like(expert), expert, num_segments=N_EXPERTS)
    padded = (counts + MOE_BLOCK - 1) // MOE_BLOCK * MOE_BLOCK
    p_end = jnp.cumsum(padded)
    p_start = p_end - padded
    start = jnp.cumsum(counts) - counts
    dest = p_start[e_sorted] + jnp.arange(n_assign) - start[e_sorted]
    cap = -(-n_assign // MOE_BLOCK) * MOE_BLOCK + N_EXPERTS * MOE_BLOCK
    n_blk = cap // MOE_BLOCK
    buf_tok = jnp.full((cap,), n_tok, jnp.int32).at[dest].set(tok[order])
    buf_w = jnp.zeros((cap,), jnp.float32).at[dest].set(weights[order])
    blk_e = jnp.clip(jnp.searchsorted(p_end, jnp.arange(n_blk) * MOE_BLOCK, side='right'), 0, N_EXPERTS - 1)
    t_pad = jnp.concatenate([t, jnp.zeros((1, d), t.dtype)], axis=0)
    xb = t_pad[buf_tok].reshape(n_blk, MOE_BLOCK, d)

    def expert_block(args):
        x_blk, e = args
        hidden = jax.nn.silu(x_blk @ w_gate[e]) * (x_blk @ w_up[e])
        return hidden @ w_down[e]

    yb = lax.map(expert_block, (xb, blk_e)).reshape(cap, d)
    out = jnp.zeros((n_tok + 1, d), t.dtype).at[buf_tok].add(yb * buf_w[:, None].astype(yb.dtype))
    return out[:n_tok]

def _n_layers_of(m):
    return len(range(m, DEPTH, N_MIXERS))

def first_inputs(seed: int = 0) -> dict:
    key = jax.random.key(seed)
    keys = iter(jax.random.split(key, 64))

    def nrm(shape, std):
        return std * jax.random.normal(next(keys), shape, jnp.float32)

    D = D_MODEL
    n_a, n_b, n_c, n_d = (_n_layers_of(m) for m in range(N_MIXERS))
    a_cols = 4 * DA_HEADS * HEAD_DIM + DA_HEADS * DA_V_DIM
    b_cols = (SWA_HEADS + 2 * SWA_KV_HEADS) * HEAD_DIM
    c_cols = (GA_HEADS + 2 * GA_KV_HEADS) * HEAD_DIM
    d_cols = 3 * NA_HEADS * HEAD_DIM
    return {
        'x': nrm((BATCH, SEQ, D), 1.0),
        'c': nrm((BATCH, D), 1.0),
        'ctx': nrm((BATCH, CTX_LEN, D), 1.0),
        'c_ctx': nrm((D,), 1.0),
        'mod_w': nrm((DEPTH, D, 6 * D), 0.5 / math.sqrt(D)),
        'mod_b': nrm((DEPTH, 6 * D), 0.02),
        'norm1_g': 1.0 + nrm((DEPTH, D), 0.02),
        'norm2_g': 1.0 + nrm((DEPTH, D), 0.02),
        'a_w_qkv': nrm((n_a, D, a_cols), D ** -0.5),
        'a_w_o': nrm((n_a, DA_HEADS * DA_V_DIM, D), (DA_HEADS * DA_V_DIM) ** -0.5),
        'a_lam': nrm((n_a, 4, HEAD_DIM), 0.1),
        'a_subln_g': 1.0 + nrm((n_a, DA_V_DIM), 0.02),
        'b_w_qkv': nrm((n_b, D, b_cols), D ** -0.5),
        'b_w_o': nrm((n_b, SWA_HEADS * HEAD_DIM, D), (SWA_HEADS * HEAD_DIM) ** -0.5),
        'b_sink': nrm((n_b, SWA_HEADS), 0.5),
        'c_w_qkv': nrm((n_c, D, c_cols), D ** -0.5),
        'c_w_o': nrm((n_c, GA_HEADS * HEAD_DIM, D), (GA_HEADS * HEAD_DIM) ** -0.5),
        'c_qk_norm_g': 1.0 + nrm((n_c, 2, HEAD_DIM), 0.02),
        'd_w_qkv': nrm((n_d, D, d_cols), D ** -0.5),
        'd_w_o': nrm((n_d, NA_HEADS * HEAD_DIM, D), (NA_HEADS * HEAD_DIM) ** -0.5),
        'd_rpb': nrm((n_d, NA_HEADS, 2 * NA_ROWS - 1, 2 * NA_COLS - 1), 0.1),
        'moe_router_g': nrm((DEPTH, D, N_GROUPS), D ** -0.5),
        'moe_router_g_b': nrm((DEPTH, N_GROUPS), 0.01),
        'moe_router_e': nrm((DEPTH, D, N_EXPERTS), D ** -0.5),
        'moe_router_e_b': nrm((DEPTH, N_EXPERTS), 0.01),
        'moe_w_gate': nrm((DEPTH, N_EXPERTS, D, D_EXPERT), D ** -0.5),
        'moe_w_up': nrm((DEPTH, N_EXPERTS, D, D_EXPERT), D ** -0.5),
        'moe_w_down': nrm((DEPTH, N_EXPERTS, D_EXPERT, D), D_EXPERT ** -0.5),
        'final_g': 1.0 + nrm((D,), 0.02),
    }

def first_block(x, c, ctx, c_ctx, mod_w, mod_b, norm1_g, norm2_g,
              a_w_qkv, a_w_o, a_lam, a_subln_g,
              b_w_qkv, b_w_o, b_sink,
              c_w_qkv, c_w_o, c_qk_norm_g,
              d_w_qkv, d_w_o, d_rpb,
              moe_router_g, moe_router_g_b, moe_router_e, moe_router_e_b,
              moe_w_gate, moe_w_up, moe_w_down, final_g):
    b, s, d = x.shape
    n_ctx = ctx.shape[1]
    cos, sin = _axial_rope_tables(s)
    xc = ctx
    for i in range(DEPTH):
        m, j = i % N_MIXERS, i // N_MIXERS
        need_ctx = i < DEPTH - 1
        mod = jax.nn.silu(c) @ mod_w[i] + mod_b[i]
        sh1, sc1, g1, sh2, sc2, g2 = jnp.split(mod[:, None, :], 6, axis=-1)
        mod_c = jax.nn.silu(c_ctx) @ mod_w[i] + mod_b[i]
        shc1, scc1, gc1, shc2, scc2, gc2 = jnp.split(mod_c, 6)
        h = _modulate(_rmsnorm(x, norm1_g[i]), sh1, sc1)
        hc = _modulate(_rmsnorm(xc, norm1_g[i]), shc1, scc1)
        if m == 0:
            lam_init = 0.8 - 0.6 * math.exp(-0.3 * i)
            y, yc = _diff_mixer(h, hc, a_w_qkv[j], a_w_o[j], a_lam[j], a_subln_g[j], lam_init, cos, sin, need_ctx)
        elif m == 1:
            y, yc = _swa_mixer(h, hc, b_w_qkv[j], b_w_o[j], b_sink[j], cos, sin, need_ctx)
        elif m == 2:
            y, yc = _axial_gqa_mixer(h, hc, c_w_qkv[j], c_w_o[j], c_qk_norm_g[j], cos, sin, need_ctx)
        else:
            y, yc = _na_mixer(h, hc, d_w_qkv[j], d_w_o[j], d_rpb[j], need_ctx)
        x = x + g1 * y
        h2 = _modulate(_rmsnorm(x, norm2_g[i]), sh2, sc2).reshape(b * s, d)
        if need_ctx:
            xc = xc + gc1 * yc
            h2c = _modulate(_rmsnorm(xc, norm2_g[i]), shc2, scc2).reshape(b * n_ctx, d)
            tokens = jnp.concatenate([h2, h2c], axis=0)
        else:
            tokens = h2
        f = _hier_moe(tokens, moe_router_g[i], moe_router_g_b[i], moe_router_e[i], moe_router_e_b[i],
                      moe_w_gate[i], moe_w_up[i], moe_w_down[i])
        x = x + g2 * f[:b * s].reshape(b, s, d)
        if need_ctx:
            xc = xc + gc2 * f[b * s:].reshape(b, n_ctx, d)
    return _rmsnorm(x, final_g)


DEPTH_2 = 1

N_MIX_HEADS = D_MODEL // HEAD_DIM
HEADS_PER_MIXER = N_MIX_HEADS // 4
GROUP_WIDTH = HEADS_PER_MIXER * HEAD_DIM
MOBA_BLOCK = 256
MOBA_TOPK = 3
MLA_Q_RANK = D_MODEL // 4
MLA_KV_RANK = D_MODEL // 8
MLA_NOPE = HEAD_DIM
MLA_ROPE = HEAD_DIM // 2
MLA_V = HEAD_DIM
DILATED_BRANCHES = ((128, 1), (512, 4), (2048, 16))
SWA_KV_HEADS_2 = 2
SWA_KV_WIDTH = SWA_KV_HEADS_2 * HEAD_DIM
D_FF = 4 * D_MODEL
EPS = 1e-6
NEG = -1e30
COL_WIDTHS = (GROUP_WIDTH, GROUP_WIDTH, GROUP_WIDTH,
              MLA_Q_RANK, MLA_KV_RANK, MLA_ROPE,
              GROUP_WIDTH, GROUP_WIDTH, GROUP_WIDTH,
              GROUP_WIDTH, SWA_KV_WIDTH, SWA_KV_WIDTH)
IN_COLS = sum(COL_WIDTHS)


def rms_norm(x, g):
    xf = x.astype(jnp.float32)
    y = xf * lax.rsqrt(jnp.mean(xf * xf, axis=-1, keepdims=True) + EPS)
    return (y * g.astype(jnp.float32)).astype(x.dtype)

def split_columns(h):
    parts, off = [], 0
    for wdt in COL_WIDTHS:
        parts.append(h[..., off:off + wdt])
        off += wdt
    return parts

def alibi_slopes():
    n = 3 * HEADS_PER_MIXER
    idx = np.arange(1, n + 1, dtype=np.float32).reshape(HEADS_PER_MIXER, 3)
    s = jnp.asarray(np.exp2(-8.0 * idx / n), dtype=jnp.float32)
    return s[:, 0], s[:, 1], s[:, 2]

def rope_tables(S):
    inv = 1.0 / (ROPE_THETA ** (jnp.arange(0, MLA_ROPE, 2, dtype=jnp.float32) / MLA_ROPE))
    ang = jnp.arange(S, dtype=jnp.float32)[:, None] * inv[None, :]
    return jnp.cos(ang), jnp.sin(ang)

def apply_rope(x, cos, sin):
    x1, x2 = jnp.split(x.astype(jnp.float32), 2, axis=-1)
    c, s = cos[None, :, None, :], sin[None, :, None, :]
    return jnp.concatenate([x1 * c - x2 * s, x1 * s + x2 * c], axis=-1).astype(x.dtype)

def moba_attention(q, k, v, slopes):
    B, H, S, dh = q.shape
    nb = -(-S // MOBA_BLOCK)
    Sp = nb * MOBA_BLOCK
    topk = min(MOBA_TOPK, nb)
    pad = ((0, 0), (0, 0), (0, Sp - S), (0, 0))
    qp, kp, vp = jnp.pad(q, pad), jnp.pad(k, pad), jnp.pad(v, pad)
    kb = kp.reshape(B, H, nb, MOBA_BLOCK, dh)
    vb = vp.reshape(B, H, nb, MOBA_BLOCK, dh)
    kmean = jnp.mean(kb.astype(jnp.float32), axis=3)
    scale = dh ** -0.5
    bi = jnp.arange(B)[:, None, None, None]
    hi = jnp.arange(H)[None, :, None, None]
    slope_b = slopes.astype(jnp.float32)

    def chunk(c):
        t0 = c * Q_BLOCK
        qc = lax.dynamic_slice_in_dim(qp, t0, Q_BLOCK, axis=2)
        tpos = t0 + jnp.arange(Q_BLOCK)
        qblk = tpos // MOBA_BLOCK
        own = t0 // MOBA_BLOCK
        gate = jnp.einsum('bhqd,bhnd->bhqn', qc.astype(jnp.float32), kmean)
        past = jnp.arange(nb)[None, :] < qblk[:, None]
        gate = jnp.where(past, gate, NEG)
        _, sel = lax.top_k(gate, topk)
        sel_ok = sel < qblk[:, None]
        ksel = kb[bi, hi, sel]
        vsel = vb[bi, hi, sel]
        kpos_sel = sel[..., None] * MOBA_BLOCK + jnp.arange(MOBA_BLOCK)
        dist_sel = (tpos[:, None, None] - kpos_sel).astype(jnp.float32)
        s_sel = (jnp.einsum('bhqd,bhqjkd->bhqjk', qc, ksel).astype(jnp.float32) * scale
                 - slope_b[None, :, None, None, None] * dist_sel)
        s_sel = jnp.where(sel_ok[..., None], s_sel, NEG).reshape(B, H, Q_BLOCK, topk * MOBA_BLOCK)
        kown = lax.dynamic_slice_in_dim(kb, own, 1, axis=2)[:, :, 0]
        vown = lax.dynamic_slice_in_dim(vb, own, 1, axis=2)[:, :, 0]
        dist_own = tpos[:, None] - (own * MOBA_BLOCK + jnp.arange(MOBA_BLOCK))[None, :]
        s_own = (jnp.einsum('bhqd,bhkd->bhqk', qc, kown).astype(jnp.float32) * scale
                 - slope_b[None, :, None, None] * dist_own.astype(jnp.float32))
        s_own = jnp.where(dist_own >= 0, s_own, NEG)
        p = jax.nn.softmax(jnp.concatenate([s_sel, s_own], axis=-1), axis=-1)
        p_sel = p[..., :topk * MOBA_BLOCK].reshape(B, H, Q_BLOCK, topk, MOBA_BLOCK)
        p_own = p[..., topk * MOBA_BLOCK:]
        return (jnp.einsum('bhqjk,bhqjkd->bhqd', p_sel.astype(v.dtype), vsel)
                + jnp.einsum('bhqk,bhkd->bhqd', p_own.astype(v.dtype), vown))

    out = lax.map(chunk, jnp.arange(Sp // Q_BLOCK))
    return out.transpose(1, 2, 0, 3, 4).reshape(B, H, Sp, dh)[:, :, :S]

def causal_dense_attention(q, k, v, scale):
    B, H, S, _ = q.shape
    kpos = jnp.arange(S)

    def blk(c):
        qc = lax.dynamic_slice_in_dim(q, c * Q_BLOCK, Q_BLOCK, axis=2)
        s = jnp.einsum('bhqd,bhkd->bhqk', qc, k).astype(jnp.float32) * scale
        tpos = c * Q_BLOCK + jnp.arange(Q_BLOCK)
        s = jnp.where(kpos[None, :] <= tpos[:, None], s, NEG)
        p = jax.nn.softmax(s, axis=-1)
        return jnp.einsum('bhqk,bhkd->bhqd', p.astype(v.dtype), v)

    out = lax.map(blk, jnp.arange(S // Q_BLOCK))
    return out.transpose(1, 2, 0, 3, 4).reshape(B, H, S, -1)

def mla_attention(q_lat, kv_lat, k_rope, g_qlat, g_kvlat, w_uq, w_ukv, g_q, g_k):
    B, S, _ = q_lat.shape
    H = HEADS_PER_MIXER
    qk_dim = MLA_NOPE + MLA_ROPE
    q = (rms_norm(q_lat, g_qlat) @ w_uq).reshape(B, S, H, qk_dim)
    kv = (rms_norm(kv_lat, g_kvlat) @ w_ukv).reshape(B, S, H, MLA_NOPE + MLA_V)
    k_nope, v = kv[..., :MLA_NOPE], kv[..., MLA_NOPE:]
    k = jnp.concatenate([k_nope, jnp.broadcast_to(k_rope[:, :, None, :], (B, S, H, MLA_ROPE))], axis=-1)
    q, k = rms_norm(q, g_q), rms_norm(k, g_k)
    cos, sin = rope_tables(S)
    q = jnp.concatenate([q[..., :MLA_NOPE], apply_rope(q[..., MLA_NOPE:], cos, sin)], axis=-1)
    k = jnp.concatenate([k[..., :MLA_NOPE], apply_rope(k[..., MLA_NOPE:], cos, sin)], axis=-1)
    t = lambda a: a.transpose(0, 2, 1, 3)
    return causal_dense_attention(t(q), t(k), t(v), qk_dim ** -0.5)

def dilated_branch(q, k, v, slopes, window, dilation):
    B, H, S, dh = q.shape
    span = dilation * Q_BLOCK
    Sp = -(-S // span) * span
    L = Sp // dilation
    nb = L // Q_BLOCK
    steps = window // dilation

    def to_sub(t):
        t = jnp.pad(t, ((0, 0), (0, 0), (0, Sp - S), (0, 0)))
        return t.reshape(B, H, L, dilation, dh).transpose(0, 1, 3, 2, 4).reshape(B, H, dilation, nb, Q_BLOCK, dh)

    def with_prev(t):
        prev = jnp.pad(t, ((0, 0), (0, 0), (0, 0), (1, 0), (0, 0), (0, 0)))[:, :, :, :-1]
        return jnp.concatenate([prev, t], axis=4)

    qs = to_sub(q)
    kk, vv = with_prev(to_sub(k)), with_prev(to_sub(v))
    qi = jnp.arange(Q_BLOCK)[:, None]
    kidx = jnp.arange(2 * Q_BLOCK)[None, :]
    rel = qi + Q_BLOCK - kidx
    blk = jnp.arange(nb)[:, None, None]
    valid = (rel >= 0) & (rel <= steps) & (blk * Q_BLOCK + kidx[None] - Q_BLOCK >= 0)
    s = (jnp.einsum('bhrnqd,bhrnkd->bhrnqk', qs, kk).astype(jnp.float32) * (dh ** -0.5)
         - slopes.astype(jnp.float32)[None, :, None, None, None, None] * (dilation * rel).astype(jnp.float32))
    s = jnp.where(valid, s, NEG)
    m = jnp.max(s, axis=-1, keepdims=True)
    e = jnp.exp(s - m)
    l = jnp.sum(e, axis=-1, keepdims=True)
    o = jnp.einsum('bhrnqk,bhrnkd->bhrnqd', e, vv.astype(jnp.float32))
    back = lambda t: t.reshape(B, H, dilation, L, -1).transpose(0, 1, 3, 2, 4).reshape(B, H, Sp, -1)[:, :, :S]
    return back(o), back(m), back(l)

def dilated_mixture(q, k, v, slopes):
    branches = [dilated_branch(q, k, v, slopes, w, d) for (w, d) in DILATED_BRANCHES]
    M = functools.reduce(jnp.maximum, [b[1] for b in branches])
    num = jnp.zeros(q.shape, jnp.float32)
    den = jnp.zeros(q.shape[:-1] + (1,), jnp.float32)
    for o, m, l in branches:
        w = jnp.exp(m - M)
        num = num + w * o
        den = den + w * l
    return (num / den).astype(q.dtype)

def swa_sink_attention(q, k, v, sinks, slopes):
    B, H, S, dh = q.shape
    G = H // SWA_KV_HEADS_2
    nb = S // Q_BLOCK
    qb = q.reshape(B, SWA_KV_HEADS_2, G, nb, Q_BLOCK, dh)

    def with_prev(t):
        t = t.reshape(B, SWA_KV_HEADS_2, nb, Q_BLOCK, dh)
        prev = jnp.pad(t, ((0, 0), (0, 0), (1, 0), (0, 0), (0, 0)))[:, :, :-1]
        return jnp.concatenate([prev, t], axis=3)

    kk, vv = with_prev(k), with_prev(v)
    qi = jnp.arange(Q_BLOCK)[:, None]
    kidx = jnp.arange(2 * Q_BLOCK)[None, :]
    rel = qi + Q_BLOCK - kidx
    blk = jnp.arange(nb)[:, None, None]
    valid = (rel >= 0) & (rel < SWA_WINDOW) & (blk * Q_BLOCK + kidx[None] - Q_BLOCK >= 0)
    sl = slopes.astype(jnp.float32).reshape(SWA_KV_HEADS_2, G)[None, :, :, None, None, None]
    s = jnp.einsum('bkgnqd,bkncd->bkgnqc', qb, kk).astype(jnp.float32) * (dh ** -0.5) - sl * rel.astype(jnp.float32)
    s = jnp.where(valid, s, NEG)
    sink = jnp.broadcast_to(sinks.astype(jnp.float32).reshape(SWA_KV_HEADS_2, G)[None, :, :, None, None, None],
                            s.shape[:-1] + (1,))
    p = jax.nn.softmax(jnp.concatenate([s, sink], axis=-1), axis=-1)[..., :-1]
    o = jnp.einsum('bkgnqc,bkncd->bkgnqd', p.astype(v.dtype), vv)
    return o.reshape(B, H, S, dh)

def hybrid_layer(x, attn_norm_g, w_in, moba_q_g, moba_k_g, mla_qlat_g, mla_kvlat_g,
                 mla_w_uq, mla_w_ukv, mla_q_g, mla_k_g, dil_q_g, dil_k_g, swa_q_g, swa_k_g,
                 swa_sinks, group_out_g, w_o, mlp_norm_g, w_up, w_down):
    B, S, _ = x.shape
    H = HEADS_PER_MIXER
    slope_a, slope_c, slope_d = alibi_slopes()
    h = rms_norm(x, attn_norm_g) @ w_in
    a_q, a_k, a_v, b_ql, b_kvl, b_kr, c_q, c_k, c_v, d_q, d_k, d_v = split_columns(h)
    heads = lambda t, n: t.reshape(B, S, n, HEAD_DIM)
    tr = lambda t: t.transpose(0, 2, 1, 3)
    oa = moba_attention(tr(rms_norm(heads(a_q, H), moba_q_g)), tr(rms_norm(heads(a_k, H), moba_k_g)),
                        tr(heads(a_v, H)), slope_a)
    ob = mla_attention(b_ql, b_kvl, b_kr, mla_qlat_g, mla_kvlat_g, mla_w_uq, mla_w_ukv, mla_q_g, mla_k_g)
    oc = dilated_mixture(tr(rms_norm(heads(c_q, H), dil_q_g)), tr(rms_norm(heads(c_k, H), dil_k_g)),
                         tr(heads(c_v, H)), slope_c)
    od = swa_sink_attention(tr(rms_norm(heads(d_q, H), swa_q_g)),
                            tr(rms_norm(heads(d_k, SWA_KV_HEADS_2), swa_k_g)),
                            tr(heads(d_v, SWA_KV_HEADS_2)), swa_sinks, slope_d)
    groups = [tr(o).reshape(B, S, GROUP_WIDTH) for o in (oa, ob, oc, od)]
    mixed = jnp.concatenate([rms_norm(gr, group_out_g[i]) for i, gr in enumerate(groups)], axis=-1)
    x = x + mixed @ w_o
    u = jax.nn.relu(rms_norm(x, mlp_norm_g) @ w_up)
    return x + (u * u) @ w_down

def second_inputs(seed: int = 0) -> dict:
    key = jax.random.key(seed)
    ks = jax.random.split(key, 24)
    f = jnp.float32
    H = HEADS_PER_MIXER
    w = lambda k, shape, fan_in: jax.random.normal(k, shape, f) * (fan_in ** -0.5)
    g = lambda k, shape: 1.0 + 0.02 * jax.random.normal(k, shape, f)
    return {
        "x": jax.random.normal(ks[0], (BATCH, SEQ, D_MODEL), f),
        "attn_norm_g": g(ks[1], (DEPTH_2, D_MODEL)),
        "w_in": w(ks[2], (DEPTH_2, D_MODEL, IN_COLS), D_MODEL),
        "moba_q_g": g(ks[3], (DEPTH_2, HEAD_DIM)),
        "moba_k_g": g(ks[4], (DEPTH_2, HEAD_DIM)),
        "mla_qlat_g": g(ks[5], (DEPTH_2, MLA_Q_RANK)),
        "mla_kvlat_g": g(ks[6], (DEPTH_2, MLA_KV_RANK)),
        "mla_w_uq": w(ks[7], (DEPTH_2, MLA_Q_RANK, H * (MLA_NOPE + MLA_ROPE)), MLA_Q_RANK),
        "mla_w_ukv": w(ks[8], (DEPTH_2, MLA_KV_RANK, H * (MLA_NOPE + MLA_V)), MLA_KV_RANK),
        "mla_q_g": g(ks[9], (DEPTH_2, MLA_NOPE + MLA_ROPE)),
        "mla_k_g": g(ks[10], (DEPTH_2, MLA_NOPE + MLA_ROPE)),
        "dil_q_g": g(ks[11], (DEPTH_2, HEAD_DIM)),
        "dil_k_g": g(ks[12], (DEPTH_2, HEAD_DIM)),
        "swa_q_g": g(ks[13], (DEPTH_2, HEAD_DIM)),
        "swa_k_g": g(ks[14], (DEPTH_2, HEAD_DIM)),
        "swa_sinks": 0.5 * jax.random.normal(ks[15], (DEPTH_2, H), f),
        "group_out_g": g(ks[16], (DEPTH_2, 4, GROUP_WIDTH)),
        "w_o": w(ks[17], (DEPTH_2, D_MODEL, D_MODEL), D_MODEL),
        "mlp_norm_g": g(ks[18], (DEPTH_2, D_MODEL)),
        "w_up": w(ks[19], (DEPTH_2, D_MODEL, D_FF), D_MODEL),
        "w_down": w(ks[20], (DEPTH_2, D_FF, D_MODEL), D_FF),
    }

def second_block(x, attn_norm_g, w_in, moba_q_g, moba_k_g, mla_qlat_g, mla_kvlat_g, mla_w_uq,
              mla_w_ukv, mla_q_g, mla_k_g, dil_q_g, dil_k_g, swa_q_g, swa_k_g, swa_sinks,
              group_out_g, w_o, mlp_norm_g, w_up, w_down):
    for l in range(DEPTH_2):
        x = hybrid_layer(x, attn_norm_g[l], w_in[l], moba_q_g[l], moba_k_g[l], mla_qlat_g[l],
                         mla_kvlat_g[l], mla_w_uq[l], mla_w_ukv[l], mla_q_g[l], mla_k_g[l],
                         dil_q_g[l], dil_k_g[l], swa_q_g[l], swa_k_g[l], swa_sinks[l],
                         group_out_g[l], w_o[l], mlp_norm_g[l], w_up[l], w_down[l])
    return x


def setup_inputs(seed=0):
    out = dict(first_inputs(seed))
    for name, value in second_inputs(seed + 1).items():
        if name != "x":
            out[name + "_2"] = value
    return out


def reference(
    x, c, ctx, c_ctx, mod_w, mod_b, norm1_g, norm2_g, a_w_qkv, a_w_o, a_lam, a_subln_g, b_w_qkv,
    b_w_o, b_sink, c_w_qkv, c_w_o, c_qk_norm_g, d_w_qkv, d_w_o, d_rpb, moe_router_g,
    moe_router_g_b, moe_router_e, moe_router_e_b, moe_w_gate, moe_w_up, moe_w_down, final_g,
    attn_norm_g_2, w_in_2, moba_q_g_2, moba_k_g_2, mla_qlat_g_2, mla_kvlat_g_2, mla_w_uq_2,
    mla_w_ukv_2, mla_q_g_2, mla_k_g_2, dil_q_g_2, dil_k_g_2, swa_q_g_2, swa_k_g_2, swa_sinks_2,
    group_out_g_2, w_o_2, mlp_norm_g_2, w_up_2, w_down_2,
):
    x = first_block(
        x, c, ctx, c_ctx, mod_w, mod_b, norm1_g, norm2_g, a_w_qkv, a_w_o, a_lam, a_subln_g,
        b_w_qkv, b_w_o, b_sink, c_w_qkv, c_w_o, c_qk_norm_g, d_w_qkv, d_w_o, d_rpb,
        moe_router_g, moe_router_g_b, moe_router_e, moe_router_e_b, moe_w_gate, moe_w_up,
        moe_w_down, final_g,
    )
    return second_block(
        x, attn_norm_g_2, w_in_2, moba_q_g_2, moba_k_g_2, mla_qlat_g_2, mla_kvlat_g_2,
        mla_w_uq_2, mla_w_ukv_2, mla_q_g_2, mla_k_g_2, dil_q_g_2, dil_k_g_2, swa_q_g_2,
        swa_k_g_2, swa_sinks_2, group_out_g_2, w_o_2, mlp_norm_g_2, w_up_2, w_down_2,
    )


_drawn_inputs = setup_inputs


def setup_inputs(seed=0):
    import zlib

    import numpy as np

    out = dict(_drawn_inputs(seed))
    spreads = {}
    factors = {'norm1_g': 5.55,
     'norm2_g': 3.397,
     'a_subln_g': 3.884,
     'b_sink': 8.0,
     'moe_router_g_b': 4.532,
     'moe_router_e_b': 7.262,
     'attn_norm_g_2': 2.968,
     'moba_q_g_2': 8.0,
     'moba_k_g_2': 8.0,
     'mla_qlat_g_2': 8.0,
     'mla_kvlat_g_2': 6.88,
     'mla_q_g_2': 8.0,
     'mla_k_g_2': 8.0,
     'dil_q_g_2': 8.0,
     'dil_k_g_2': 8.0,
     'swa_q_g_2': 8.0,
     'swa_k_g_2': 8.0,
     'group_out_g_2': 3.757,
     'mlp_norm_g_2': 3.669,
     'swa_sinks_2': 64.0}
    for name, (base, spread) in spreads.items():
        noise = np.random.default_rng([zlib.crc32(name.encode()), seed]).standard_normal(out[name].shape)
        drawn = base * np.exp(spread * noise) if base else spread * noise
        out[name] = jnp.asarray(drawn.astype(out[name].dtype))
    for name, factor in factors.items():
        out[name] = (out[name] * factor).astype(out[name].dtype)
    return out
```

```python
import math
from contextlib import ExitStack

import numpy as np

import concourse.bass as bass
from concourse import mybir

F32 = mybir.dt.float32
I32 = mybir.dt.int32
ALU = mybir.AluOpType
ACT = mybir.ActivationFunctionType
AX = mybir.AxisListType

P = 128
D = 1024
KD = D // P
SEQ, CTX = 512, 256
TX, TC = SEQ // P, CTX // P
NT = TX + TC
HD = 64
NH = D // HD
NCHUNK = 512
EPS = 1e-6
NEG = -1e30
LAYERS = 2
NE, NG, EPG = 32, 4, 8
FE = 512
BIG = 8192.0
FF = 4096
QKV2 = 2464
LOG2E = 1.4426950408889634
LN2_HI, LN2_LO = 0.693359375, -2.12194440054690583e-4
ROUND = 1.5 * 2.0 ** 23 + 127.0
LAM_INIT = 0.8 - 0.6 * math.exp(0.0)



def rope_table(angles, copies):
    cos, sin = np.cos(angles), np.sin(angles)
    both = np.stack([np.concatenate([cos, cos], -1), np.concatenate([-sin, sin], -1)])
    return both.reshape(2, angles.shape[0], copies * 2 * angles.shape[-1]).astype(np.float32)


def constants():
    f = np.float32
    out = {"ident": np.eye(P, dtype=f)}
    t = np.arange(SEQ)
    inv = (1.0 / (f(10000.0) ** (np.arange(16, dtype=f) / f(16)))).astype(f)
    pos = np.stack([t // 64, t % 64], -1).astype(f)
    out["axial"] = rope_table((pos[:, :, None] * inv).astype(f), 2)
    inv = (1.0 / (f(10000.0) ** (np.arange(0, 32, 2, dtype=f) / f(32)))).astype(f)
    out["line"] = rope_table((t.astype(f)[:, None] * inv).astype(f), 1)
    q = np.arange(P)[:, None]
    band = np.zeros((TX, P, 640), f)
    for b in range(TX):
        k = np.arange(max(0, b - 1) * P, min(TX, b + 2) * P)[None, :]
        band[b, :, CTX:CTX + k.shape[1]] = np.where(np.abs(k - b * P - q) <= 128, 0, NEG)
    out["band"] = band
    slopes = np.exp2(-8.0 * np.arange(1, 13, dtype=f).reshape(4, 3) / 12).astype(f)
    dist = q + 384 - np.arange(512)[None, :]
    tables = []
    for h in range(4):
        tables.append(np.where(dist >= 0, -slopes[h, 0] * dist.astype(f), NEG))
    tables.append(np.where(dist >= 0, 0, NEG))
    n = ((dist >= 0) & (dist <= 128)).astype(int) + ((dist >= 0) & (dist % 4 == 0)) + (
        (dist >= 0) & (dist % 16 == 0))
    for h in range(4):
        tables.append(np.where(n > 0, -slopes[h, 1] * dist.astype(f) + np.log(np.maximum(n, 1)), NEG))
    for h in range(4):
        tables.append(np.where((dist >= 0) & (dist < 128), -slopes[h, 2] * dist.astype(f), NEG))
    out["bias2"] = np.stack(tables).astype(f)
    out["before"] = np.triu(np.ones((P, P), f), 1)
    out["ones"] = np.ones((P, P), f)
    out["iota"] = np.broadcast_to(np.arange(P, dtype=f), (P, P)).copy()
    rows = np.arange(NT * P).reshape(NT, P).T
    out["neg"] = np.full((12,), NEG, f)
    out["rowid"] = (np.stack([rows, rows, rows + NT * P], 1) - BIG).astype(f)
    return out



class Phase:

    def __init__(self, nc, name):
        self.nc, self.name, self.stack, self.sems = nc, name, ExitStack(), []

    def sb(self, name, shape, dt=F32):
        return self.stack.enter_context(self.nc.sbuf_tensor(f"{self.name}_{name}", shape, dt))

    def ps(self, name, shape):
        return self.stack.enter_context(self.nc.psum_tensor(f"{self.name}_{name}", shape, F32))

    def sem(self, name):
        self.sems.append(self.nc.alloc_semaphore(f"{self.name}_{name}"))
        return self.sems[-1]

    def block(self):
        return self.stack.enter_context(self.nc.Block())

    def __enter__(self):
        return self

    def __exit__(self, *e):
        self.stack.close()
        numbers = sorted(sem.num for sem in self.sems)
        while numbers:
            n = next((i for i, x in enumerate(numbers) if x != numbers[0] + i), len(numbers))
            self.nc.gpsimd.sem_clear(range(numbers[0], numbers[0] + n))
            numbers = numbers[n:]
        for sem in self.sems:
            self.nc.release_semaphore(sem)


class Chain:

    def __init__(self, eng, sem):
        self.eng, self.sem, self.n = eng, sem, 0

    def __call__(self, ins):
        self.n += 1
        ins.then_inc(self.sem, 1)
        self.eng.wait_ge(self.sem, self.n)


def rsqrt_mean(v, link, out, std, ss, tmp, scale):
    link(v.reciprocal(out, std))
    link(v.tensor_scalar(tmp, ss, scale, EPS, ALU.mult, ALU.add))
    link(v.tensor_tensor(tmp, tmp, out, ALU.mult))
    link(v.tensor_tensor(tmp, tmp, out, ALU.mult))
    link(v.tensor_scalar(tmp, tmp, -0.5, 1.5, ALU.mult, ALU.add))
    link(v.tensor_tensor(out, out, tmp, ALU.mult))


def bcast_rows(vec):
    return vec.partition_broadcast(P)


def inner(ap, n):
    return ap.unsqueeze(2).broadcast_to([ap.shape[0], ap.shape[1], n])


def middle(ap, n):
    return ap.unsqueeze(1).broadcast_to([ap.shape[0], n, ap.shape[1]])


def stream_weights(sp, buffers, view, chunks, loaded, mm_done, per_chunk):
    ring = buffers.shape[1]
    for j, (n0, width) in enumerate(chunks):
        if j >= ring:
            sp.wait_ge(mm_done, (j - ring + 1) * per_chunk)
        sp.dma_start(buffers[:, j % ring, :, 0:width], view[:, :, n0:n0 + width]).then_inc(
            loaded[j % ring], 16)



def load_constants(nc, e):
    with Phase(nc, "load") as ph:
        arrived = ph.sem("arrived")
        block = ph.block()

        @block.sync
        def _(sp):
            loads = [
                (e["res"][:, TC:NT, :], e["x"][0].rearrange("(t p) d -> p t d", p=P)),
                (e["res"][:, 0:TC, :], e["ctx"][0].rearrange("(t p) d -> p t d", p=P)),
                (e["ident"][:], e["c_ident"]), (e["ones"][:], e["c_ones"]),
            ]
            for dst, src in loads:
                sp.dma_start(dst, src).then_inc(arrived, 16)
            sp.wait_ge(arrived, 16 * len(loads))


def modulation(nc, e):
    per_layer = 6 * D // NCHUNK
    chunks = LAYERS * per_layer
    ring = 3
    with Phase(nc, "mod") as ph:
        vec = ph.sb("vec", [P, 2, KD])
        expn, whole, rest = (ph.sb(x, [P, 2, KD]) for x in ("expn", "whole", "rest"))
        act = ph.sb("act", [P, KD, 2])
        w = ph.sb("w", [P, ring, KD, NCHUNK])
        bias = ph.sb("bias", [2, LAYERS * 6 * D])
        rows = ph.sb("rows", [2, LAYERS * 6 * D])
        acc = [ph.ps(f"acc{i}", [P, NCHUNK]) for i in range(4)]
        vec_in, bias_in, stored = ph.sem("vec_in"), ph.sem("bias_in"), ph.sem("stored")
        exp_done, act_done, step = ph.sem("exp_done"), ph.sem("act_done"), ph.sem("step")
        rest_done = ph.sem("rest_done")
        loaded = [ph.sem(f"loaded{i}") for i in range(ring)]
        mm_done, rows_done = ph.sem("mm_done"), ph.sem("rows_done")
        block = ph.block()

        @block.sync
        def _(sp):
            sp.dma_start(vec[:, 0, :], e["c"][0].rearrange("(p k) -> p k", k=KD)).then_inc(vec_in, 16)
            sp.dma_start(vec[:, 1, :], e["c_ctx"].rearrange("(p k) -> p k", k=KD)).then_inc(vec_in, 16)
            sp.dma_start(bias[:], e["mod_b"].rearrange("l n -> (l n)").partition_broadcast(2)).then_inc(
                bias_in, 16)
            for j in range(chunks):
                if j >= ring:
                    sp.wait_ge(mm_done, j - ring + 1)
                layer, n0 = j // per_layer, j % per_layer * NCHUNK
                src = e["mod_w"][layer].rearrange("(p k) n -> p k n", k=KD)
                sp.dma_start(w[:, j % ring, :, :], src[:, :, n0:n0 + NCHUNK]).then_inc(
                    loaded[j % ring], 16)
            sp.wait_ge(rows_done, chunks)
            sp.dma_start(e["mod_dram"], rows[:]).then_inc(stored, 16)
            sp.wait_ge(stored, 16)

        @block.scalar
        def _(act_eng):
            act_eng.wait_ge(rest_done, 1)
            nc.scalar.activation(expn[:], rest[:], ACT.Exp, scale=0.25).then_inc(exp_done, 1)

        @block.vector
        def _(dve):
            link = Chain(dve, step)
            v = nc.vector
            dve.wait_ge(vec_in, 32)
            link(v.tensor_scalar(rest[:], vec[:], -1.0, None, ALU.mult))
            link(v.tensor_scalar(rest[:], rest[:], 80.0, -80.0, ALU.min, ALU.max))
            link(v.tensor_scalar(whole[:], rest[:], LOG2E, ROUND, ALU.mult, ALU.add))
            link(v.tensor_scalar(expn[:], whole[:], ROUND, None, ALU.subtract))
            link(v.scalar_tensor_tensor(rest[:], expn[:], -LN2_HI, rest[:], ALU.mult, ALU.add))
            v.scalar_tensor_tensor(rest[:], expn[:], -LN2_LO, rest[:], ALU.mult, ALU.add).then_inc(
                rest_done, 1)
            link(v.tensor_single_scalar(whole[:].bitcast(I32), whole[:].bitcast(I32), 23,
                                        ALU.logical_shift_left))
            dve.wait_ge(exp_done, 1)
            link(v.tensor_tensor(expn[:], expn[:], expn[:], ALU.mult))
            link(v.tensor_tensor(expn[:], expn[:], expn[:], ALU.mult))
            link(v.tensor_tensor(expn[:], expn[:], whole[:], ALU.mult))
            link(nc.vector.tensor_scalar(expn[:], expn[:], 1.0, None, ALU.add))
            link(nc.vector.reciprocal(expn[:], expn[:]))
            nc.vector.tensor_tensor(act[:].rearrange("p k v -> p v k"), vec[:], expn[:],
                                    ALU.mult).then_inc(act_done, 1)
            dve.wait_ge(bias_in, 16)
            for j in range(chunks):
                n0 = j * NCHUNK
                dve.wait_ge(mm_done, j + 1)
                nc.vector.tensor_tensor(rows[:, n0:n0 + NCHUNK], acc[j % 4][0:2, :],
                                        bias[:, n0:n0 + NCHUNK], ALU.add).then_inc(rows_done, 1)

        @block.tensor
        def _(pe):
            pe.wait_ge(act_done, 1)
            for j in range(chunks):
                pe.wait_ge(loaded[j % ring], 16 * (j // ring + 1))
                if j >= 4:
                    pe.wait_ge(rows_done, j - 3)
                for k in range(KD):
                    mm = nc.tensor.matmul(acc[j % 4][0:2, :], act[:, k, :], w[:, j % ring, k, :],
                                          start=(k == 0), stop=(k == KD - 1))
                mm.then_inc(mm_done, 1)


def normalise(nc, e, name, tiles, gain, shift_scale, h_t, strided=False, store=None, final=None):
    vecs = sorted({0 if t >= TC else 1 for t in tiles}) if shift_scale else []
    nt = len(tiles)
    with Phase(nc, name) as ph:
        g = ph.sb("g", [P, D])
        gf = ph.sb("gf", [P, D]) if final is not None else None
        mul = ph.sb("mul", [P, 2, D])
        add = ph.sb("add", [P, 2, D])
        h = ph.sb("h", [P, 2, D])
        sq = ph.sb("sq", [P, 2, D])
        part = ph.sb("part", [P, 32])
        ss = ph.sb("ss", [P, 2, nt])
        rstd = ph.sb("rstd", [P, 2, nt])
        std = ph.sb("std", [P, 2, nt])
        tmp = ph.sb("tmp", [P, nt])
        eps = ph.sb("eps", [P, 1])
        tp = [ph.ps(f"tp{i}", [P, 4, P]) for i in range(4)]
        vec_in, stored = ph.sem("vec_in"), [ph.sem(f"stored{i}") for i in range(2)]
        sq_done, std_done, summed = ph.sem("sq_done"), ph.sem("std_done"), ph.sem("summed")
        eps_done, ready = ph.sem("eps_done"), ph.sem("ready")
        step, h_done, tp_done, tp_read = (ph.sem(s) for s in ("step", "h_done", "tp_done", "tp_read"))
        block = ph.block()
        n_vec = 1 + (final is not None) + 2 * len(vecs)

        @block.sync
        def _(sp):
            sp.dma_start(g[:], bcast_rows(gain)).then_inc(vec_in, 16)
            if final is not None:
                sp.dma_start(gf[:], bcast_rows(final)).then_inc(vec_in, 16)
            for v in vecs:
                shift, scale = shift_scale(v)
                sp.dma_start(add[:, v, :], bcast_rows(shift)).then_inc(vec_in, 16)
                sp.dma_start(mul[:, v, :], bcast_rows(scale)).then_inc(vec_in, 16)
            if store is not None:
                for i, t in enumerate(tiles):
                    sp.wait_ge(h_done, i + 1)
                    sp.dma_start(store[t * P:(t + 1) * P, :], h[:, i % 2, :]).then_inc(
                        stored[i % 2], 16)
                for b in range(2):
                    sp.wait_ge(stored[b], 16 * (nt // 2))

        @block.scalar
        def _(act):
            act.wait_ge(eps_done, 1)
            for rnd in range(2 if final is not None else 1):
                if rnd:
                    act.wait_ge(ready, nt)
                for i, t in enumerate(tiles):
                    j = rnd * nt + i
                    if j >= 2:
                        act.wait_ge(summed, j - 1)
                    nc.scalar.activation(sq[:, j % 2, :], e["res"][:, t, :], ACT.Square).then_inc(
                        sq_done, 1)
                act.wait_ge(summed, (rnd + 1) * nt)
                nc.scalar.activation(std[:, rnd, :], ss[:, rnd, :], ACT.Sqrt, scale=1.0 / D,
                                     bias=eps[:]).then_inc(std_done, 1)
            for j in range(2 * nt):
                i, half = j // 2, j % 2
                act.wait_ge(tp_done, j + 1)
                nc.scalar.copy(h_t[:, 4 * half:4 * half + 4, i * P:(i + 1) * P],
                               tp[j % 4][:]).then_inc(tp_read, 1)

        @block.vector
        def _(dve):
            link = Chain(dve, step)
            nc.vector.memset(eps[:], EPS).then_inc(eps_done, 1)
            dve.wait_ge(vec_in, 16 * n_vec)
            for v in vecs:
                link(nc.vector.scalar_tensor_tensor(mul[:, v, :], mul[:, v, :], 1.0, g[:],
                                                    ALU.add, ALU.mult))

            def sum_squares(rnd):
                for i in range(nt):
                    j = rnd * nt + i
                    dve.wait_ge(sq_done, j + 1)
                    link(nc.vector.tensor_reduce(
                        part[:], sq[:, j % 2, :].rearrange("p (a b) -> p a b", b=32), AX.X, ALU.add))
                    nc.vector.tensor_reduce(ss[:, rnd, i:i + 1], part[:], AX.X, ALU.add).then_inc(
                        summed, 1)
                    dve.wait_ge(summed, j + 1)

            sum_squares(0)
            if final is not None:
                dve.wait_ge(std_done, 1)
                rsqrt_mean(nc.vector, link, rstd[:, 0, :], std[:, 0, :], ss[:, 0, :], tmp[:], 1.0 / D)
                for i, t in enumerate(tiles):
                    nc.vector.scalar_tensor_tensor(
                        e["res"][:, t, :], e["res"][:, t, :], rstd[:, 0, i:i + 1], gf[:],
                        ALU.mult, ALU.mult).then_inc(ready, 1)
                dve.wait_ge(ready, nt)
                sum_squares(1)
            rnd = int(final is not None)
            dve.wait_ge(std_done, rnd + 1)
            rsqrt_mean(nc.vector, link, rstd[:, rnd, :], std[:, rnd, :], ss[:, rnd, :], tmp[:], 1.0 / D)
            for i, t in enumerate(tiles):
                v = 0 if t >= TC else 1
                if i >= 2:
                    dve.wait_ge(tp_done, 2 * (i - 1))
                    if store is not None:
                        dve.wait_ge(stored[i % 2], 16 * (i // 2))
                out = h[:, i % 2, :]
                if not vecs:
                    nc.vector.scalar_tensor_tensor(out, e["res"][:, t, :], rstd[:, rnd, i:i + 1],
                                                   g[:], ALU.mult, ALU.mult).then_inc(h_done, 1)
                    continue
                link(nc.vector.scalar_tensor_tensor(out, e["res"][:, t, :], rstd[:, rnd, i:i + 1],
                                                    mul[:, v, :], ALU.mult, ALU.mult))
                nc.vector.tensor_tensor(out, out, add[:, v, :], ALU.add).then_inc(h_done, 1)

        @block.tensor
        def _(pe):
            for j in range(2 * nt):
                i, half = j // 2, j % 2
                pe.wait_ge(h_done, i + 1)
                if j >= 4:
                    pe.wait_ge(tp_read, j - 3)
                for q in range(4):
                    k = 4 * half + q
                    src = h[:, i % 2, k:D:KD] if strided else h[:, i % 2, k * P:(k + 1) * P]
                    tr = nc.tensor.transpose(tp[j % 4][:, q, :], src, e["ident"][:])
                tr.then_inc(tp_done, 1)


def rope_heads(dve, nc, link, out, src, tmp, cos, sin, half):
    heads, width = src.shape[1], src.shape[2]
    pairs = width // (2 * half)
    link(nc.vector.tensor_tensor(out, src, middle(cos, heads), ALU.mult))
    for side in range(2):
        for a in range(pairs):
            lo, other = (2 * a + side) * half, (2 * a + 1 - side) * half
            op = nc.vector.tensor_tensor(tmp[:, :, lo:lo + half], src[:, :, other:other + half],
                                         middle(sin[:, lo:lo + half], heads), ALU.mult)
            if (side, a) != (1, pairs - 1):
                op.then_inc(link.sem, 1)
                link.n += 1
            else:
                link(op)
    return nc.vector.tensor_tensor(out, out, tmp, ALU.add)


def project_heads(nc, e, name, h_t, w_dram, items, stores, values=None):
    chunks = sorted({c for c, _, _ in items})
    ends = [max(i for i, it in enumerate(items) if it[0] == c) + 1 for c in chunks]
    ring, stages = 3, 3
    with Phase(nc, name) as ph:
        w = ph.sb("w", [P, ring, KD, NCHUNK])
        rope = ph.sb("rope", [P, 2, TX, HD])
        stage = ph.sb("stage", [P, stages, 8, HD])
        tmp = ph.sb("tmp", [P, 8, HD])
        acc = [ph.ps(f"acc{i}", [P, NCHUNK]) for i in range(4)]
        tp = [ph.ps(f"tp{i}", [P, 4, P]) for i in range(2)]
        loaded = [ph.sem(f"loaded{i}") for i in range(ring)]
        rope_in, mm_done, acc_read = ph.sem("rope_in"), ph.sem("mm_done"), ph.sem("acc_read")
        tp_done, tp_read, step = ph.sem("tp_done"), ph.sem("tp_read"), ph.sem("step")
        block = ph.block()
        turned = [i for i, it in enumerate(items) if it[2] != "value"]

        @block.sync
        def _(sp):
            view = w_dram.rearrange("(k p) n -> p k n", p=P)
            for j, c in enumerate(chunks):
                if j >= ring:
                    sp.wait_ge(mm_done, ends[j - ring])
                sp.dma_start(w[:, j % ring, :, :],
                             view[:, :, c * NCHUNK:(c + 1) * NCHUNK]).then_inc(loaded[j % ring], 16)
                if j == 0:
                    sp.dma_start(rope[:], e["c_axial"].rearrange("s (t p) d -> p s t d", p=P)).then_inc(
                        rope_in, 16)

        @block.tensor
        def _(pe):
            def turn(j):
                i = turned[j]
                pe.wait_ge(acc_read, i + 1)
                if j >= 2:
                    pe.wait_ge(tp_read, j - 1)
                for q in range(4):
                    tr = nc.tensor.transpose(
                        tp[j % 2][:, q, :],
                        stage[:, j % stages, 2 * q:2 * q + 2, :].rearrange("p a d -> p (a d)"),
                        e["ident"][:])
                tr.then_inc(tp_done, 1)

            last, j = None, 0
            for i, (c, t, kind) in enumerate(items):
                b = chunks.index(c)
                if c != last:
                    pe.wait_ge(loaded[b % ring], 16 * (b // ring + 1))
                    last = c
                if i >= 4:
                    pe.wait_ge(acc_read, i - 3)
                for k in range(KD):
                    mm = nc.tensor.matmul(acc[i % 4][:], h_t[:, k, t * P:(t + 1) * P],
                                          w[:, b % ring, k, :], start=(k == 0), stop=(k == KD - 1))
                mm.then_inc(mm_done, 1)
                if j < len(turned) and turned[j] <= i - 1:
                    turn(j)
                    j += 1
            while j < len(turned):
                turn(j)
                j += 1

        @block.vector
        def _(dve):
            link = Chain(dve, step)
            dve.wait_ge(rope_in, 16)
            j = 0
            for i, (c, t, kind) in enumerate(items):
                dve.wait_ge(mm_done, i + 1)
                if kind == "value":
                    nc.vector.tensor_copy(stores(c, t), acc[i % 4][:]).then_inc(acc_read, 1)
                    continue
                if j >= stages:
                    dve.wait_ge(tp_done, j - stages + 1)
                dst = stage[:, j % stages, :, :]
                src = acc[i % 4][:].rearrange("p (h d) -> p h d", d=HD)
                j += 1
                if kind == "plain":
                    nc.vector.tensor_copy(dst, src).then_inc(acc_read, 1)
                elif kind == "shared":
                    twice = dst.rearrange("p (g c) d -> p g c d", c=2)
                    first, keys = twice[:, :, 0, :], src[:, 0:4, :]
                    if t < TC:
                        link(nc.vector.tensor_copy(first, keys))
                    else:
                        link(rope_heads(dve, nc, link, first, keys, tmp[:, 0:4, :],
                                        rope[:, 0, t - TC, :], rope[:, 1, t - TC, :], 16))
                    link(nc.vector.tensor_copy(twice[:, :, 1, :], first))
                    nc.vector.tensor_copy(values(t), acc[i % 4][:, 4 * HD:8 * HD]).then_inc(
                        acc_read, 1)
                elif kind == "rope":
                    rope_heads(dve, nc, link, dst, src, tmp[:], rope[:, 0, t - TC, :],
                               rope[:, 1, t - TC, :], 16).then_inc(acc_read, 1)

        @block.scalar
        def _(act):
            for j, i in enumerate(turned):
                c, t, kind = items[i]
                act.wait_ge(tp_done, j + 1)
                dst, scale = stores(c, t)
                nc.scalar.activation(dst, tp[j % 2][:], ACT.Copy, scale=scale).then_inc(tp_read, 1)


def diff_attention(nc, e, q_t, k_t, v, o):
    pairs = [(t, h) for t in [*range(TC, NT), *range(TC)] for h in range(8)]
    n = len(pairs)
    keys = lambda t: NT if t >= TC else TC
    with Phase(nc, "dif") as ph:
        lam_v = ph.sb("lam_v", [P, 4, HD])
        lam_p = ph.sb("lam_p", [P, 2, HD])
        lam = ph.sb("lam", [P, 4])
        prob = ph.sb("prob", [P, 2, 2, NT * P])
        prob_t = ph.sb("prob_t", [P, 2, NT, P])
        neg_max = ph.sb("neg_max", [P, 2, 2])
        total = ph.sb("total", [P, 2, 2])
        score = [ph.ps(f"score{i}", [P, 1024]) for i in range(2)]
        tp_a, tp_b = ph.ps("tp_a", [P, 4, P]), ph.ps("tp_b", [P, 4, P])
        out = [ph.ps(f"out{i}", [P, NCHUNK]) for i in range(2)]
        names = "lam_in lam_exp lam_done scored maxed exped combined turned read_a read_b weighed out_read step"
        s = {x: ph.sem(x) for x in names.split()}
        block = ph.block()

        @block.sync
        def _(sp):
            sp.dma_start(lam_v[:].rearrange("p a d -> p (a d)"),
                         e["a_lam"][0].rearrange("a d -> (a d)").partition_broadcast(P)).then_inc(
                             s["lam_in"], 16)

        @block.tensor
        def _(pe):
            def scores(g):
                t, h = pairs[g]
                for m in range(2):
                    u = 2 * g + m
                    if g >= 1:
                        pe.wait_ge(s["exped"], u - 1)
                    lo = HD * m
                    width = keys(t) * P
                    for n0 in range(0, width, NCHUNK):
                        w = min(NCHUNK, width - n0)
                        mm = nc.tensor.matmul(score[m][:, n0:n0 + w],
                                              q_t[lo:lo + HD, h, t * P:(t + 1) * P],
                                              k_t[lo:lo + HD, h, n0:n0 + w], start=True, stop=True)
                    mm.then_inc(s["scored"], 1)

            def weigh(g):
                t, h = pairs[g]
                pe.wait_ge(s["combined"], g + 1)
                if g >= 1:
                    pe.wait_ge(s["read_a"], g)
                    pe.wait_ge(s["read_b"], g)
                for k in range(keys(t)):
                    bank = tp_a if k < 4 else tp_b
                    tr = nc.tensor.transpose(bank[:, k % 4, :], prob[:, g % 2, 0, k * P:(k + 1) * P],
                                             e["ident"][:])
                tr.then_inc(s["turned"], 1)
                if g >= 2:
                    pe.wait_ge(s["out_read"], g - 1)
                pe.wait_ge(s["read_a"], g + 1)
                pe.wait_ge(s["read_b"], g + 1)
                for k in range(keys(t)):
                    mm = nc.tensor.matmul(out[g % 2][:, 0:P], prob_t[:, g % 2, k, :],
                                          v[:, k, h * P:(h + 1) * P], start=(k == 0),
                                          stop=(k == keys(t) - 1))
                mm.then_inc(s["weighed"], 1)

            for g in range(n + 1):
                if g < n:
                    scores(g)
                if g >= 1:
                    weigh(g - 1)

        @block.vector
        def _(dve):
            link = Chain(dve, s["step"])
            dve.wait_ge(s["lam_in"], 16)
            link(nc.vector.tensor_tensor(lam_p[:], lam_v[:, 0:4:2, :], lam_v[:, 1:4:2, :], ALU.mult))
            nc.vector.tensor_reduce(lam[:, 0:2], lam_p[:], AX.X, ALU.add).then_inc(s["lam_done"], 1)
            dve.wait_ge(s["lam_exp"], 1)
            link(nc.vector.tensor_tensor(lam[:, 3:4], lam[:, 1:2], lam[:, 0:1], ALU.subtract))
            link(nc.vector.tensor_scalar(lam[:, 3:4], lam[:, 3:4], -LAM_INIT, None, ALU.add))

            def maxima(g):
                t, _ = pairs[g]
                for m in range(2):
                    dve.wait_ge(s["scored"], 2 * g + m + 1)
                    if g >= 2:
                        dve.wait_ge(s["exped"], 2 * (g - 2) + m + 1)
                    nc.vector.tensor_reduce(neg_max[:, g % 2, m:m + 1], score[m][:, 0:keys(t) * P],
                                            AX.X, ALU.max, negate=True).then_inc(s["maxed"], 1)

            def combine(g):
                t, _ = pairs[g]
                width = keys(t) * P
                dve.wait_ge(s["exped"], 2 * g + 2)
                tot = total[:, g % 2, :]
                link(nc.vector.reciprocal(tot, tot))
                link(nc.vector.tensor_tensor(tot[:, 1:2], tot[:, 1:2], lam[:, 3:4], ALU.mult))
                a, b = prob[:, g % 2, 0, 0:width], prob[:, g % 2, 1, 0:width]
                link(nc.vector.tensor_scalar(a, a, tot[:, 0:1], None, ALU.mult))
                nc.vector.scalar_tensor_tensor(a, b, tot[:, 1:2], a, ALU.mult, ALU.add).then_inc(
                    s["combined"], 1)

            def read_b(g):
                t, _ = pairs[g]
                dve.wait_ge(s["turned"], g + 1)
                if g >= 2:
                    dve.wait_ge(s["weighed"], g - 1)
                if keys(t) > 4:
                    nc.vector.tensor_copy(prob_t[:, g % 2, 4:keys(t), :],
                                          tp_b[:, 0:keys(t) - 4, :]).then_inc(s["read_b"], 1)
                else:
                    dve.sem_inc(s["read_b"], 1)

            def read_out(g):
                t, h = pairs[g]
                dve.wait_ge(s["weighed"], g + 1)
                nc.vector.tensor_copy(o[:, t, h * P:(h + 1) * P], out[g % 2][:, 0:P]).then_inc(
                    s["out_read"], 1)

            for g in range(n + 1):
                if g < n:
                    maxima(g)
                if g >= 1:
                    read_b(g - 1)
                if g < n:
                    combine(g)
                if g >= 1:
                    read_out(g - 1)

        @block.scalar
        def _(act):
            act.wait_ge(s["lam_done"], 1)
            nc.scalar.activation(lam[:, 0:2], lam[:, 0:2], ACT.Exp).then_inc(s["lam_exp"], 1)
            for g in range(n + 1):
                if g < n:
                    t, _ = pairs[g]
                    width = keys(t) * P
                    if g >= 2:
                        act.wait_ge(s["combined"], g - 1)
                        act.wait_ge(s["turned"], g - 1)
                    for m in range(2):
                        act.wait_ge(s["maxed"], 2 * g + m + 1)
                        nc.scalar.activation(prob[:, g % 2, m, 0:width], score[m][:, 0:width],
                                             ACT.Exp, bias=neg_max[:, g % 2, m:m + 1],
                                             accum_out=total[:, g % 2, m:m + 1]).then_inc(s["exped"], 1)
                if g >= 1:
                    t, _ = pairs[g - 1]
                    act.wait_ge(s["turned"], g)
                    if g >= 3:
                        act.wait_ge(s["weighed"], g - 2)
                    k = min(4, keys(t))
                    nc.scalar.copy(prob_t[:, (g - 1) % 2, 0:k, :], tp_a[:, 0:k, :]).then_inc(
                        s["read_a"], 1)


def masked_attention(nc, e, name, units, mask, mask_src, sink_src, o):
    n = len(units)
    groups = n // 8
    with Phase(nc, name) as ph:
        masks = ph.sb("masks", [P, *mask])
        sinks = ph.sb("sinks", [P, NH])
        masked = ph.sb("masked", [P, 2, 640])
        prob = ph.sb("prob", [P, 2, 640])
        prob_t = ph.sb("prob_t", [P, 2, 5, P])
        top = ph.sb("top", [P, 2, 8])
        neg_top = ph.sb("neg_top", [P, 2, 8])
        total = ph.sb("total", [P, 2, 8])
        sink_e = ph.sb("sink_e", [P, 2, 8])
        score = [ph.ps(f"score{i}", [P, 1024]) for i in range(2)]
        tp_a, tp_b = ph.ps("tp_a", [P, 4, P]), ph.ps("tp_b", [P, 4, P])
        out = [ph.ps(f"out{i}", [P, 8, HD]) for i in range(2)]
        names = ("const_in scored masked topped exped turned read_a read_b weighed sink_d sink_x "
                 "out_read step")
        s = {x: ph.sem(x) for x in names.split()}
        block = ph.block()
        n_sink = len(sink_src)

        @block.sync
        def _(sp):
            sp.dma_start(masks[:], mask_src).then_inc(s["const_in"], 16)
            for dst0, src in sink_src:
                sp.dma_start(sinks[:, dst0:dst0 + src.shape[0]], bcast_rows(src)).then_inc(
                    s["const_in"], 16)

        @block.tensor
        def _(pe):
            def scores(u):
                unit = units[u]
                if u >= 2:
                    pe.wait_ge(s["masked"], u - 1)
                for col, rhs, w in unit["keys"]:
                    mm = nc.tensor.matmul(score[u % 2][:, col:col + w], unit["q"], rhs,
                                          start=True, stop=True)
                mm.then_inc(s["scored"], 1)

            def weigh(u):
                unit = units[u]
                kt = unit["width"] // P
                pe.wait_ge(s["exped"], u + 1)
                if u >= 1:
                    pe.wait_ge(s["read_a"], u)
                    pe.wait_ge(s["read_b"], u)
                for k in range(kt):
                    bank = tp_a if k < 4 else tp_b
                    tr = nc.tensor.transpose(bank[:, k % 4, :], prob[:, u % 2, k * P:(k + 1) * P],
                                             e["ident"][:])
                tr.then_inc(s["turned"], 1)
                g = u // 8
                if u % 8 == 0 and g >= 2:
                    pe.wait_ge(s["out_read"], g - 1)
                pe.wait_ge(s["read_a"], u + 1)
                pe.wait_ge(s["read_b"], u + 1)
                for k in range(kt):
                    mm = nc.tensor.matmul(out[g % 2][:, u % 8, :], prob_t[:, u % 2, k, :],
                                          unit["values"][k], start=(k == 0), stop=(k == kt - 1))
                mm.then_inc(s["weighed"], 1)

            for u in range(n + 1):
                if u < n:
                    scores(u)
                if u >= 1:
                    weigh(u - 1)

        @block.vector
        def _(dve):
            link = Chain(dve, s["step"])
            dve.wait_ge(s["const_in"], 16 * (1 + n_sink))

            def mask_and_max(u):
                unit, g = units[u], u // 8
                dve.wait_ge(s["scored"], u + 1)
                if u >= 2:
                    dve.wait_ge(s["exped"], u - 1)
                if u % 8 == 0 and g >= 2:
                    dve.wait_ge(s["sink_x"], g - 1)
                col = top[:, g % 2, u % 8:u % 8 + 1]
                nc.vector.tensor_tensor_reduce(
                    masked[:, u % 2, 0:unit["width"]], score[u % 2][:, 0:unit["width"]],
                    masks[:, unit["mask"], unit["mask0"]:unit["mask0"] + unit["width"]], 1.0,
                    sinks[:, unit["head"]:unit["head"] + 1], ALU.add, ALU.max, col).then_inc(s["masked"], 1)
                dve.wait_ge(s["masked"], u + 1)
                nc.vector.tensor_scalar(neg_top[:, g % 2, u % 8:u % 8 + 1], col, -1.0, None,
                                        ALU.mult).then_inc(s["topped"], 1)

            def read_b(u):
                unit = units[u]
                dve.wait_ge(s["turned"], u + 1)
                if u >= 2:
                    dve.wait_ge(s["weighed"], u - 1)
                if unit["width"] > 4 * P:
                    nc.vector.tensor_copy(prob_t[:, u % 2, 4:5, :], tp_b[:, 0:1, :]).then_inc(
                        s["read_b"], 1)
                else:
                    dve.sem_inc(s["read_b"], 1)

            def finish(g):
                head = units[8 * g]["head"]
                dve.wait_ge(s["topped"], 8 * g + 8)
                if g >= 2:
                    dve.wait_ge(s["sink_x"], g - 1)
                nc.vector.tensor_tensor(sink_e[:, g % 2, :], sinks[:, head:head + 8],
                                        top[:, g % 2, :], ALU.subtract).then_inc(s["sink_d"], 1)
                dve.wait_ge(s["sink_x"], g + 1)
                dve.wait_ge(s["exped"], 8 * g + 8)
                tot = total[:, g % 2, :]
                link(nc.vector.tensor_tensor(tot, tot, sink_e[:, g % 2, :], ALU.add))
                link(nc.vector.reciprocal(tot, tot))
                dve.wait_ge(s["weighed"], 8 * g + 8)
                nc.vector.tensor_tensor(o(g), out[g % 2][:], inner(tot, HD), ALU.mult).then_inc(
                    s["out_read"], 1)

            for u in range(n + 2):
                if u < n:
                    mask_and_max(u)
                if 1 <= u <= n:
                    read_b(u - 1)
                if u >= 9 and (u - 1) % 8 == 0:
                    finish((u - 1) // 8 - 1)

        @block.scalar
        def _(act):
            for u in range(n + 2):
                if u < n:
                    unit, g = units[u], u // 8
                    if u >= 2:
                        act.wait_ge(s["turned"], u - 1)
                    if u % 8 == 0 and g >= 2:
                        act.wait_ge(s["out_read"], g - 1)
                    act.wait_ge(s["topped"], u + 1)
                    nc.scalar.activation(prob[:, u % 2, 0:unit["width"]],
                                         masked[:, u % 2, 0:unit["width"]], ACT.Exp,
                                         bias=neg_top[:, g % 2, u % 8:u % 8 + 1],
                                         accum_out=total[:, g % 2, u % 8:u % 8 + 1]).then_inc(
                                             s["exped"], 1)
                if 1 <= u <= n:
                    k = min(4, units[u - 1]["width"] // P)
                    act.wait_ge(s["turned"], u)
                    if u >= 3:
                        act.wait_ge(s["weighed"], u - 2)
                    nc.scalar.copy(prob_t[:, (u - 1) % 2, 0:k, :], tp_a[:, 0:k, :]).then_inc(
                        s["read_a"], 1)
                if u >= 9 and (u - 1) % 8 == 0:
                    g = (u - 1) // 8 - 1
                    act.wait_ge(s["sink_d"], g + 1)
                    nc.scalar.activation(sink_e[:, g % 2, :], sink_e[:, g % 2, :],
                                         ACT.Exp).then_inc(s["sink_x"], 1)


def project_out(nc, e, name, o, tiles, heads, gain, gain_scale, w_dram, gate):
    nt = len(tiles)
    vecs = sorted({0 if t >= TC else 1 for t in tiles}) if gate else []
    with Phase(nc, name) as ph:
        w = ph.sb("w", [P, 2, KD, NCHUNK])
        o_t = ph.sb("o_t", [P, KD, nt * P])
        gates = ph.sb("gates", [P, 2, D])
        g = ph.sb("g", [P, D])
        sq = ph.sb("sq", [P, 2, D])
        ss, std, rstd, tmp = (ph.sb(x, [P, nt * (heads or 1)]) for x in ("ss", "std", "rstd", "tmp"))
        part = ph.sb("part", [P, 2, NCHUNK])
        eps = ph.sb("eps", [P, 1])
        tp = [ph.ps(f"tp{i}", [P, 4, P]) for i in range(4)]
        acc = [ph.ps(f"acc{i}", [P, NCHUNK]) for i in range(4)]
        names = "vec_in sq_done sum_done std_done eps_done o_done tp_done tp_read mm_done added step"
        s = {x: ph.sem(x) for x in names.split()}
        loaded = [ph.sem(f"loaded{i}") for i in range(2)]
        block = ph.block()
        chunks = [(0, NCHUNK), (NCHUNK, NCHUNK)]
        n_vec = len(vecs) + (1 if gain is not None else 0)

        @block.sync
        def _(sp):
            for v in vecs:
                sp.dma_start(gates[:, v, :], bcast_rows(gate(v))).then_inc(s["vec_in"], 16)
            if gain is not None:
                sp.dma_start(g[:, 0:gain.shape[0]], bcast_rows(gain)).then_inc(s["vec_in"], 16)
            stream_weights(sp, w, w_dram.rearrange("(k p) n -> p k n", p=P), chunks, loaded,
                           s["mm_done"], nt)

        @block.scalar
        def _(act):
            if gain is not None:
                for i, t in enumerate(tiles):
                    if i >= 2:
                        act.wait_ge(s["sum_done"], i - 1)
                    nc.scalar.activation(sq[:, i % 2, :], o[:, t, :], ACT.Square).then_inc(
                        s["sq_done"], 1)
                act.wait_ge(s["eps_done"], 1)
                act.wait_ge(s["sum_done"], nt)
                nc.scalar.activation(std[:], ss[:], ACT.Sqrt, scale=heads / D,
                                     bias=eps[:]).then_inc(s["std_done"], 1)
            for j in range(2 * nt):
                i, half = j // 2, j % 2
                act.wait_ge(s["tp_done"], j + 1)
                nc.scalar.copy(o_t[:, 4 * half:4 * half + 4, i * P:(i + 1) * P],
                               tp[j % 4][:]).then_inc(s["tp_read"], 1)

        @block.vector
        def _(dve):
            link = Chain(dve, s["step"])
            nc.vector.memset(eps[:], EPS).then_inc(s["eps_done"], 1)
            if n_vec:
                dve.wait_ge(s["vec_in"], 16 * n_vec)
            if gain is not None:
                width = D // heads
                for i, t in enumerate(tiles):
                    dve.wait_ge(s["sq_done"], i + 1)
                    nc.vector.tensor_reduce(
                        ss[:, i * heads:(i + 1) * heads],
                        sq[:, i % 2, :].rearrange("p (h d) -> p h d", h=heads), AX.X,
                        ALU.add).then_inc(s["sum_done"], 1)
                dve.wait_ge(s["std_done"], 1)
                rsqrt_mean(nc.vector, link, rstd[:], std[:], ss[:], tmp[:], heads / D)
                if gain_scale != 1.0:
                    link(nc.vector.tensor_scalar(rstd[:], rstd[:], gain_scale, None, ALU.mult))
                for i, t in enumerate(tiles):
                    slices = o[:, t, :].rearrange("p (h d) -> p h d", h=heads)
                    link(nc.vector.tensor_tensor(slices, slices,
                                                 inner(rstd[:, i * heads:(i + 1) * heads], width),
                                                 ALU.mult))
                    if gain.shape[0] == width:
                        op = nc.vector.tensor_tensor(slices, slices, middle(g[:, 0:width], heads),
                                                     ALU.mult)
                    else:
                        op = nc.vector.tensor_tensor(o[:, t, :], o[:, t, :], g[:], ALU.mult)
                    op.then_inc(s["o_done"], 1)
            for j in range(2 * nt):
                n0, t = j // nt * NCHUNK, tiles[j % nt]
                dst = e["res"][:, t, n0:n0 + NCHUNK]
                dve.wait_ge(s["mm_done"], j + 1)
                if not gate:
                    nc.vector.tensor_tensor(dst, dst, acc[j % 4][:], ALU.add).then_inc(s["added"], 1)
                    continue
                v = 0 if t >= TC else 1
                link(nc.vector.tensor_tensor(part[:, j % 2, :], acc[j % 4][:],
                                             gates[:, v, n0:n0 + NCHUNK], ALU.mult))
                nc.vector.tensor_tensor(dst, dst, part[:, j % 2, :], ALU.add).then_inc(s["added"], 1)

        @block.tensor
        def _(pe):
            for j in range(2 * nt):
                i, half = j // 2, j % 2
                if gain is not None:
                    pe.wait_ge(s["o_done"], i + 1)
                if j >= 4:
                    pe.wait_ge(s["tp_read"], j - 3)
                for q in range(4):
                    k = 4 * half + q
                    tr = nc.tensor.transpose(tp[j % 4][:, q, :], o[:, tiles[i], k * P:(k + 1) * P],
                                             e["ident"][:])
                tr.then_inc(s["tp_done"], 1)
            for j in range(2 * nt):
                c, i = j // nt, j % nt
                if i == 0:
                    pe.wait_ge(loaded[c], 16)
                if c == 0:
                    pe.wait_ge(s["tp_read"], 2 * (i + 1))
                if j >= 4:
                    pe.wait_ge(s["added"], j - 3)
                for k in range(KD):
                    mm = nc.tensor.matmul(acc[j % 4][:], o_t[:, k, i * P:(i + 1) * P],
                                          w[:, c, k, :], start=(k == 0), stop=(k == KD - 1))
                mm.then_inc(s["mm_done"], 1)


def max_blocks(nt):
    n = NE + 2 * nt
    return n + n % 2


def route(nc, e, layer, tiles, h_t, r):
    nt = len(tiles)
    nb = max_blocks(nt)
    with Phase(nc, f"route{layer}") as ph:
        wr = ph.sb("wr", [P, KD, NG + NE])
        bias = ph.sb("bias", [P, NG + NE])
        before = ph.sb("before", [P, P])
        iota = ph.sb("iota", [P, P])
        rowid = ph.sb("rowid", [P, 3, NT])
        logits = ph.sb("logits", [P, nt, NG + NE])
        gate_t = ph.sb("gate_t", [P, nt, NG])
        tg = ph.sb("tg", [P, nt, NG])
        hot_g = ph.sb("hot_g", [P, nt, NG])
        le = ph.sb("le", [P, nt, NE])
        te = ph.sb("te", [P, nt, NE])
        hot = ph.sb("hot", [P, 2, nt, NE])
        both = ph.sb("both", [P, nt, NE])
        small = ph.sb("small", [P, 12, nt])
        place = ph.sb("place", [P, nt, NE])
        cnt = ph.sb("cnt", [P, NE])
        blocks = ph.sb("blocks", [P, NE])
        end = [ph.sb(f"end{i}", [P, NE]) for i in range(2)]
        dest = ph.sb("dest", [P, 2, nt])
        dest_i = ph.sb("dest_i", [P, 2, 2, nt], I32)
        dest_f = ph.sb("dest_f", [P, 2, 2, nt])
        lane = ph.sb("lane", [P, 2, nt, P])
        what = ph.sb("what", [P, 2, nt, 2, nb])
        past = ph.sb("past", [1, nb, NE])
        expert_f = ph.sb("expert_f", [1, nb])
        acc = [ph.ps(f"acc{i}", [P, NCHUNK]) for i in range(2)]
        where, slots = ph.ps("where", [P, nt, NE]), ph.ps("slots", [P, 2, nb])
        names = "const_in mm_done lg_read gexp_in gexp_done wexp_in wexp_done hot_done where_done tables_in slots_done step fill"
        s = {x: ph.sem(x) for x in names.split()}
        block = ph.block()

        @block.sync
        def _(sp):
            loads = [
                (wr[:, :, 0:NG], e["moe_router_g"][layer].rearrange("(k p) n -> p k n", p=P)),
                (wr[:, :, NG:], e["moe_router_e"][layer].rearrange("(k p) n -> p k n", p=P)),
                (bias[:, 0:NG], bcast_rows(e["moe_router_g_b"][layer])),
                (bias[:, NG:], bcast_rows(e["moe_router_e_b"][layer])),
                (before[:], e["c_before"]), (iota[:], e["c_iota"]), (rowid[:], e["c_rowid"]),
            ]
            for dst, src in loads:
                sp.dma_start(dst, src).then_inc(s["const_in"], 16)

        @block.tensor
        def _(pe):
            pe.wait_ge(s["const_in"], 16 * 7)
            for i in range(nt):
                if i >= 2:
                    pe.wait_ge(s["lg_read"], i - 1)
                for k in range(KD):
                    mm = nc.tensor.matmul(acc[i % 2][:, 0:NG + NE], h_t[:, k, i * P:(i + 1) * P],
                                          wr[:, k, :], start=(k == 0), stop=(k == KD - 1))
                mm.then_inc(s["mm_done"], 1)
            pe.wait_ge(s["hot_done"], 1)
            pe.wait_ge(s["lg_read"], nt)
            for i in range(nt):
                for j in range(i + 1):
                    nc.tensor.matmul(where[:, i, :], before[:] if j == i else e["ones"][:],
                                     both[:, j, :], start=(j == 0), stop=(j == i))
            for j in range(nt):
                mm = nc.tensor.matmul(acc[0][:, 0:NE], e["ones"][:], both[:, j, :], start=(j == 0),
                                      stop=(j == nt - 1))
            mm.then_inc(s["where_done"], 1)
            pe.wait_ge(s["tables_in"], 1)
            for j in range(2 * nt):
                a, i = j // nt, j % nt
                mm = nc.tensor.matmul(slots[:], lane[:, a, i, :], what[:, a, i, :, :],
                                      start=(j == 0), stop=(j == 2 * nt - 1))
            mm.then_inc(s["slots_done"], 1)

        @block.scalar
        def _(act):
            act.wait_ge(s["gexp_in"], 1)
            nc.scalar.activation(tg[:], tg[:], ACT.Exp).then_inc(s["gexp_done"], 1)
            act.wait_ge(s["wexp_in"], 1)
            nc.scalar.activation(small[:, 5, :], small[:, 5, :], ACT.Exp).then_inc(s["wexp_done"], 1)

        @block.vector
        def _(dve):
            v = nc.vector
            link = Chain(dve, s["step"])
            dve.wait_ge(s["const_in"], 16 * 7)
            for i in range(nt):
                dve.wait_ge(s["mm_done"], i + 1)
                v.tensor_tensor(logits[:, i, :], acc[i % 2][:, 0:NG + NE], bias[:],
                                ALU.add).then_inc(s["lg_read"], 1)
            dve.wait_ge(s["lg_read"], nt)
            row = lambda j: small[:, j, :]

            def first_max(hot_out, values, scratch, n, best):
                link(v.tensor_reduce(best, values, AX.X, ALU.max))
                link(v.tensor_tensor(scratch, values, inner(best, n), ALU.is_equal))
                link(v.scalar_tensor_tensor(scratch, middle(iota[:, 0:n], nt), float(n), scratch,
                                            ALU.subtract, ALU.mult))
                link(v.tensor_reduce(row(9), scratch, AX.X, ALU.min))
                link(v.tensor_scalar(row(9), row(9), float(n), None, ALU.add))
                link(v.tensor_tensor(hot_out, middle(iota[:, 0:n], nt), inner(row(9), n),
                                     ALU.is_equal))

            lg, lge = logits[:, :, 0:NG], logits[:, :, NG:]
            first_max(hot_g[:], lg, gate_t[:], NG, row(0))
            v.tensor_tensor(tg[:], lg, inner(row(0), NG), ALU.subtract).then_inc(s["gexp_in"], 1)
            dve.wait_ge(s["gexp_done"], 1)
            link(v.tensor_reduce(row(1), tg[:], AX.X, ALU.add))
            link(v.reciprocal(row(1), row(1)))
            for g in range(NG):
                sl = slice(g * EPG, (g + 1) * EPG)
                oh = hot_g[:, :, g]
                link(v.tensor_tensor(le[:, :, sl], lge[:, :, sl], inner(oh, EPG), ALU.mult))
                link(v.tensor_scalar(row(2), oh, -1.0, -NEG, ALU.add, ALU.mult))
                link(v.tensor_tensor(le[:, :, sl], le[:, :, sl], inner(row(2), EPG), ALU.add))
            first_max(hot[:, 0, :, :], le[:], te[:], NE, row(3))
            link(v.scalar_tensor_tensor(le[:], hot[:, 0, :, :], 2 * NEG, le[:], ALU.mult, ALU.add))
            first_max(hot[:, 1, :, :], le[:], te[:], NE, row(4))
            v.tensor_tensor(row(5), row(4), row(3), ALU.subtract).then_inc(s["wexp_in"], 1)
            v.tensor_tensor(both[:], hot[:, 0, :, :], hot[:, 1, :, :], ALU.add).then_inc(
                s["hot_done"], 1)
            dve.wait_ge(s["wexp_done"], 1)
            link(v.tensor_scalar(row(6), row(5), 1.0, None, ALU.add))
            link(v.reciprocal(row(6), row(6)))
            link(v.tensor_tensor(r["weight"][:, 0, 0:nt], row(6), row(1), ALU.mult))
            link(v.tensor_tensor(r["weight"][:, 1, 0:nt], r["weight"][:, 0, 0:nt], row(5), ALU.mult))
            dve.wait_ge(s["where_done"], 1)
            link(v.tensor_copy(cnt[:], acc[0][:, 0:NE]))
            link(v.tensor_scalar(blocks[:], cnt[:], 0.0, None, ALU.is_gt))
            for k in range(1, nt):
                link(v.scalar_tensor_tensor(blocks[:], cnt[:], float(k * P), blocks[:], ALU.is_gt,
                                            ALU.add))
            link(v.tensor_copy(end[0][:], blocks[:]))
            a = 0
            for k in (1, 2, 4, 8, 16):
                link(v.tensor_copy(end[1 - a][:, 0:k], end[a][:, 0:k]))
                link(v.tensor_tensor(end[1 - a][:, k:], end[a][:, k:], end[a][:, 0:NE - k], ALU.add))
                a = 1 - a
            last = end[a]
            link(v.tensor_tensor(cnt[:], last[:], blocks[:], ALU.subtract))
            link(v.tensor_scalar(cnt[:], cnt[:], float(P), None, ALU.mult))
            link(v.tensor_tensor(place[:], where[:], middle(cnt[:], nt), ALU.add))
            for a in range(2):
                link(v.tensor_tensor(te[:], place[:], hot[:, a, :, :], ALU.mult))
                link(v.tensor_reduce(dest[:, a, :], te[:], AX.X, ALU.add))
            link(v.tensor_copy(dest_i[:, 0, :, :], dest[:]))
            link(v.tensor_copy(dest_i[:, 1, :, :], dest[:]))
            link(v.tensor_single_scalar(dest_i[:, 0, :, :], dest_i[:, 0, :, :], P - 1,
                                        ALU.bitwise_and))
            link(v.tensor_single_scalar(dest_i[:, 1, :, :], dest_i[:, 1, :, :], 7,
                                        ALU.arith_shift_right))
            link(v.tensor_copy(dest_f[:], dest_i[:]))
            for a in range(2):
                for i in range(nt):
                    v.tensor_scalar(lane[:, a, i, :], iota[:], dest_f[:, 0, a, i:i + 1], None,
                                    ALU.is_equal).then_inc(s["fill"], 1)
                    for z in range(2):
                        idr = rowid[:, z * (1 + a), tiles[i]:tiles[i] + 1]
                        v.tensor_scalar(what[:, a, i, z, :], iota[:, 0:nb],
                                        dest_f[:, 1, a, i:i + 1], idr, ALU.is_equal,
                                        ALU.mult).then_inc(s["fill"], 1)
            dve.wait_ge(s["fill"], 6 * nt)
            dve.sem_inc(s["tables_in"], 1)
            link(v.tensor_tensor(past[:], middle(last[0:1, :], nb), inner(iota[0:1, 0:nb], NE),
                                 ALU.is_le))
            link(v.tensor_reduce(expert_f[:], past[:], AX.X, ALU.add))
            link(v.tensor_scalar(expert_f[:], expert_f[:], float(NE - 1), None, ALU.min))
            link(v.tensor_copy(r["expert"][:, 0:nb], expert_f[:]))
            link(v.tensor_copy(r["count"][:], last[0:1, NE - 1:NE]))
            dve.wait_ge(s["slots_done"], 1)
            link(v.tensor_scalar(r["index"][:, :, 0:nb], slots[:], BIG, None, ALU.add))
            link(v.memset(r["index"][:, :, nb:], int(BIG)))


def experts(nc, e, layer, nt, r):
    nb = max_blocks(nt)
    with Phase(nc, f"moe{layer}") as ph:
        wg = [ph.sb(f"wg{b}", [P, KD, FE]) for b in range(2)]
        wu = [ph.sb(f"wu{b}", [P, KD, FE]) for b in range(2)]
        wd = [ph.sb(f"wd{b}", [P, FE // P, D]) for b in range(2)]
        xg = [ph.sb(f"xg{b}", [P, D]) for b in range(2)]
        xg_t = [ph.sb(f"xg_t{b}", [P, KD, P]) for b in range(2)]
        idx = [ph.sb(f"idx{b}", [P, 2], I32) for b in range(2)]
        sig = ph.sb("sig", [P, FE])
        hid = ph.sb("hid", [P, FE])
        hid_t = ph.sb("hid_t", [P, FE // P, P])
        y = [ph.sb(f"y{b}", [P, D]) for b in range(2)]
        tp = [ph.ps(f"tp{i}", [P, 4, P]) for i in range(2)]
        HF = FE // 2
        gate = [ph.ps(f"gate{f}", [P, HF]) for f in range(2)]
        up = [ph.ps(f"up{f}", [P, HF]) for f in range(2)]
        down = [ph.ps(f"down{i}", [P, NCHUNK]) for i in range(2)]
        names = ("y_free cleared idx_done turned_x read_x gated upped expd hid_done issue indexed "
                 "turned_h read_h downed y_done step")
        s = {x: ph.sem(x) for x in names.split()}
        gu_in = [ph.sem(f"gu_in{b}") for b in range(2)]
        d_in = [ph.sem(f"d_in{b}") for b in range(2)]
        x_in = [nc.alloc_semaphore(f"moe{layer}_x_in{b}") for b in range(2)]
        y_out = [nc.alloc_semaphore(f"moe{layer}_y_out{b}") for b in range(2)]
        block = ph.block()
        view_g = e["moe_w_gate"][layer].rearrange("x (p k) n -> x p k n", k=KD)
        view_u = e["moe_w_up"][layer].rearrange("x (p k) n -> x p k n", k=KD)
        view_d = e["moe_w_down"][layer].rearrange("x (k p) n -> x p k n", p=P)

        def count_of(eng):
            return eng.value_load(r["count"][0:1, 0:1], min_val=0, max_val=nb)

        @block.sync
        def _(sp):
            n = count_of(sp)
            with sp.Fori(0, nb // 2) as i2:
                for b in range(2):
                    i = 2 * i2 + b
                    with sp.If(i < n):
                        x = sp.value_load(r["expert"][0:1, bass.ds(i, 1)], min_val=0, max_val=NE - 1)
                        sp.wait_ge(s["downed"], i + 1)
                        sp.sem_inc(s["issue"], 1)
                        sp.dma_start(wg[b][:], view_g[bass.ds(x, 1)].rearrange(
                            "o p k n -> (o p) k n")).then_inc(gu_in[b], 16)
                        sp.dma_start(wu[b][:], view_u[bass.ds(x, 1)].rearrange(
                            "o p k n -> (o p) k n")).then_inc(gu_in[b], 16)
                        sp.dma_start(wd[b][:], view_d[bass.ds(x, 1)].rearrange(
                            "o p k n -> (o p) k n")).then_inc(d_in[b], 16)

        @block.gpsimd
        def _(pool):
            nc.gpsimd.memset(xg[0][:], 0.0).then_inc(s["cleared"], 1)
            nc.gpsimd.memset(xg[1][:], 0.0).then_inc(s["cleared"], 1)
            pool.wait_ge(s["cleared"], 2)
            n = count_of(pool)
            last_token = pool.to_reg(NT * P - 1)
            last_result = pool.to_reg(2 * NT * P - 1)

            def fetch(b, i):
                nc.gpsimd.tensor_copy(idx[b][:], r["index"][:, :, bass.ds(i, 1)].rearrange(
                    "p z o -> p (z o)")).then_inc(s["idx_done"], 1)
                pool.wait_ge(s["idx_done"], i + 1)
                pool.sem_inc(s["indexed"], 1)
                nc.gpsimd.indirect_dma_start(
                    xg[b][:], None, e["h_dram"],
                    bass.IndirectOffsetOnAxis(ap=idx[b][:, 0:1], axis=0),
                    bounds_check=last_token, oob_is_err=False).then_inc(x_in[b], 16)

            fetch(0, 0)
            with pool.Fori(0, nb // 2) as i2:
                for b in range(2):
                    i = 2 * i2 + b
                    with pool.If(i < n):
                        pool.wait_ge(s["turned_x"], 2 * i + 2)
                        fetch(1 - b, i + 1)
                        pool.wait_ge(s["y_done"], 2 * i + 3)
                        pool.sem_inc(s["indexed"], 1)
                        nc.gpsimd.indirect_dma_start(
                            e["y_dram"], bass.IndirectOffsetOnAxis(ap=idx[b][:, 1:2], axis=0),
                            y[b][:], None, bounds_check=last_result,
                            oob_is_err=False).then_inc(y_out[b], 16)
                        pool.wait_ge(y_out[b], 16 * (i2 + 1))
                        pool.sem_inc(s["y_free"], 1)

        @block.tensor
        def _(pe):
            n = count_of(pe)
            pe.sem_inc(s["downed"], 2)

            def turn_x(b, half):
                for q in range(4):
                    tr = nc.tensor.transpose(tp[half][:, q, :], xg[b][:, 4 * half + q:D:KD],
                                             e["ident"][:])
                tr.then_inc(s["turned_x"], 1)

            pe.wait_ge(x_in[0], 16)
            turn_x(0, 0)
            turn_x(0, 1)
            with pe.Fori(0, nb // 2) as i2:
                for b in range(2):
                    i = 2 * i2 + b
                    with pe.If(i < n):
                        pe.wait_ge(gu_in[b], 32 * (i2 + 1))
                        pe.wait_ge(s["read_x"], 2 * i + 2)
                        pe.wait_ge(s["hid_done"], 2 * i + 1)
                        for f in range(2):
                            cols = slice(f * HF, (f + 1) * HF)
                            for k in range(KD):
                                mm = nc.tensor.matmul(gate[f][:], xg_t[b][:, k, :],
                                                      wg[b][:, k, cols], start=(k == 0),
                                                      stop=(k == KD - 1))
                            mm.then_inc(s["gated"], 1)
                            for k in range(KD):
                                mm = nc.tensor.matmul(up[f][:], xg_t[b][:, k, :],
                                                      wu[b][:, k, cols], start=(k == 0),
                                                      stop=(k == KD - 1))
                            mm.then_inc(s["upped"], 1)
                        pe.wait_ge(d_in[b], 16 * (i2 + 1))
                        pe.wait_ge(s["y_done"], 2 * i + 1)
                        for f in range(2):
                            pe.wait_ge(s["hid_done"], 2 * i + f + 2)
                            for k in (2 * f, 2 * f + 1):
                                tr = nc.tensor.transpose(tp[f][:, k % 2, :],
                                                         hid[:, k * P:(k + 1) * P], e["ident"][:])
                            tr.then_inc(s["turned_h"], 1)
                            if f == 1:
                                pe.wait_ge(x_in[1 - b], 16 * (i2 + 1 + b))
                                turn_x(1 - b, 0)
                            pe.wait_ge(s["read_h"], 2 * i + f + 1)
                            if f == 1:
                                turn_x(1 - b, 1)
                            for c in range(2):
                                for k in (2 * f, 2 * f + 1):
                                    mm = nc.tensor.matmul(
                                        down[c][:], hid_t[:, k, :],
                                        wd[b][:, k, c * NCHUNK:(c + 1) * NCHUNK],
                                        start=(k == 0), stop=(k == 3), skip_group_check=True)
                        mm.then_inc(s["downed"], 1)

        @block.scalar
        def _(act):
            n = count_of(act)

            def read_x(b, i):
                for half in range(2):
                    act.wait_ge(s["turned_x"], 2 * i + 1 + half)
                    nc.scalar.copy(xg_t[b][:, 4 * half:4 * half + 4, :], tp[half][:]).then_inc(
                        s["read_x"], 1)

            read_x(0, 0)
            with act.Fori(0, nb // 2) as i2:
                for b in range(2):
                    i = 2 * i2 + b
                    with act.If(i < n):
                        act.wait_ge(s["hid_done"], 2 * i + 1)
                        for f in range(2):
                            act.wait_ge(s["gated"], 2 * i + f + 1)
                            nc.scalar.activation(sig[:, f * HF:(f + 1) * HF], gate[f][:], ACT.Exp,
                                                 scale=-1.0).then_inc(s["expd"], 1)
                        for f in range(2):
                            act.wait_ge(s["turned_h"], 2 * i + f + 1)
                            nc.scalar.copy(hid_t[:, 2 * f:2 * f + 2, :],
                                           tp[f][:, 0:2, :]).then_inc(s["read_h"], 1)
                        read_x(1 - b, i + 1)

        @block.vector
        def _(dve):
            n = count_of(dve)
            dve.sem_inc(s["y_free"], 2)
            dve.sem_inc(s["hid_done"], 1)
            dve.sem_inc(s["y_done"], 1)
            with dve.Fori(0, nb // 2) as i2:
                for b in range(2):
                    i = 2 * i2 + b
                    with dve.If(i < n):
                        for f in range(2):
                            half = sig[:, f * HF:(f + 1) * HF]
                            at = 6 * i + 3 * f
                            dve.wait_ge(s["expd"], 2 * i + f + 1)
                            nc.vector.tensor_scalar(half, half, 1.0, None, ALU.add).then_inc(
                                s["step"], 1)
                            dve.wait_ge(s["step"], at + 1)
                            nc.vector.reciprocal(half, half).then_inc(s["step"], 1)
                            dve.wait_ge(s["step"], at + 2)
                            nc.vector.tensor_tensor(half, half, gate[f][:], ALU.mult).then_inc(
                                s["step"], 1)
                            dve.wait_ge(s["step"], at + 3)
                            dve.wait_ge(s["upped"], 2 * i + f + 1)
                            nc.vector.tensor_tensor(hid[:, f * HF:(f + 1) * HF], half, up[f][:],
                                                    ALU.mult).then_inc(s["hid_done"], 1)
                        dve.wait_ge(s["downed"], i + 3)
                        dve.wait_ge(s["y_free"], i + 1)
                        for c in range(2):
                            nc.vector.tensor_copy(y[b][:, c * NCHUNK:(c + 1) * NCHUNK],
                                                  down[c][:]).then_inc(s["y_done"], 1)


def combine_experts(nc, e, layer, tiles, r, gate):
    nt = len(tiles)
    vecs = sorted({0 if t >= TC else 1 for t in tiles})
    with Phase(nc, f"comb{layer}") as ph:
        ys = ph.sb("ys", [P, 4, 2, D])
        gates = ph.sb("gates", [P, 2, D])
        vec_in, step, used = ph.sem("vec_in"), ph.sem("step"), ph.sem("used")
        y_in = [ph.sem(f"y_in{i}") for i in range(4)]
        block = ph.block()

        @block.sync
        def _(sp):
            for v in vecs:
                sp.dma_start(gates[:, v, :], bcast_rows(gate(v))).then_inc(vec_in, 16)
            src = e["y_dram"].rearrange("(a t p) d -> t p a d", a=2, p=P)
            for i, t in enumerate(tiles):
                if i >= 4:
                    sp.wait_ge(used, i - 3)
                sp.dma_start(ys[:, i % 4, :, :], src[t]).then_inc(y_in[i % 4], 16)

        @block.vector
        def _(dve):
            link = Chain(dve, step)
            dve.wait_ge(vec_in, 16 * len(vecs))
            for i, t in enumerate(tiles):
                v = 0 if t >= TC else 1
                a, b = ys[:, i % 4, 0, :], ys[:, i % 4, 1, :]
                dve.wait_ge(y_in[i % 4], 16 * (i // 4 + 1))
                link(nc.vector.tensor_scalar(a, a, r["weight"][:, 0, i:i + 1], None, ALU.mult))
                link(nc.vector.scalar_tensor_tensor(a, b, r["weight"][:, 1, i:i + 1], a, ALU.mult,
                                                    ALU.add))
                link(nc.vector.tensor_tensor(a, a, gates[:, v, :], ALU.mult))
                nc.vector.tensor_tensor(e["res"][:, t, :], e["res"][:, t, :], a, ALU.add).then_inc(used, 1)


def moe_layer(nc, e, layer, tiles):
    mod = lambda part: (lambda v: e["mod_dram"][v, (layer * 6 + part) * D:(layer * 6 + part + 1) * D])
    with ExitStack() as stack:
        nb = max_blocks(len(tiles))
        r = dict(
            index=stack.enter_context(nc.sbuf_tensor(f"r_index{layer}", [P, 2, nb + 2], I32)),
            expert=stack.enter_context(nc.sbuf_tensor(f"r_expert{layer}", [1, nb], I32)),
            count=stack.enter_context(nc.sbuf_tensor(f"r_count{layer}", [1, 1], I32)),
            weight=stack.enter_context(nc.sbuf_tensor(f"r_weight{layer}", [P, 2, NT], F32)))
        with nc.sbuf_tensor(f"h2_t{layer}", [P, KD, len(tiles) * P], F32) as h_t:
            normalise(nc, e, f"norm2_{layer}", tiles, e["norm2_g"][layer],
                      lambda v: (mod(3)(v), mod(4)(v)), h_t, store=e["h_dram"])
            route(nc, e, layer, tiles, h_t, r)
        experts(nc, e, layer, len(tiles), r)
        combine_experts(nc, e, layer, tiles, r, mod(5))


def layer_0(nc, e):
    mod = lambda part: (lambda v: e["mod_dram"][v, part * D:(part + 1) * D])
    tiles = list(range(NT))
    sb = nc.sbuf_tensor
    with sb("a_q", [P, 8, NT * P], F32) as q_t, sb("a_k", [P, 8, NT * P], F32) as k_t, \
            sb("a_v", [P, NT, D], F32) as v:
        with sb("a_h", [P, KD, NT * P], F32) as h_t:
            normalise(nc, e, "norm1_0", tiles, e["norm1_g"][0], lambda v_: (mod(0)(v_), mod(1)(v_)), h_t)

            def stores(c, t):
                if c >= 4:
                    return v[:, t, (c - 4) * NCHUNK:(c - 3) * NCHUNK]
                dst = (q_t if c < 2 else k_t)[:, 4 * (c % 2):4 * (c % 2) + 4, t * P:(t + 1) * P]
                return dst, (0.125 if c < 2 else 1.0)

            items = [(c, t, "value" if c >= 4 else "rope" if t >= TC else "plain")
                     for c in range(6) for t in tiles]
            project_heads(nc, e, "qkv0", h_t, e["a_w_qkv"][0], items, stores)
        with sb("a_o", [P, NT, D], F32) as o:
            diff_attention(nc, e, q_t, k_t, v, o)
            project_out(nc, e, "out0", o, tiles, 8, e["a_subln_g"][0], 1.0 - LAM_INIT, e["a_w_o"][0], mod(2))
    moe_layer(nc, e, 0, tiles)


def layer_1(nc, e):
    mod = lambda part: (lambda v: e["mod_dram"][v, (6 + part) * D:(7 + part) * D])
    stream = list(range(TC, NT))
    sb = nc.sbuf_tensor
    with sb("b_q", [P, 8, NT * P], F32) as q_t, sb("b_k", [P, 4, NT * P], F32) as k_t, \
            sb("b_v", [P, NT, 4 * HD], F32) as v:
        with sb("b_h", [P, KD, NT * P], F32) as h_t:
            normalise(nc, e, "norm1_1", list(range(NT)), e["norm1_g"][1],
                      lambda v_: (mod(0)(v_), mod(1)(v_)), h_t)

            def stores(c, t):
                if c == 2:
                    return k_t[:, :, t * P:(t + 1) * P], 1.0
                return q_t[:, 4 * c:4 * c + 4, t * P:(t + 1) * P], 0.125

            items = [(c, t, "rope") for c in range(2) for t in stream]
            items += [(2, t, "shared") for t in range(NT)]
            project_heads(nc, e, "qkv1", h_t, e["b_w_qkv"][0], items, stores, lambda t: v[:, t, :])
        with sb("b_o", [P, NT, D], F32) as o:
            units = []
            for b in range(TX):
                lo, hi = max(0, b - 1), min(TX, b + 2)
                tiles = [*range(TC), *range(TC + lo, TC + hi)]
                for head in range(NH):
                    rows = slice(HD * (head % 2), HD * (head % 2) + HD)
                    kv = head // 4
                    keys = []
                    for j0 in range(0, len(tiles), 4):
                        j = j0
                        while j < min(j0 + 4, len(tiles)):
                            k = j
                            while k + 1 < min(j0 + 4, len(tiles)) and tiles[k + 1] == tiles[k] + 1:
                                k += 1
                            keys.append((j * P, k_t[rows, kv, tiles[j] * P:(tiles[k] + 1) * P],
                                         (k - j + 1) * P))
                            j = k + 1
                    units.append(dict(
                        q=q_t[rows, head // 2, (TC + b) * P:(TC + b + 1) * P], keys=keys,
                        width=len(tiles) * P, mask=b, mask0=0, head=head,
                        values=[v[:, j, kv * HD:(kv + 1) * HD] for j in tiles]))
            masked_attention(
                nc, e, "swa", units, [TX, 640], e["c_band"].rearrange("b p n -> p b n"),
                [(0, e["b_sink"][0])],
                lambda g: o[:, TC + g // 2, (g % 2) * NCHUNK:(g % 2 + 1) * NCHUNK].rearrange(
                    "p (h d) -> p h d", d=HD))
            project_out(nc, e, "out1", o, stream, None, None, 1.0, e["b_w_o"][0], mod(2))
    moe_layer(nc, e, 1, stream)


def project_in(nc, e, h_t, hh):
    chunks = [(n0, min(NCHUNK, QKV2 - n0)) for n0 in range(0, QKV2, NCHUNK)]
    with Phase(nc, "in2") as ph:
        w = ph.sb("w", [P, 3, KD, NCHUNK])
        acc = [ph.ps(f"acc{i}", [P, NCHUNK]) for i in range(4)]
        loaded = [ph.sem(f"loaded{i}") for i in range(3)]
        mm_done, read = ph.sem("mm_done"), ph.sem("read")
        block = ph.block()

        @block.sync
        def _(sp):
            stream_weights(sp, w, e["w_in_2"][0].rearrange("(k p) n -> p k n", p=P), chunks, loaded,
                           mm_done, TX)

        @block.tensor
        def _(pe):
            for j in range(len(chunks) * TX):
                c, t = j // TX, j % TX
                width = chunks[c][1]
                if t == 0:
                    pe.wait_ge(loaded[c % 3], 16 * (c // 3 + 1))
                if j >= 4:
                    pe.wait_ge(read, j - 3)
                for k in range(KD):
                    mm = nc.tensor.matmul(acc[j % 4][:, 0:width], h_t[:, k, t * P:(t + 1) * P],
                                          w[:, c % 3, k, 0:width], start=(k == 0),
                                          stop=(k == KD - 1))
                mm.then_inc(mm_done, 1)

        @block.scalar
        def _(act):
            for j in range(len(chunks) * TX):
                n0, width = chunks[j // TX]
                act.wait_ge(mm_done, j + 1)
                nc.scalar.copy(hh[:, j % TX, n0:n0 + width], acc[j % 4][:, 0:width]).then_inc(read, 1)


RUNS2 = [(0, 8), (1184, 8), (1952, 6)]
GAINS2 = [("moba_q_g_2", 0, 4), ("moba_k_g_2", 256, 4), ("dil_q_g_2", 1184, 4),
          ("dil_k_g_2", 1440, 4), ("swa_q_g_2", 1952, 4), ("swa_k_g_2", 2208, 2)]
LATENTS = [("mla_qlat_g_2", 768, 256), ("mla_kvlat_g_2", 1024, 128)]
ROPE_COLS = (1152, 32)
VALUES2 = (512, 1696, 2336)
QK = 96


def heads_of(ap, width):
    return ap.rearrange("p t (h d) -> p t h d", d=width)


def over(ap, n):
    return ap.unsqueeze(3).broadcast_to([*ap.shape, n])


def gain_over(ap, t, h):
    return ap.unsqueeze(1).unsqueeze(1).broadcast_to([ap.shape[0], t, h, ap.shape[1]])


def prepare_heads(nc, e, hh, mq, mk, mv):
    with Phase(nc, "prep2") as ph:
        sq = ph.sb("sq", [P, TX, QKV2])
        ss, std, rstd, tmp = (ph.sb(x, [P, TX, 22]) for x in ("ss", "std", "rstd", "tmp"))
        sl, stl, rsl, tml = (ph.sb(x, [P, 2, TX]) for x in ("sl", "stl", "rsl", "tml"))
        gains = ph.sb("gains", [P, 6, HD])
        lat_g = ph.sb("lat_g", [P, 384])
        eps = ph.sb("eps", [P, 1])
        w_uq = ph.sb("w_uq", [P, 2, 4 * QK])
        w_ukv = ph.sb("w_ukv", [P, 4 * P])
        lat_t = ph.sb("lat_t", [P, TX, 3, P])
        tp = [ph.ps(f"tp{i}", [P, 3, P]) for i in range(2)]
        pq = [ph.ps(f"pq{i}", [P, 4 * QK]) for i in range(2)]
        pkv = [ph.ps(f"pkv{i}", [P, 4 * P]) for i in range(2)]
        names = "const_in w_in sq_done eps_done summed std_done lat_done tp_done tp_read q_done kv_done q_read kv_read step"
        s = {x: ph.sem(x) for x in names.split()}
        block = ph.block()

        @block.sync
        def _(sp):
            for j, (name, _, _) in enumerate(GAINS2):
                sp.dma_start(gains[:, j, :], bcast_rows(e["small"][name])).then_inc(s["const_in"], 16)
            for name, c0, width in LATENTS:
                sp.dma_start(lat_g[:, c0 - 768:c0 - 768 + width],
                             bcast_rows(e["small"][name])).then_inc(s["const_in"], 16)
            sp.dma_start(w_uq[:], e["mla_w_uq_2"][0].rearrange("(k p) n -> p k n", p=P)).then_inc(
                s["w_in"], 16)
            sp.dma_start(w_ukv[:], e["mla_w_ukv_2"][0]).then_inc(s["w_in"], 16)

        @block.scalar
        def _(act):
            for t in range(TX):
                nc.scalar.activation(sq[:, t, :], hh[:, t, :], ACT.Square).then_inc(s["sq_done"], 1)
            act.wait_ge(s["eps_done"], 1)
            act.wait_ge(s["summed"], 5)
            nc.scalar.activation(std[:], ss[:], ACT.Sqrt, scale=1.0 / HD, bias=eps[:]).then_inc(
                s["std_done"], 1)
            for j, (_, _, width) in enumerate(LATENTS):
                nc.scalar.activation(stl[:, j, :], sl[:, j, :], ACT.Sqrt, scale=1.0 / width,
                                     bias=eps[:]).then_inc(s["std_done"], 1)
            for t in range(TX):
                act.wait_ge(s["tp_done"], t + 1)
                nc.scalar.copy(lat_t[:, t, :, :], tp[t % 2][:]).then_inc(s["tp_read"], 1)
            for t in range(TX):
                act.wait_ge(s["q_done"], t + 1)
                nc.scalar.copy(mq[:, t, :, :].rearrange("p h d -> p (h d)"), pq[t % 2][:]).then_inc(
                    s["q_read"], 1)

        @block.vector
        def _(dve):
            v = nc.vector
            link = Chain(dve, s["step"])
            v.memset(eps[:], EPS).then_inc(s["eps_done"], 1)
            dve.wait_ge(s["sq_done"], TX)
            h0 = 0
            for c0, n in RUNS2:
                v.tensor_reduce(ss[:, :, h0:h0 + n], heads_of(sq[:, :, c0:c0 + n * HD], HD), AX.X,
                                ALU.add).then_inc(s["summed"], 1)
                h0 += n
            for j, (_, c0, width) in enumerate(LATENTS):
                v.tensor_reduce(sl[:, j, :], sq[:, :, c0:c0 + width], AX.X, ALU.add).then_inc(
                    s["summed"], 1)
            dve.wait_ge(s["std_done"], 3)
            dve.wait_ge(s["const_in"], 16 * 8)
            for j, (_, _, width) in enumerate(LATENTS):
                rsqrt_mean(v, link, rsl[:, j, :], stl[:, j, :], sl[:, j, :], tml[:, j, :], 1.0 / width)
            for j, (_, c0, width) in enumerate(LATENTS):
                x = hh[:, :, c0:c0 + width]
                link(v.tensor_tensor(x, x, inner(rsl[:, j, :], width), ALU.mult))
                v.tensor_tensor(x, x, middle(lat_g[:, c0 - 768:c0 - 768 + width], TX),
                                ALU.mult).then_inc(s["lat_done"], 1)
            rsqrt_mean(v, link, rstd[:], std[:], ss[:], tmp[:], 1.0 / HD)
            h0 = 0
            for c0, n in RUNS2:
                x = heads_of(hh[:, :, c0:c0 + n * HD], HD)
                link(v.tensor_tensor(x, x, over(rstd[:, :, h0:h0 + n], HD), ALU.mult))
                h0 += n
            for j, (_, c0, n) in enumerate(GAINS2):
                x = heads_of(hh[:, :, c0:c0 + n * HD], HD)
                link(v.tensor_tensor(x, x, gain_over(gains[:, j, :], TX, n), ALU.mult))
            for t in range(TX):
                dve.wait_ge(s["kv_done"], t + 1)
                both = pkv[t % 2][:].rearrange("p (h d) -> p h d", d=P)
                link(v.tensor_copy(mk[:, t, :, 0:HD], both[:, :, 0:HD]))
                link(v.tensor_copy(mk[:, t, :, HD:QK],
                                   middle(hh[:, t, ROPE_COLS[0]:sum(ROPE_COLS)], 4)))
                v.tensor_copy(mv[:, t, :, :], both[:, :, HD:P]).then_inc(s["kv_read"], 1)

        @block.tensor
        def _(pe):
            pe.wait_ge(s["lat_done"], 2)
            pe.wait_ge(s["w_in"], 32)
            for t in range(TX):
                if t >= 2:
                    pe.wait_ge(s["tp_read"], t - 1)
                for k in range(3):
                    tr = nc.tensor.transpose(tp[t % 2][:, k, :],
                                             hh[:, t, 768 + k * P:768 + (k + 1) * P], e["ident"][:])
                tr.then_inc(s["tp_done"], 1)
            for t in range(TX):
                pe.wait_ge(s["tp_read"], t + 1)
                if t >= 2:
                    pe.wait_ge(s["q_read"], t - 1)
                    pe.wait_ge(s["kv_read"], t - 1)
                for k in range(2):
                    mm = nc.tensor.matmul(pq[t % 2][:], lat_t[:, t, k, :], w_uq[:, k, :],
                                          start=(k == 0), stop=(k == 1))
                mm.then_inc(s["q_done"], 1)
                nc.tensor.matmul(pkv[t % 2][:], lat_t[:, t, 2, :], w_ukv[:], start=True,
                                 stop=True).then_inc(s["kv_done"], 1)


def turn_heads(nc, e, hh, mq, mk, q_t, k_t):
    with Phase(nc, "turn2") as ph:
        sq = ph.sb("sq", [P, 2, TX, 4, QK])
        ss, std, rstd, tms = (ph.sb(x, [P, 2, TX, 4]) for x in ("ss", "std", "rstd", "tms"))
        tmp = ph.sb("tmp", [P, TX, 4, 32])
        gains = ph.sb("gains", [P, 2, QK])
        line = ph.sb("line", [P, 2, TX, 32])
        dk = ph.sb("dk", [P, TX, 4, HD])
        eps = ph.sb("eps", [P, 1])
        tp = [ph.ps(f"tp{i}", [P, TX, P]) for i in range(4)]
        names = "const_in sq_done summed std_done eps_done ready dk_done tp_done tp_read step"
        s = {x: ph.sem(x) for x in names.split()}
        block = ph.block()
        pair = lambda c0, t: hh[:, t, c0:c0 + P]
        jobs = []
        for which, (a, c, d) in enumerate([(0, 1184, 1952), (256, 1440, None)]):
            sc = (1.0, 0.125)[which == 0]
            for j in range(2):
                jobs.append((lambda t, x=a + j * P: pair(x, t), P, which, j, sc))
                jobs.append((lambda t, x=c + j * P: pair(x, t), P, which, 6 + j, sc))
                if d is not None:
                    jobs.append((lambda t, x=d + j * P: pair(x, t), P, which, 8 + j, sc))
                else:
                    jobs.append((lambda t, j=j: dk[:, t, 2 * j:2 * j + 2, :].rearrange(
                        "p h d -> p (h d)"), P, which, 8 + j, sc))
        early = len(jobs)
        for which, m in enumerate([mq, mk]):
            for h in range(4):
                jobs.append((lambda t, m=m, h=h: m[:, t, h, :], QK, which, 2 + h,
                             QK ** -0.5 if which == 0 else 1.0))

        @block.sync
        def _(sp):
            sp.dma_start(gains[:, 0, :], bcast_rows(e["small"]["mla_q_g_2"])).then_inc(s["const_in"], 16)
            sp.dma_start(gains[:, 1, :], bcast_rows(e["small"]["mla_k_g_2"])).then_inc(s["const_in"], 16)
            sp.dma_start(line[:], e["c_line"].rearrange("s (t p) d -> p s t d", p=P)).then_inc(
                s["const_in"], 16)

        @block.scalar
        def _(act):
            for j, m in enumerate([mq, mk]):
                nc.scalar.activation(sq[:, j], m[:], ACT.Square).then_inc(s["sq_done"], 1)
            act.wait_ge(s["eps_done"], 1)
            act.wait_ge(s["summed"], 2)
            nc.scalar.activation(std[:], ss[:], ACT.Sqrt, scale=1.0 / QK, bias=eps[:]).then_inc(
                s["std_done"], 1)
            for j, (_, rows, which, slot, scale) in enumerate(jobs):
                act.wait_ge(s["tp_done"], j + 1)
                dst = (q_t, k_t)[which][0:rows, slot, :].rearrange("p (t n) -> p t n", n=P)
                nc.scalar.activation(dst, tp[j % 4][0:rows], ACT.Copy, scale=scale).then_inc(
                    s["tp_read"], 1)

        @block.vector
        def _(dve):
            v = nc.vector
            link = Chain(dve, s["step"])
            v.memset(eps[:], EPS).then_inc(s["eps_done"], 1)
            for c in range(2):
                v.tensor_copy(dk[:, :, c:4:2, :], heads_of(hh[:, :, 2208:2336], HD)).then_inc(
                    s["dk_done"], 1)
            for j in range(2):
                dve.wait_ge(s["sq_done"], j + 1)
                v.tensor_reduce(ss[:, j], sq[:, j], AX.X, ALU.add).then_inc(s["summed"], 1)
            dve.wait_ge(s["const_in"], 48)
            dve.wait_ge(s["std_done"], 1)
            rsqrt_mean(v, link, rstd[:], std[:], ss[:], tms[:], 1.0 / QK)
            for j, m in enumerate([mq, mk]):
                link(v.tensor_tensor(m[:], m[:], over(rstd[:, j], QK), ALU.mult))
                link(v.tensor_tensor(m[:], m[:], gain_over(gains[:, j, :], TX, 4), ALU.mult))
                x = m[:, :, :, HD:QK]
                wide = lambda ap: ap.unsqueeze(2).broadcast_to([P, TX, 4, ap.shape[2]])
                link(v.tensor_tensor(tmp[:, :, :, 0:16], x[:, :, :, 16:32],
                                     wide(line[:, 1, :, 0:16]), ALU.mult))
                link(v.tensor_tensor(tmp[:, :, :, 16:32], x[:, :, :, 0:16],
                                     wide(line[:, 1, :, 16:32]), ALU.mult))
                link(v.tensor_tensor(x, x, wide(line[:, 0]), ALU.mult))
                last = v.tensor_tensor(x, x, tmp[:], ALU.add)
                if j == 0:
                    link(last)
                else:
                    last.then_inc(s["ready"], 1)

        @block.tensor
        def _(pe):
            pe.wait_ge(s["dk_done"], 2)
            for j, (src, rows, _, _, _) in enumerate(jobs):
                if j == early:
                    pe.wait_ge(s["ready"], 1)
                if j >= 4:
                    pe.wait_ge(s["tp_read"], j - 3)
                for t in range(TX):
                    tr = nc.tensor.transpose(tp[j % 4][0:rows, t, :], src(t), e["ident"][:])
                tr.then_inc(s["tp_done"], 1)


def mlp(nc, e):
    with nc.sbuf_tensor("m_h", [P, KD, SEQ], F32) as h_t:
        normalise(nc, e, "norm_mlp", list(range(TC, NT)), e["mlp_norm_g_2"][0], None, h_t)
        with Phase(nc, "mlp") as ph:
            ring, groups = 4, FF // NCHUNK
            w = ph.sb("w", [P, ring, 4096])
            u_t = ph.sb("u_t", [P, FF // P, SEQ])
            acc = [ph.ps(f"acc{i}", [P, NCHUNK]) for i in range(8)]
            loaded = [ph.sem(f"loaded{i}") for i in range(ring)]
            group_used, up_done, up_read = ph.sem("group_used"), ph.sem("up_done"), ph.sem("up_read")
            squared = ph.sem("squared")
            down_done, added, stored = ph.sem("down_done"), ph.sem("added"), ph.sem("stored")
            block = ph.block()
            up_view = e["w_up_2"][0].rearrange("(k p) n -> p k n", p=P)
            down_view = e["w_down_2"][0].rearrange("(k p) n -> p k n", p=P)

            @block.sync
            def _(sp):
                for j in range(2 * groups):
                    g = j % groups
                    if j >= ring:
                        sp.wait_ge(group_used, j - ring + 1)
                    if j < groups:
                        dst = w[:, j % ring, :].rearrange("p (k n) -> p k n", k=KD)
                        src = up_view[:, :, g * NCHUNK:(g + 1) * NCHUNK]
                    else:
                        dst = w[:, j % ring, :].rearrange("p (k n) -> p k n", k=4)
                        src = down_view[:, 4 * g:4 * g + 4, :]
                    sp.dma_start(dst, src).then_inc(loaded[j % ring], 16)
                rows = e["out"][0].rearrange("(t p) d -> p t d", p=P)
                for t in range(TX):
                    sp.wait_ge(added, 2 * t + 2)
                    sp.dma_start(rows[:, t, :], e["res"][:, TC + t, :]).then_inc(stored, 16)
                sp.wait_ge(stored, 16 * TX)

            @block.tensor
            def _(pe):
                for j in range(groups):
                    pe.wait_ge(loaded[j % ring], 16 * (j // ring + 1))
                    wj = w[:, j % ring, :].rearrange("p (k n) -> p k n", k=KD)
                    for q in range(4):
                        i = 4 * j + q
                        if i >= 8:
                            pe.wait_ge(up_read, i - 7)
                        for k in range(KD):
                            mm = nc.tensor.matmul(acc[i % 8][:], wj[:, k, q * P:(q + 1) * P],
                                                  h_t[:, k, :], start=(k == 0), stop=(k == KD - 1))
                        mm.then_inc(up_done, 1)
                    pe.wait_ge(up_done, 4 * j + 4)
                    pe.sem_inc(group_used, 1)
                pe.wait_ge(squared, 4 * groups)
                for j in range(groups):
                    b = (groups + j) % ring
                    pe.wait_ge(loaded[b], 16 * ((groups + j) // ring + 1))
                    wj = w[:, b, :].rearrange("p (k n) -> p k n", k=4)
                    for q in range(4):
                        f = 4 * j + q
                        for t in range(TX):
                            for c in range(2):
                                mm = nc.tensor.matmul(acc[2 * t + c][:],
                                                      u_t[:, f, t * P:(t + 1) * P],
                                                      wj[:, q, c * NCHUNK:(c + 1) * NCHUNK],
                                                      start=(f == 0), stop=(f == FF // P - 1),
                                                      skip_group_check=True)
                                if f == FF // P - 1:
                                    mm.then_inc(down_done, 1)
                                elif q == 3 and (t, c) == (TX - 1, 1):
                                    mm.then_inc(group_used, 1)

            @block.scalar
            def _(act):
                for i in range(4 * groups):
                    act.wait_ge(up_done, i + 1)
                    nc.scalar.activation(u_t[:, i, :], acc[i % 8][:], ACT.Relu).then_inc(up_read, 1)

            @block.vector
            def _(dve):
                for i in range(4 * groups):
                    dve.wait_ge(up_read, i + 1)
                    nc.vector.tensor_tensor(u_t[:, i, :], u_t[:, i, :], u_t[:, i, :],
                                            ALU.mult).then_inc(squared, 1)
                for i in range(2 * TX):
                    t, c = i // 2, i % 2
                    dst = e["res"][:, TC + t, c * NCHUNK:(c + 1) * NCHUNK]
                    dve.wait_ge(down_done, i + 1)
                    nc.vector.tensor_tensor(dst, dst, acc[i][:], ALU.add).then_inc(added, 1)


def block_2(nc, e):
    stream = list(range(TC, NT))
    sb = nc.sbuf_tensor
    with sb("c_hh", [P, TX, QKV2], F32) as hh, sb("c_mv", [P, TX, 4, HD], F32) as mv:
        with sb("c_h", [P, KD, SEQ], F32) as h_t:
            normalise(nc, e, "norm_in2", stream, e["attn_norm_g_2"][0], None, h_t, final=e["final_g"])
            project_in(nc, e, h_t, hh)
        with sb("c_q", [P, 10, SEQ], F32) as q_t, sb("c_k", [P, 10, SEQ], F32) as k_t:
            with sb("c_mq", [P, TX, 4, QK], F32) as mq, sb("c_mk", [P, TX, 4, QK], F32) as mk:
                prepare_heads(nc, e, hh, mq, mk, mv)
                turn_heads(nc, e, hh, mq, mk, q_t, k_t)
            with sb("c_o", [P, NT, D], F32) as o:
                units = []
                for b in range(TX):
                    for head in range(NH):
                        kind, h = head // 4, head % 4
                        slot = {0: h // 2, 1: 2 + h, 2: 6 + h // 2, 3: 8 + h // 2}[kind]
                        rows = slice(0, QK) if kind == 1 else slice(HD * (h % 2), HD * (h % 2) + HD)
                        first = max(0, b - 1) if kind == 3 else 0
                        width = (b + 1 - first) * P
                        if kind == 1:
                            values = [mv[:, j, h, :] for j in range(first, b + 1)]
                        else:
                            c0 = {0: VALUES2[0] + h * HD, 2: VALUES2[1] + h * HD,
                                  3: VALUES2[2] + h // 2 * HD}[kind]
                            values = [hh[:, j, c0:c0 + HD] for j in range(first, b + 1)]
                        units.append(dict(
                            q=q_t[rows, slot, b * P:(b + 1) * P],
                            keys=[(0, k_t[rows, slot, first * P:(b + 1) * P], width)],
                            width=width, mask=(h, 4, 5 + h, 9 + h)[kind], mask0=512 - width,
                            head=head, values=values))
                masked_attention(
                    nc, e, "att2", units, [13, 512], e["c_bias2"].rearrange("h p n -> p h n"),
                    [(0, e["c_neg"]), (12, e["small"]["swa_sinks_2"])],
                    lambda g: o[:, TC + g // 2, (g % 2) * NCHUNK:(g % 2 + 1) * NCHUNK].rearrange(
                        "p (h d) -> p h d", d=HD))
                project_out(nc, e, "out2", o, stream, 4,
                            e["group_out_g_2"][0].rearrange("a d -> (a d)"), 1.0, e["w_o_2"][0], None)
    mlp(nc, e)


def build(nc, e, upto=3):
    e["res"] = nc.alloc_sbuf_tensor("res", [P, NT, D], F32).ap()
    e["ident"] = nc.alloc_sbuf_tensor("ident_sb", [P, P], F32).ap()
    e["ones"] = nc.alloc_sbuf_tensor("ones_sb", [P, P], F32).ap()
    load_constants(nc, e)
    modulation(nc, e)
    if upto >= 1:
        layer_0(nc, e)
    if upto >= 2:
        layer_1(nc, e)
    if upto >= 3:
        block_2(nc, e)



_INS = ["x", "c", "ctx", "c_ctx", "mod_w", "mod_b", "norm1_g", "norm2_g", "a_w_qkv", "a_w_o",
        "a_lam", "a_subln_g", "b_w_qkv", "b_w_o", "b_sink", "moe_router_g", "moe_router_g_b",
        "moe_router_e", "moe_router_e_b", "moe_w_gate", "moe_w_up", "moe_w_down", "final_g",
        "attn_norm_g_2", "w_in_2", "mla_w_uq_2", "mla_w_ukv_2", "group_out_g_2", "w_o_2",
        "mlp_norm_g_2", "w_up_2", "w_down_2"]
_SMALL = ["moba_q_g_2", "moba_k_g_2", "mla_qlat_g_2", "mla_kvlat_g_2", "mla_q_g_2", "mla_k_g_2",
          "dil_q_g_2", "dil_k_g_2", "swa_q_g_2", "swa_k_g_2", "swa_sinks_2"]


def kernel(**inputs):
    import concourse.bacc as bacc
    from concourse.bass_utils import run_bass_kernel_spmd

    nc = bacc.Bacc("TRN2", target_bir_lowering=False, num_devices=1)
    arrays, e = {}, {"small": {}}

    def give(name, a):
        arrays[name] = np.ascontiguousarray(a)
        return nc.dram_tensor(name, a.shape, F32, kind="ExternalInput").ap()

    for name in _INS:
        e[name] = give(f"in_{name}", inputs[name])
    for name in _SMALL:
        e["small"][name] = give(f"in_{name}", inputs[name])[0]
    for name, a in constants().items():
        e[f"c_{name}"] = give(f"const_{name}", a)
    e["out"] = nc.dram_tensor("result", (1, SEQ, D), F32, kind="ExternalOutput").ap()
    e["mod_dram"] = nc.dram_tensor("mod_scratch", (2, LAYERS * 6 * D), F32, kind="Internal").ap()
    e["h_dram"] = nc.dram_tensor("moe_tokens", (NT * P, D), F32, kind="Internal").ap()
    e["y_dram"] = nc.dram_tensor("moe_results", (2 * NT * P, D), F32, kind="Internal").ap()
    build(nc, e)
    r = run_bass_kernel_spmd(nc, [arrays], core_ids=[0])
    return r.results[0]["result"]
```

```python
import math
from contextlib import ExitStack

import numpy as np

import concourse.bass as bass
from concourse import mybir

F32 = mybir.dt.float32
I32 = mybir.dt.int32
ALU = mybir.AluOpType
ACT = mybir.ActivationFunctionType
AX = mybir.AxisListType

P = 128
D = 1024
KD = D // P
SEQ, CTX = 512, 256
TX, TC = SEQ // P, CTX // P
NT = TX + TC
HD = 64
NH = D // HD
HALVES = (slice(0, HD), slice(HD, P))
NCHUNK = 512
EPS = 1e-6
NEG = -1e30
LAYERS = 2
NE, NG, EPG = 32, 4, 8
FE = 512
BIG = 8192.0
FF = 4096
QKV2 = 2464
LOG2E = 1.4426950408889634
LN2_HI, LN2_LO = 0.693359375, -2.12194440054690583e-4
ROUND = 1.5 * 2.0 ** 23 + 127.0
LAM_INIT = 0.8 - 0.6 * math.exp(0.0)



def rope_table(angles, copies):
    cos, sin = np.cos(angles), np.sin(angles)
    both = np.stack([np.concatenate([cos, cos], -1), np.concatenate([-sin, sin], -1)])
    return both.reshape(2, angles.shape[0], copies * 2 * angles.shape[-1]).astype(np.float32)


def constants():
    f = np.float32
    out = {"ident": np.eye(P, dtype=f)}
    t = np.arange(SEQ)
    inv = (1.0 / (f(10000.0) ** (np.arange(16, dtype=f) / f(16)))).astype(f)
    pos = np.stack([t // 64, t % 64], -1).astype(f)
    out["axial"] = rope_table((pos[:, :, None] * inv).astype(f), 2)
    inv = (1.0 / (f(10000.0) ** (np.arange(0, 32, 2, dtype=f) / f(32)))).astype(f)
    out["line"] = rope_table((t.astype(f)[:, None] * inv).astype(f), 1)
    q = np.arange(P)[:, None]
    band = np.zeros((TX, P, 640), f)
    for b in range(TX):
        k = np.arange(max(0, b - 1) * P, min(TX, b + 2) * P)[None, :]
        band[b, :, CTX:CTX + k.shape[1]] = np.where(np.abs(k - b * P - q) <= 128, 0, NEG)
    out["band"] = band
    slopes = np.exp2(-8.0 * np.arange(1, 13, dtype=f).reshape(4, 3) / 12).astype(f)
    dist = q + 384 - np.arange(512)[None, :]
    tables = []
    for h in range(4):
        tables.append(np.where(dist >= 0, -slopes[h, 0] * dist.astype(f), NEG))
    tables.append(np.where(dist >= 0, 0, NEG))
    n = ((dist >= 0) & (dist <= 128)).astype(int) + ((dist >= 0) & (dist % 4 == 0)) + (
        (dist >= 0) & (dist % 16 == 0))
    for h in range(4):
        tables.append(np.where(n > 0, -slopes[h, 1] * dist.astype(f) + np.log(np.maximum(n, 1)), NEG))
    for h in range(4):
        tables.append(np.where((dist >= 0) & (dist < 128), -slopes[h, 2] * dist.astype(f), NEG))
    out["bias2"] = np.stack(tables).astype(f)
    out["before"] = np.triu(np.ones((P, P), f), 1)
    out["ones"] = np.ones((P, P), f)
    out["iota"] = np.broadcast_to(np.arange(P, dtype=f), (P, P)).copy()
    rows = np.arange(NT * P).reshape(NT, P).T
    out["neg"] = np.full((12,), NEG, f)
    out["rowid"] = (np.stack([rows, rows, rows + NT * P], 1) - BIG).astype(f)
    return out



class Phase:

    def __init__(self, nc, name):
        self.nc, self.name, self.stack, self.sems = nc, name, ExitStack(), []

    def sb(self, name, shape, dt=F32):
        return self.stack.enter_context(self.nc.sbuf_tensor(f"{self.name}_{name}", shape, dt))

    def ps(self, name, shape):
        return self.stack.enter_context(self.nc.psum_tensor(f"{self.name}_{name}", shape, F32))

    def sem(self, name):
        self.sems.append(self.nc.alloc_semaphore(f"{self.name}_{name}"))
        return self.sems[-1]

    def block(self):
        return self.stack.enter_context(self.nc.Block())

    def __enter__(self):
        return self

    def __exit__(self, *e):
        self.stack.close()
        numbers = sorted(sem.num for sem in self.sems)
        while numbers:
            n = next((i for i, x in enumerate(numbers) if x != numbers[0] + i), len(numbers))
            self.nc.gpsimd.sem_clear(range(numbers[0], numbers[0] + n))
            numbers = numbers[n:]
        for sem in self.sems:
            self.nc.release_semaphore(sem)


class Chain:

    def __init__(self, eng, sem):
        self.eng, self.sem, self.n = eng, sem, 0

    def __call__(self, ins):
        self.n += 1
        ins.then_inc(self.sem, 1)
        self.eng.wait_ge(self.sem, self.n)


def rsqrt_mean(v, link, out, std, ss, tmp, scale):
    link(v.reciprocal(out, std))
    link(v.tensor_scalar(tmp, ss, scale, EPS, ALU.mult, ALU.add))
    link(v.tensor_tensor(tmp, tmp, out, ALU.mult))
    link(v.tensor_tensor(tmp, tmp, out, ALU.mult))
    link(v.tensor_scalar(tmp, tmp, -0.5, 1.5, ALU.mult, ALU.add))
    link(v.tensor_tensor(out, out, tmp, ALU.mult))


def bcast_rows(vec):
    return vec.partition_broadcast(P)


def inner(ap, n):
    return ap.unsqueeze(2).broadcast_to([ap.shape[0], ap.shape[1], n])


def middle(ap, n):
    return ap.unsqueeze(1).broadcast_to([ap.shape[0], n, ap.shape[1]])


def stream_weights(sp, buffers, view, chunks, loaded, mm_done, per_chunk):
    ring = buffers.shape[1]
    for j, (n0, width) in enumerate(chunks):
        if j >= ring:
            sp.wait_ge(mm_done, (j - ring + 1) * per_chunk)
        sp.dma_start(buffers[:, j % ring, :, 0:width], view[:, :, n0:n0 + width]).then_inc(
            loaded[j % ring], 16)



def load_constants(nc, e):
    with Phase(nc, "load") as ph:
        arrived = ph.sem("arrived")
        block = ph.block()

        @block.sync
        def _(sp):
            loads = [
                (e["res"][:, TC:NT, :], e["x"][0].rearrange("(t p) d -> p t d", p=P)),
                (e["res"][:, 0:TC, :], e["ctx"][0].rearrange("(t p) d -> p t d", p=P)),
                (e["ident"][:], e["c_ident"]), (e["ones"][:], e["c_ones"]),
            ]
            for dst, src in loads:
                sp.dma_start(dst, src).then_inc(arrived, 16)
            sp.wait_ge(arrived, 16 * len(loads))


def modulation(nc, e):
    per_layer = 6 * D // NCHUNK
    chunks = LAYERS * per_layer
    ring = 3
    with Phase(nc, "mod") as ph:
        vec = ph.sb("vec", [P, 2, KD])
        expn, whole, rest = (ph.sb(x, [P, 2, KD]) for x in ("expn", "whole", "rest"))
        act = ph.sb("act", [P, KD, 2])
        w = ph.sb("w", [P, ring, KD, NCHUNK])
        bias = ph.sb("bias", [2, LAYERS * 6 * D])
        rows = ph.sb("rows", [2, LAYERS * 6 * D])
        acc = [ph.ps(f"acc{i}", [P, NCHUNK]) for i in range(4)]
        vec_in, bias_in, stored = ph.sem("vec_in"), ph.sem("bias_in"), ph.sem("stored")
        exp_done, act_done, step = ph.sem("exp_done"), ph.sem("act_done"), ph.sem("step")
        rest_done = ph.sem("rest_done")
        loaded = [ph.sem(f"loaded{i}") for i in range(ring)]
        mm_done, rows_done = ph.sem("mm_done"), ph.sem("rows_done")
        block = ph.block()

        @block.sync
        def _(sp):
            sp.dma_start(vec[:, 0, :], e["c"][0].rearrange("(p k) -> p k", k=KD)).then_inc(vec_in, 16)
            sp.dma_start(vec[:, 1, :], e["c_ctx"].rearrange("(p k) -> p k", k=KD)).then_inc(vec_in, 16)
            sp.dma_start(bias[:], e["mod_b"].rearrange("l n -> (l n)").partition_broadcast(2)).then_inc(
                bias_in, 16)
            for j in range(chunks):
                if j >= ring:
                    sp.wait_ge(mm_done, j - ring + 1)
                layer, n0 = j // per_layer, j % per_layer * NCHUNK
                src = e["mod_w"][layer].rearrange("(p k) n -> p k n", k=KD)
                sp.dma_start(w[:, j % ring, :, :], src[:, :, n0:n0 + NCHUNK]).then_inc(
                    loaded[j % ring], 16)
            sp.wait_ge(rows_done, chunks)
            sp.dma_start(e["mod_dram"], rows[:]).then_inc(stored, 16)
            sp.wait_ge(stored, 16)

        @block.scalar
        def _(act_eng):
            act_eng.wait_ge(rest_done, 1)
            nc.scalar.activation(expn[:], rest[:], ACT.Exp, scale=0.25).then_inc(exp_done, 1)

        @block.vector
        def _(dve):
            link = Chain(dve, step)
            v = nc.vector
            dve.wait_ge(vec_in, 32)
            link(v.tensor_scalar(rest[:], vec[:], -1.0, None, ALU.mult))
            link(v.tensor_scalar(rest[:], rest[:], 80.0, -80.0, ALU.min, ALU.max))
            link(v.tensor_scalar(whole[:], rest[:], LOG2E, ROUND, ALU.mult, ALU.add))
            link(v.tensor_scalar(expn[:], whole[:], ROUND, None, ALU.subtract))
            link(v.scalar_tensor_tensor(rest[:], expn[:], -LN2_HI, rest[:], ALU.mult, ALU.add))
            v.scalar_tensor_tensor(rest[:], expn[:], -LN2_LO, rest[:], ALU.mult, ALU.add).then_inc(
                rest_done, 1)
            link(v.tensor_single_scalar(whole[:].bitcast(I32), whole[:].bitcast(I32), 23,
                                        ALU.logical_shift_left))
            dve.wait_ge(exp_done, 1)
            link(v.tensor_tensor(expn[:], expn[:], expn[:], ALU.mult))
            link(v.tensor_tensor(expn[:], expn[:], expn[:], ALU.mult))
            link(v.tensor_tensor(expn[:], expn[:], whole[:], ALU.mult))
            link(nc.vector.tensor_scalar(expn[:], expn[:], 1.0, None, ALU.add))
            link(nc.vector.reciprocal(expn[:], expn[:]))
            nc.vector.tensor_tensor(act[:].rearrange("p k v -> p v k"), vec[:], expn[:],
                                    ALU.mult).then_inc(act_done, 1)
            dve.wait_ge(bias_in, 16)
            for j in range(chunks):
                n0 = j * NCHUNK
                dve.wait_ge(mm_done, j + 1)
                nc.vector.tensor_tensor(rows[:, n0:n0 + NCHUNK], acc[j % 4][0:2, :],
                                        bias[:, n0:n0 + NCHUNK], ALU.add).then_inc(rows_done, 1)

        @block.tensor
        def _(pe):
            pe.wait_ge(act_done, 1)
            for j in range(chunks):
                pe.wait_ge(loaded[j % ring], 16 * (j // ring + 1))
                if j >= 4:
                    pe.wait_ge(rows_done, j - 3)
                for k in range(KD):
                    mm = nc.tensor.matmul(acc[j % 4][0:2, :], act[:, k, :], w[:, j % ring, k, :],
                                          start=(k == 0), stop=(k == KD - 1))
                mm.then_inc(mm_done, 1)


def normalise(nc, e, name, tiles, gain, shift_scale, h_t, strided=False, store=None, final=None):
    vecs = sorted({0 if t >= TC else 1 for t in tiles}) if shift_scale else []
    nt = len(tiles)
    with Phase(nc, name) as ph:
        g = ph.sb("g", [P, D])
        gf = ph.sb("gf", [P, D]) if final is not None else None
        mul = ph.sb("mul", [P, 2, D])
        add = ph.sb("add", [P, 2, D])
        h = ph.sb("h", [P, 2, D])
        sq = ph.sb("sq", [P, 2, D])
        part = ph.sb("part", [P, 32])
        ss = ph.sb("ss", [P, 2, nt])
        rstd = ph.sb("rstd", [P, 2, nt])
        std = ph.sb("std", [P, 2, nt])
        tmp = ph.sb("tmp", [P, nt])
        eps = ph.sb("eps", [P, 1])
        tp = [ph.ps(f"tp{i}", [P, 4, P]) for i in range(4)]
        vec_in, stored = ph.sem("vec_in"), [ph.sem(f"stored{i}") for i in range(2)]
        sq_done, std_done, summed = ph.sem("sq_done"), ph.sem("std_done"), ph.sem("summed")
        eps_done, ready = ph.sem("eps_done"), ph.sem("ready")
        step, h_done, tp_done, tp_read = (ph.sem(s) for s in ("step", "h_done", "tp_done", "tp_read"))
        block = ph.block()
        n_vec = 1 + (final is not None) + 2 * len(vecs)

        @block.sync
        def _(sp):
            sp.dma_start(g[:], bcast_rows(gain)).then_inc(vec_in, 16)
            if final is not None:
                sp.dma_start(gf[:], bcast_rows(final)).then_inc(vec_in, 16)
            for v in vecs:
                shift, scale = shift_scale(v)
                sp.dma_start(add[:, v, :], bcast_rows(shift)).then_inc(vec_in, 16)
                sp.dma_start(mul[:, v, :], bcast_rows(scale)).then_inc(vec_in, 16)
            if store is not None:
                for i, t in enumerate(tiles):
                    sp.wait_ge(h_done, i + 1)
                    sp.dma_start(store[t * P:(t + 1) * P, :], h[:, i % 2, :]).then_inc(
                        stored[i % 2], 16)
                for b in range(2):
                    sp.wait_ge(stored[b], 16 * (nt // 2))

        @block.scalar
        def _(act):
            act.wait_ge(eps_done, 1)
            for rnd in range(2 if final is not None else 1):
                if rnd:
                    act.wait_ge(ready, nt)
                for i, t in enumerate(tiles):
                    j = rnd * nt + i
                    if j >= 2:
                        act.wait_ge(summed, j - 1)
                    nc.scalar.activation(sq[:, j % 2, :], e["res"][:, t, :], ACT.Square).then_inc(
                        sq_done, 1)
                act.wait_ge(summed, (rnd + 1) * nt)
                nc.scalar.activation(std[:, rnd, :], ss[:, rnd, :], ACT.Sqrt, scale=1.0 / D,
                                     bias=eps[:]).then_inc(std_done, 1)
            for j in range(2 * nt):
                i, half = j // 2, j % 2
                act.wait_ge(tp_done, j + 1)
                nc.scalar.copy(h_t[:, 4 * half:4 * half + 4, i * P:(i + 1) * P],
                               tp[j % 4][:]).then_inc(tp_read, 1)

        @block.vector
        def _(dve):
            link = Chain(dve, step)
            nc.vector.memset(eps[:], EPS).then_inc(eps_done, 1)

            def sum_squares(rnd):
                for i in range(nt):
                    j = rnd * nt + i
                    dve.wait_ge(sq_done, j + 1)
                    link(nc.vector.tensor_reduce(
                        part[:], sq[:, j % 2, :].rearrange("p (a b) -> p a b", b=32), AX.X, ALU.add))
                    nc.vector.tensor_reduce(ss[:, rnd, i:i + 1], part[:], AX.X, ALU.add).then_inc(
                        summed, 1)
                    dve.wait_ge(summed, j + 1)

            sum_squares(0)
            dve.wait_ge(vec_in, 16 * n_vec)
            for v in vecs:
                link(nc.vector.scalar_tensor_tensor(mul[:, v, :], mul[:, v, :], 1.0, g[:],
                                                    ALU.add, ALU.mult))
            if final is not None:
                dve.wait_ge(std_done, 1)
                rsqrt_mean(nc.vector, link, rstd[:, 0, :], std[:, 0, :], ss[:, 0, :], tmp[:], 1.0 / D)
                for i, t in enumerate(tiles):
                    nc.vector.scalar_tensor_tensor(
                        e["res"][:, t, :], e["res"][:, t, :], rstd[:, 0, i:i + 1], gf[:],
                        ALU.mult, ALU.mult).then_inc(ready, 1)
                dve.wait_ge(ready, nt)
                sum_squares(1)
            rnd = int(final is not None)
            dve.wait_ge(std_done, rnd + 1)
            rsqrt_mean(nc.vector, link, rstd[:, rnd, :], std[:, rnd, :], ss[:, rnd, :], tmp[:], 1.0 / D)
            for i, t in enumerate(tiles):
                v = 0 if t >= TC else 1
                if i >= 2:
                    dve.wait_ge(tp_done, 2 * (i - 1))
                    if store is not None:
                        dve.wait_ge(stored[i % 2], 16 * (i // 2))
                out = h[:, i % 2, :]
                if not vecs:
                    nc.vector.scalar_tensor_tensor(out, e["res"][:, t, :], rstd[:, rnd, i:i + 1],
                                                   g[:], ALU.mult, ALU.mult).then_inc(h_done, 1)
                    continue
                link(nc.vector.scalar_tensor_tensor(out, e["res"][:, t, :], rstd[:, rnd, i:i + 1],
                                                    mul[:, v, :], ALU.mult, ALU.mult))
                nc.vector.tensor_tensor(out, out, add[:, v, :], ALU.add).then_inc(h_done, 1)

        @block.tensor
        def _(pe):
            for j in range(2 * nt):
                i, half = j // 2, j % 2
                pe.wait_ge(h_done, i + 1)
                if j >= 4:
                    pe.wait_ge(tp_read, j - 3)
                for q in range(4):
                    k = 4 * half + q
                    src = h[:, i % 2, k:D:KD] if strided else h[:, i % 2, k * P:(k + 1) * P]
                    tr = nc.tensor.transpose(tp[j % 4][:, q, :], src, e["ident"][:])
                tr.then_inc(tp_done, 1)


def rope_heads(dve, nc, link, out, src, tmp, cos, sin, half):
    heads, width = src.shape[1], src.shape[2]
    pairs = width // (2 * half)
    link(nc.vector.tensor_tensor(out, src, middle(cos, heads), ALU.mult))
    for side in range(2):
        for a in range(pairs):
            lo, other = (2 * a + side) * half, (2 * a + 1 - side) * half
            op = nc.vector.tensor_tensor(tmp[:, :, lo:lo + half], src[:, :, other:other + half],
                                         middle(sin[:, lo:lo + half], heads), ALU.mult)
            if (side, a) != (1, pairs - 1):
                op.then_inc(link.sem, 1)
                link.n += 1
            else:
                link(op)
    return nc.vector.tensor_tensor(out, out, tmp, ALU.add)


def project_heads(nc, e, name, h_t, w_dram, items, stores, keys, values=None):
    chunks = sorted({c for c, _, _ in items})
    ends = [max(i for i, it in enumerate(items) if it[0] == c) + 1 for c in chunks]
    ring, stages = 3, 3
    with Phase(nc, name) as ph:
        w = ph.sb("w", [P, ring, KD, NCHUNK])
        rope = ph.sb("rope", [P, 2, TX, HD])
        stage = ph.sb("stage", [P, stages, 8, HD])
        tmp = ph.sb("tmp", [P, 8, HD])
        acc = [ph.ps(f"acc{i}", [P, NCHUNK]) for i in range(4)]
        tp = [ph.ps(f"tp{i}", [P, 4, P]) for i in range(2)]
        loaded = [ph.sem(f"loaded{i}") for i in range(ring)]
        rope_in, mm_done, acc_read = ph.sem("rope_in"), ph.sem("mm_done"), ph.sem("acc_read")
        zeroed = ph.sem("zeroed")
        tp_done, tp_read, step = ph.sem("tp_done"), ph.sem("tp_read"), ph.sem("step")
        block = ph.block()
        turned = [i for i, it in enumerate(items) if it[2] != "value"]
        reads = [0]
        for i in turned:
            reads.append(reads[-1] + len(stores(items[i][0], items[i][1])[0]))

        @block.gpsimd
        def _(pool):
            for side in range(2):
                other = slice(HD * (1 - side), HD * (2 - side))
                nc.gpsimd.memset(keys[other, side], 0.0).then_inc(zeroed, 1)
                pool.wait_ge(zeroed, side + 1)

        @block.sync
        def _(sp):
            view = w_dram.rearrange("(k p) n -> p k n", p=P)
            for j, c in enumerate(chunks):
                if j >= ring:
                    sp.wait_ge(mm_done, ends[j - ring])
                sp.dma_start(w[:, j % ring, :, :],
                             view[:, :, c * NCHUNK:(c + 1) * NCHUNK]).then_inc(loaded[j % ring], 16)
                if j == 0:
                    sp.dma_start(rope[:], e["c_axial"].rearrange("s (t p) d -> p s t d", p=P)).then_inc(
                        rope_in, 16)

        @block.tensor
        def _(pe):
            def turn(j):
                i = turned[j]
                pe.wait_ge(acc_read, i + 1)
                if j >= 2:
                    pe.wait_ge(tp_read, reads[j - 1])
                for q in range(4):
                    tr = nc.tensor.transpose(
                        tp[j % 2][:, q, :],
                        stage[:, j % stages, 2 * q:2 * q + 2, :].rearrange("p a d -> p (a d)"),
                        e["ident"][:])
                tr.then_inc(tp_done, 1)

            last, j = None, 0
            for i, (c, t, kind) in enumerate(items):
                b = chunks.index(c)
                if c != last:
                    pe.wait_ge(loaded[b % ring], 16 * (b // ring + 1))
                    last = c
                if i >= 4:
                    pe.wait_ge(acc_read, i - 3)
                for k in range(KD):
                    mm = nc.tensor.matmul(acc[i % 4][:], h_t[:, k, t * P:(t + 1) * P],
                                          w[:, b % ring, k, :], start=(k == 0), stop=(k == KD - 1))
                mm.then_inc(mm_done, 1)
                if j < len(turned) and turned[j] <= i - 1:
                    turn(j)
                    j += 1
            while j < len(turned):
                turn(j)
                j += 1

        @block.vector
        def _(dve):
            link = Chain(dve, step)
            dve.wait_ge(rope_in, 16)
            j = 0
            for i, (c, t, kind) in enumerate(items):
                dve.wait_ge(mm_done, i + 1)
                if kind == "value":
                    nc.vector.tensor_copy(stores(c, t), acc[i % 4][:]).then_inc(acc_read, 1)
                    continue
                if j >= stages:
                    dve.wait_ge(tp_done, j - stages + 1)
                dst = stage[:, j % stages, :, :]
                src = acc[i % 4][:].rearrange("p (h d) -> p h d", d=HD)
                j += 1
                if kind == "plain":
                    nc.vector.tensor_copy(dst, src).then_inc(acc_read, 1)
                elif kind == "shared":
                    twice = dst.rearrange("p (g c) d -> p g c d", c=2)
                    first, keys = twice[:, :, 0, :], src[:, 0:4, :]
                    if t < TC:
                        link(nc.vector.tensor_copy(first, keys))
                    else:
                        link(rope_heads(dve, nc, link, first, keys, tmp[:, 0:4, :],
                                        rope[:, 0, t - TC, :], rope[:, 1, t - TC, :], 16))
                    link(nc.vector.tensor_copy(twice[:, :, 1, :], first))
                    nc.vector.tensor_copy(values(t), acc[i % 4][:, 4 * HD:8 * HD]).then_inc(
                        acc_read, 1)
                elif kind == "rope":
                    rope_heads(dve, nc, link, dst, src, tmp[:], rope[:, 0, t - TC, :],
                               rope[:, 1, t - TC, :], 16).then_inc(acc_read, 1)

        @block.scalar
        def _(act):
            for j, i in enumerate(turned):
                c, t, kind = items[i]
                act.wait_ge(tp_done, j + 1)
                parts, scale = stores(c, t)
                for rows, dst in parts:
                    nc.scalar.activation(dst, tp[j % 2][rows], ACT.Copy, scale=scale).then_inc(
                        tp_read, 1)


def diff_attention(nc, e, q_t, k_t, v, o):
    pairs = [(t, h) for t in [*range(TC, NT), *range(TC)] for h in range(8)]
    n = len(pairs)
    keys = lambda t: NT if t >= TC else TC
    with Phase(nc, "dif") as ph:
        lam_v = ph.sb("lam_v", [P, 4, HD])
        lam_p = ph.sb("lam_p", [P, 2, HD])
        lam = ph.sb("lam", [P, 4])
        prob = ph.sb("prob", [P, 2, 2, NT * P])
        prob_t = ph.sb("prob_t", [P, 2, NT, P])
        neg_max = ph.sb("neg_max", [P, 2, 2])
        total = ph.sb("total", [P, 2, 2])
        score = [ph.ps(f"score{i}", [P, 1024]) for i in range(2)]
        tp_a, tp_b = ph.ps("tp_a", [P, 4, P]), ph.ps("tp_b", [P, 4, P])
        out = [ph.ps(f"out{i}", [P, NCHUNK]) for i in range(2)]
        names = "lam_in lam_exp lam_done scored maxed exped combined turned read_a read_b weighed out_read step"
        s = {x: ph.sem(x) for x in names.split()}
        block = ph.block()

        @block.sync
        def _(sp):
            sp.dma_start(lam_v[:].rearrange("p a d -> p (a d)"),
                         e["a_lam"][0].rearrange("a d -> (a d)").partition_broadcast(P)).then_inc(
                             s["lam_in"], 16)

        @block.tensor
        def _(pe):
            def scores(g, m):
                t, h = pairs[g]
                if g >= 1:
                    pe.wait_ge(s["exped"], 2 * g + m - 1)
                width = keys(t) * P
                for n0 in range(0, width, NCHUNK):
                    w = min(NCHUNK, width - n0)
                    mm = nc.tensor.matmul(score[m][:, n0:n0 + w],
                                          q_t[:, h, t * P:(t + 1) * P],
                                          k_t[:, m, h, n0:n0 + w], start=True, stop=True)
                mm.then_inc(s["scored"], 1)

            def turn(g):
                t, h = pairs[g]
                pe.wait_ge(s["combined"], g + 1)
                if g >= 1:
                    pe.wait_ge(s["read_a"], g)
                    pe.wait_ge(s["read_b"], g)
                for k in range(keys(t)):
                    bank = tp_a if k < 4 else tp_b
                    tr = nc.tensor.transpose(bank[:, k % 4, :], prob[:, g % 2, 0, k * P:(k + 1) * P],
                                             e["ident"][:])
                tr.then_inc(s["turned"], 1)

            def weigh(g):
                t, h = pairs[g]
                if g >= 2:
                    pe.wait_ge(s["out_read"], g - 1)
                pe.wait_ge(s["read_a"], g + 1)
                pe.wait_ge(s["read_b"], g + 1)
                for k in range(keys(t)):
                    mm = nc.tensor.matmul(out[g % 2][:, 0:P], prob_t[:, g % 2, k, :],
                                          v[:, k, h * P:(h + 1) * P], start=(k == 0),
                                          stop=(k == keys(t) - 1))
                mm.then_inc(s["weighed"], 1)

            scores(0, 0)
            for g in range(n + 1):
                if g < n:
                    scores(g, 1)
                if g >= 1:
                    turn(g - 1)
                if g + 1 < n:
                    scores(g + 1, 0)
                if g >= 1:
                    weigh(g - 1)

        @block.vector
        def _(dve):
            link = Chain(dve, s["step"])
            dve.wait_ge(s["lam_in"], 16)
            link(nc.vector.tensor_tensor(lam_p[:], lam_v[:, 0:4:2, :], lam_v[:, 1:4:2, :], ALU.mult))
            nc.vector.tensor_reduce(lam[:, 0:2], lam_p[:], AX.X, ALU.add).then_inc(s["lam_done"], 1)
            dve.wait_ge(s["lam_exp"], 1)
            link(nc.vector.tensor_tensor(lam[:, 3:4], lam[:, 1:2], lam[:, 0:1], ALU.subtract))
            link(nc.vector.tensor_scalar(lam[:, 3:4], lam[:, 3:4], -LAM_INIT, None, ALU.add))

            def maximum(g, m):
                t, _ = pairs[g]
                dve.wait_ge(s["scored"], 2 * g + m + 1)
                if g >= 2:
                    dve.wait_ge(s["exped"], 2 * (g - 2) + m + 1)
                nc.vector.tensor_reduce(neg_max[:, g % 2, m:m + 1], score[m][:, 0:keys(t) * P],
                                        AX.X, ALU.max, negate=True).then_inc(s["maxed"], 1)

            def combine(g):
                t, _ = pairs[g]
                width = keys(t) * P
                dve.wait_ge(s["exped"], 2 * g + 2)
                tot = total[:, g % 2, :]
                link(nc.vector.reciprocal(tot, tot))
                link(nc.vector.tensor_tensor(tot[:, 1:2], tot[:, 1:2], lam[:, 3:4], ALU.mult))
                a, b = prob[:, g % 2, 0, 0:width], prob[:, g % 2, 1, 0:width]
                link(nc.vector.tensor_scalar(a, a, tot[:, 0:1], None, ALU.mult))
                nc.vector.scalar_tensor_tensor(a, b, tot[:, 1:2], a, ALU.mult, ALU.add).then_inc(
                    s["combined"], 1)

            def read_b(g):
                t, _ = pairs[g]
                dve.wait_ge(s["turned"], g + 1)
                if g >= 2:
                    dve.wait_ge(s["weighed"], g - 1)
                if keys(t) > 4:
                    nc.vector.tensor_copy(prob_t[:, g % 2, 4:keys(t), :],
                                          tp_b[:, 0:keys(t) - 4, :]).then_inc(s["read_b"], 1)
                else:
                    dve.sem_inc(s["read_b"], 1)

            def read_out(g):
                t, h = pairs[g]
                dve.wait_ge(s["weighed"], g + 1)
                nc.vector.tensor_copy(o[:, t, h * P:(h + 1) * P], out[g % 2][:, 0:P]).then_inc(
                    s["out_read"], 1)

            maximum(0, 0)
            for g in range(n + 1):
                if g < n:
                    maximum(g, 1)
                if g >= 1:
                    read_b(g - 1)
                if g + 1 < n:
                    maximum(g + 1, 0)
                if g < n:
                    combine(g)
                if g >= 1:
                    read_out(g - 1)

        @block.scalar
        def _(act):
            act.wait_ge(s["lam_done"], 1)
            nc.scalar.activation(lam[:, 0:2], lam[:, 0:2], ACT.Exp).then_inc(s["lam_exp"], 1)

            def exponential(g, m):
                t, _ = pairs[g]
                width = keys(t) * P
                if m == 0 and g >= 2:
                    act.wait_ge(s["combined"], g - 1)
                    act.wait_ge(s["turned"], g - 1)
                act.wait_ge(s["maxed"], 2 * g + m + 1)
                nc.scalar.activation(prob[:, g % 2, m, 0:width], score[m][:, 0:width],
                                     ACT.Exp, bias=neg_max[:, g % 2, m:m + 1],
                                     accum_out=total[:, g % 2, m:m + 1]).then_inc(s["exped"], 1)

            exponential(0, 0)
            for g in range(n + 1):
                if g < n:
                    exponential(g, 1)
                if g >= 1:
                    act.wait_ge(s["turned"], g)
                    if g >= 3:
                        act.wait_ge(s["weighed"], g - 2)
                    k = min(4, keys(pairs[g - 1][0]))
                    nc.scalar.copy(prob_t[:, (g - 1) % 2, 0:k, :], tp_a[:, 0:k, :]).then_inc(
                        s["read_a"], 1)
                if g + 1 < n:
                    exponential(g + 1, 0)


def masked_attention(nc, e, name, units, mask, mask_src, sink_src, o):
    n = len(units)
    groups = n // 8
    with Phase(nc, name) as ph:
        masks = ph.sb("masks", [P, *mask])
        sinks = ph.sb("sinks", [P, NH])
        masked = ph.sb("masked", [P, 2, 640])
        prob = ph.sb("prob", [P, 2, 640])
        prob_t = ph.sb("prob_t", [P, 2, 5, P])
        top = ph.sb("top", [P, 2, 8])
        neg_top = ph.sb("neg_top", [P, 2, 8])
        total = ph.sb("total", [P, 2, 8])
        sink_e = ph.sb("sink_e", [P, 2, 8])
        score = [ph.ps(f"score{i}", [P, 1024]) for i in range(2)]
        tp_a, tp_b = ph.ps("tp_a", [P, 4, P]), ph.ps("tp_b", [P, 4, P])
        out = [ph.ps(f"out{i}", [P, 8, HD]) for i in range(2)]
        names = ("const_in scored masked topped exped turned read_a read_b weighed sink_d sink_x "
                 "out_read step")
        s = {x: ph.sem(x) for x in names.split()}
        block = ph.block()
        n_sink = len(sink_src)

        @block.sync
        def _(sp):
            sp.dma_start(masks[:], mask_src).then_inc(s["const_in"], 16)
            for dst0, src in sink_src:
                sp.dma_start(sinks[:, dst0:dst0 + src.shape[0]], bcast_rows(src)).then_inc(
                    s["const_in"], 16)

        @block.tensor
        def _(pe):
            def scores(u):
                unit = units[u]
                if u >= 2:
                    pe.wait_ge(s["masked"], u - 1)
                for col, rhs, w in unit["keys"]:
                    mm = nc.tensor.matmul(score[u % 2][:, col:col + w], unit["q"], rhs,
                                          start=True, stop=True)
                mm.then_inc(s["scored"], 1)

            def turn(u):
                kt = units[u]["width"] // P
                pe.wait_ge(s["exped"], u + 1)
                if u >= 1:
                    pe.wait_ge(s["read_a"], u)
                    pe.wait_ge(s["read_b"], u)
                for k in range(kt):
                    bank = tp_a if k < 4 else tp_b
                    tr = nc.tensor.transpose(bank[:, k % 4, :], prob[:, u % 2, k * P:(k + 1) * P],
                                             e["ident"][:])
                tr.then_inc(s["turned"], 1)

            def weigh(u):
                unit, g = units[u], u // 8
                kt = unit["width"] // P
                if u % 8 == 0 and g >= 2:
                    pe.wait_ge(s["out_read"], g - 1)
                pe.wait_ge(s["read_a"], u + 1)
                pe.wait_ge(s["read_b"], u + 1)
                for k in range(kt):
                    mm = nc.tensor.matmul(out[g % 2][:, u % 8, :], prob_t[:, u % 2, k, :],
                                          unit["values"][k], start=(k == 0), stop=(k == kt - 1))
                mm.then_inc(s["weighed"], 1)

            scores(0)
            scores(1)
            for u in range(n):
                turn(u)
                if u + 2 < n:
                    scores(u + 2)
                weigh(u)

        @block.vector
        def _(dve):
            link = Chain(dve, s["step"])
            dve.wait_ge(s["const_in"], 16 * (1 + n_sink))

            def mask_and_max(u):
                unit, g = units[u], u // 8
                dve.wait_ge(s["scored"], u + 1)
                if u >= 2:
                    dve.wait_ge(s["exped"], u - 1)
                if u % 8 == 0 and g >= 2:
                    dve.wait_ge(s["sink_x"], g - 1)
                col = top[:, g % 2, u % 8:u % 8 + 1]
                nc.vector.tensor_tensor_reduce(
                    masked[:, u % 2, 0:unit["width"]], score[u % 2][:, 0:unit["width"]],
                    masks[:, unit["mask"], unit["mask0"]:unit["mask0"] + unit["width"]], 1.0,
                    sinks[:, unit["head"]:unit["head"] + 1], ALU.add, ALU.max, col).then_inc(s["masked"], 1)
                dve.wait_ge(s["masked"], u + 1)
                nc.vector.tensor_scalar(neg_top[:, g % 2, u % 8:u % 8 + 1], col, -1.0, None,
                                        ALU.mult).then_inc(s["topped"], 1)

            def read_b(u):
                unit = units[u]
                dve.wait_ge(s["turned"], u + 1)
                if u >= 2:
                    dve.wait_ge(s["weighed"], u - 1)
                if unit["width"] > 4 * P:
                    nc.vector.tensor_copy(prob_t[:, u % 2, 4:5, :], tp_b[:, 0:1, :]).then_inc(
                        s["read_b"], 1)
                else:
                    dve.sem_inc(s["read_b"], 1)

            def finish(g):
                head = units[8 * g]["head"]
                dve.wait_ge(s["topped"], 8 * g + 8)
                if g >= 2:
                    dve.wait_ge(s["sink_x"], g - 1)
                nc.vector.tensor_tensor(sink_e[:, g % 2, :], sinks[:, head:head + 8],
                                        top[:, g % 2, :], ALU.subtract).then_inc(s["sink_d"], 1)
                dve.wait_ge(s["sink_x"], g + 1)
                dve.wait_ge(s["exped"], 8 * g + 8)
                tot = total[:, g % 2, :]
                link(nc.vector.tensor_tensor(tot, tot, sink_e[:, g % 2, :], ALU.add))
                link(nc.vector.reciprocal(tot, tot))
                dve.wait_ge(s["weighed"], 8 * g + 8)
                nc.vector.tensor_tensor(o(g), out[g % 2][:], inner(tot, HD), ALU.mult).then_inc(
                    s["out_read"], 1)

            mask_and_max(0)
            mask_and_max(1)
            for u in range(n + 1):
                if u < n:
                    read_b(u)
                if u + 2 < n:
                    mask_and_max(u + 2)
                if u >= 8 and u % 8 == 0:
                    finish(u // 8 - 1)

        @block.scalar
        def _(act):
            def exponential(u):
                unit, g = units[u], u // 8
                if u >= 2:
                    act.wait_ge(s["turned"], u - 1)
                if u % 8 == 0 and g >= 2:
                    act.wait_ge(s["out_read"], g - 1)
                act.wait_ge(s["topped"], u + 1)
                nc.scalar.activation(prob[:, u % 2, 0:unit["width"]],
                                     masked[:, u % 2, 0:unit["width"]], ACT.Exp,
                                     bias=neg_top[:, g % 2, u % 8:u % 8 + 1],
                                     accum_out=total[:, g % 2, u % 8:u % 8 + 1]).then_inc(
                                         s["exped"], 1)

            exponential(0)
            exponential(1)
            for u in range(n + 1):
                if u < n:
                    k = min(4, units[u]["width"] // P)
                    act.wait_ge(s["turned"], u + 1)
                    if u >= 2:
                        act.wait_ge(s["weighed"], u - 1)
                    nc.scalar.copy(prob_t[:, u % 2, 0:k, :], tp_a[:, 0:k, :]).then_inc(
                        s["read_a"], 1)
                if u + 2 < n:
                    exponential(u + 2)
                if u >= 8 and u % 8 == 0:
                    g = u // 8 - 1
                    act.wait_ge(s["sink_d"], g + 1)
                    nc.scalar.activation(sink_e[:, g % 2, :], sink_e[:, g % 2, :],
                                         ACT.Exp).then_inc(s["sink_x"], 1)


def project_out(nc, e, name, o, tiles, heads, gain, gain_scale, w_dram, gate, norm_gain, shift_scale,
                h_t=None, store=None, router=None):
    nt = len(tiles)
    vecs = sorted({0 if t >= TC else 1 for t in tiles}) if gate else []
    with Phase(nc, name) as ph:
        w = ph.sb("w", [P, 2, KD, NCHUNK])
        o_t = ph.sb("o_t", [P, 2, KD, P])
        gates = ph.sb("gates", [P, 2, D])
        g = ph.sb("g", [P, D])
        sq = ph.sb("sq", [P, D])
        n_sq = ph.sb("n_sq", [P, D])
        hh = heads or 1
        ss, std, rstd, tmp = (ph.sb(x, [P, nt, hh]) for x in ("ss", "std", "rstd", "tmp"))
        n_ss, n_std, n_rstd, n_tmp = (ph.sb(x, [P, nt]) for x in ("n_ss", "n_std", "n_rstd", "n_tmp"))
        runs = ph.sb("runs", [P, 32])
        part = ph.sb("part", [P, NCHUNK])
        n_g = ph.sb("n_g", [P, D])
        mul, add = ph.sb("mul", [P, 2, D]), ph.sb("add", [P, 2, D])
        h = ph.sb("h", [P, 2, D])
        eps = ph.sb("eps", [P, 1])
        if router:
            layer, logits = router
            h_tile = ph.sb("h_tile", [P, 2, KD, P])
            wr = ph.sb("wr", [P, KD, NG + NE])
            bias = ph.sb("bias", [P, NG + NE])
            lg = ph.ps("lg", [P, NG + NE])
        tp = [ph.ps(f"tp{i}", [P, 4, P]) for i in range(2)]
        n_tp = [ph.ps(f"n_tp{i}", [P, 4, P]) for i in range(2)]
        acc = [ph.ps(f"acc{i}", [P, NCHUNK]) for i in range(3)]
        names = ("vec_in g_in sq_done summed std_done eps_done o_done tp_done tp_read mm_done added n_vec_in "
                 "n_sq_done n_summed n_std_done h_done n_tp_done n_tp_read lg_done lg_read step")
        s = {x: ph.sem(x) for x in names.split()}
        loaded = [ph.sem(f"loaded{i}") for i in range(4)]
        stored = [ph.sem(f"stored{i}") for i in range(2)]
        block = ph.block()
        n_norm = 1 + 2 * len(vecs) + (4 if router else 0)
        side = lambda t: 0 if t >= TC else 1

        @block.sync
        def _(sp):
            if gain is not None:
                sp.dma_start(g[:, 0:gain.shape[0]], bcast_rows(gain)).then_inc(s["g_in"], 16)
            view = w_dram.rearrange("(k p) n -> p k n", p=P)
            for c in range(2):
                for half in range(2):
                    ks = slice(4 * half, 4 * half + 4)
                    sp.dma_start(w[:, c, ks, :], view[:, ks, c * NCHUNK:(c + 1) * NCHUNK]).then_inc(
                        loaded[2 * c + half], 16)
            for v in vecs:
                sp.dma_start(gates[:, v, :], bcast_rows(gate(v))).then_inc(s["vec_in"], 16)
            sp.dma_start(n_g[:], bcast_rows(norm_gain)).then_inc(s["n_vec_in"], 16)
            for v in vecs:
                shift, scale = shift_scale(v)
                sp.dma_start(add[:, v, :], bcast_rows(shift)).then_inc(s["n_vec_in"], 16)
                sp.dma_start(mul[:, v, :], bcast_rows(scale)).then_inc(s["n_vec_in"], 16)
            if router:
                for dst, src in [
                        (wr[:, :, 0:NG], e["moe_router_g"][layer].rearrange("(k p) n -> p k n", p=P)),
                        (wr[:, :, NG:], e["moe_router_e"][layer].rearrange("(k p) n -> p k n", p=P)),
                        (bias[:, 0:NG], bcast_rows(e["moe_router_g_b"][layer])),
                        (bias[:, NG:], bcast_rows(e["moe_router_e_b"][layer]))]:
                    sp.dma_start(dst, src).then_inc(s["n_vec_in"], 16)
            if store is not None:
                for i, t in enumerate(tiles):
                    sp.wait_ge(s["h_done"], i + 1)
                    sp.dma_start(store[t * P:(t + 1) * P, :], h[:, i % 2, :]).then_inc(
                        stored[i % 2], 16)
                for b in range(2):
                    sp.wait_ge(stored[b], 16 * (nt // 2))

        @block.scalar
        def _(act):
            def square_slices(i):
                if gain is None or i >= nt:
                    return
                if i >= 1:
                    act.wait_ge(s["summed"], i)
                nc.scalar.activation(sq[:], o[:, i, :], ACT.Square).then_inc(s["sq_done"], 1)

            def root_slices(i):
                if gain is None or i >= nt:
                    return
                act.wait_ge(s["eps_done"], 1)
                act.wait_ge(s["summed"], i + 1)
                nc.scalar.activation(std[:, i, :], ss[:, i, :], ACT.Sqrt, scale=heads / D,
                                     bias=eps[:]).then_inc(s["std_done"], 1)

            def copy_o(i):
                for half in range(2):
                    act.wait_ge(s["tp_done"], 2 * i + half + 1)
                    if i >= 2:
                        act.wait_ge(s["mm_done"], 2 * i - 2)
                    nc.scalar.copy(o_t[:, i % 2, 4 * half:4 * half + 4, :],
                                   tp[half][:]).then_inc(s["tp_read"], 1)

            def copy_h(i):
                for half in range(2):
                    act.wait_ge(s["n_tp_done"], 2 * i + half + 1)
                    if router:
                        if i >= 2:
                            act.wait_ge(s["lg_done"], i - 1)
                        dst = h_tile[:, i % 2, 4 * half:4 * half + 4, :]
                    else:
                        dst = h_t[:, 4 * half:4 * half + 4, i * P:(i + 1) * P]
                    nc.scalar.copy(dst, n_tp[half][:]).then_inc(s["n_tp_read"], 1)

            def square_and_root(i):
                act.wait_ge(s["added"], 2 * i + 2)
                if i >= 1:
                    act.wait_ge(s["n_summed"], i)
                nc.scalar.activation(n_sq[:], e["res"][:, tiles[i], :], ACT.Square).then_inc(
                    s["n_sq_done"], 1)
                act.wait_ge(s["eps_done"], 1)
                act.wait_ge(s["n_summed"], i + 1)
                nc.scalar.activation(n_std[:, i:i + 1], n_ss[:, i:i + 1], ACT.Sqrt, scale=1.0 / D,
                                     bias=eps[:]).then_inc(s["n_std_done"], 1)

            square_slices(0)
            root_slices(0)
            square_slices(1)
            copy_o(0)
            root_slices(1)
            square_slices(2)
            root_slices(2)
            for i in range(nt + 1):
                if i + 1 < nt:
                    copy_o(i + 1)
                if i >= 1:
                    copy_h(i - 1)
                if i < nt:
                    square_and_root(i)
                    square_slices(i + 3)
                    root_slices(i + 3)

        @block.vector
        def _(dve):
            link = Chain(dve, s["step"])
            v = nc.vector
            v.memset(eps[:], EPS).then_inc(s["eps_done"], 1)

            def scale_slices(i):
                if gain is None or i >= nt:
                    return
                width = D // heads
                dve.wait_ge(s["sq_done"], i + 1)
                v.tensor_reduce(ss[:, i, :], sq[:].rearrange("p (h d) -> p h d", h=heads), AX.X,
                                ALU.add).then_inc(s["summed"], 1)
                dve.wait_ge(s["summed"], i + 1)
                dve.wait_ge(s["std_done"], i + 1)
                rsqrt_mean(v, link, rstd[:, i, :], std[:, i, :], ss[:, i, :], tmp[:, i, :], heads / D)
                if gain_scale != 1.0:
                    link(v.tensor_scalar(rstd[:, i, :], rstd[:, i, :], gain_scale, None, ALU.mult))
                slices = o[:, i, :].rearrange("p (h d) -> p h d", h=heads)
                link(v.tensor_tensor(slices, slices, inner(rstd[:, i, :], width), ALU.mult))
                if gain.shape[0] == width:
                    op = v.tensor_tensor(slices, slices, middle(g[:, 0:width], heads), ALU.mult)
                else:
                    op = v.tensor_tensor(o[:, i, :], o[:, i, :], g[:], ALU.mult)
                op.then_inc(s["o_done"], 1)

            def add_products(i):
                for c in range(2):
                    j = 2 * i + c
                    cols = slice(c * NCHUNK, (c + 1) * NCHUNK)
                    dst = e["res"][:, tiles[i], cols]
                    dve.wait_ge(s["mm_done"], j + 1)
                    if not gate:
                        v.tensor_tensor(dst, dst, acc[j % 3][:], ALU.add).then_inc(s["added"], 1)
                        continue
                    link(v.tensor_tensor(part[:], acc[j % 3][:], gates[:, side(tiles[i]), cols],
                                         ALU.mult))
                    v.tensor_tensor(dst, dst, part[:], ALU.add).then_inc(s["added"], 1)
                    dve.wait_ge(s["added"], j + 1)

            def normalise_tile(i):
                t = tiles[i]
                dve.wait_ge(s["n_sq_done"], i + 1)
                link(v.tensor_reduce(runs[:], n_sq[:].rearrange("p (a b) -> p a b", b=32), AX.X,
                                     ALU.add))
                v.tensor_reduce(n_ss[:, i:i + 1], runs[:], AX.X, ALU.add).then_inc(s["n_summed"], 1)
                dve.wait_ge(s["n_summed"], i + 1)
                dve.wait_ge(s["n_std_done"], i + 1)
                one = slice(i, i + 1)
                rsqrt_mean(v, link, n_rstd[:, one], n_std[:, one], n_ss[:, one], n_tmp[:, one], 1.0 / D)
                if i >= 2:
                    dve.wait_ge(s["n_tp_done"], 2 * (i - 1))
                    if store is not None:
                        dve.wait_ge(stored[i % 2], 16 * (i // 2))
                out = h[:, i % 2, :]
                if not vecs:
                    v.scalar_tensor_tensor(out, e["res"][:, t, :], n_rstd[:, one], n_g[:], ALU.mult,
                                           ALU.mult).then_inc(s["h_done"], 1)
                    return
                link(v.scalar_tensor_tensor(out, e["res"][:, t, :], n_rstd[:, one],
                                            mul[:, side(t), :], ALU.mult, ALU.mult))
                v.tensor_tensor(out, out, add[:, side(t), :], ALU.add).then_inc(s["h_done"], 1)

            def read_logits(i):
                dve.wait_ge(s["lg_done"], i + 1)
                v.tensor_tensor(logits[:, i, :], lg[:], bias[:], ALU.add).then_inc(s["lg_read"], 1)

            if gain is not None:
                dve.wait_ge(s["g_in"], 16)
            for i in range(3):
                scale_slices(i)
            if vecs:
                dve.wait_ge(s["vec_in"], 16 * len(vecs))
            dve.wait_ge(s["n_vec_in"], 16 * n_norm)
            for x in vecs:
                link(v.scalar_tensor_tensor(mul[:, x, :], mul[:, x, :], 1.0, n_g[:], ALU.add,
                                            ALU.mult))
            for i in range(nt + 1):
                if i < nt:
                    add_products(i)
                    normalise_tile(i)
                if i >= 1 and router:
                    read_logits(i - 1)
                scale_slices(i + 3)

        @block.tensor
        def _(pe):
            def turn_o(i):
                if gain is not None:
                    pe.wait_ge(s["o_done"], i + 1)
                for half in range(2):
                    if i >= 1:
                        pe.wait_ge(s["tp_read"], 2 * i - 1 + half)
                    for q in range(4):
                        k = 4 * half + q
                        tr = nc.tensor.transpose(tp[half][:, q, :], o[:, i, k * P:(k + 1) * P],
                                                 e["ident"][:])
                    tr.then_inc(s["tp_done"], 1)

            def products(i):
                pe.wait_ge(s["tp_read"], 2 * i + 2)
                for c in range(2):
                    j = 2 * i + c
                    if j >= 3:
                        pe.wait_ge(s["added"], j - 2)
                    for k in range(KD):
                        if i == 0 and k % 4 == 0:
                            pe.wait_ge(loaded[2 * c + k // 4], 16)
                        mm = nc.tensor.matmul(acc[j % 3][:], o_t[:, i % 2, k, :], w[:, c, k, :],
                                              start=(k == 0), stop=(k == KD - 1))
                    mm.then_inc(s["mm_done"], 1)

            def turn_h(i):
                pe.wait_ge(s["h_done"], i + 1)
                for half in range(2):
                    if i >= 1:
                        pe.wait_ge(s["n_tp_read"], 2 * i - 1 + half)
                    for q in range(4):
                        k = 4 * half + q
                        tr = nc.tensor.transpose(n_tp[half][:, q, :], h[:, i % 2, k * P:(k + 1) * P],
                                                 e["ident"][:])
                    tr.then_inc(s["n_tp_done"], 1)

            def route_tile(i):
                if i == 0:
                    pe.wait_ge(s["n_vec_in"], 16 * n_norm)
                else:
                    pe.wait_ge(s["lg_read"], i)
                pe.wait_ge(s["n_tp_read"], 2 * i + 2)
                for k in range(KD):
                    mm = nc.tensor.matmul(lg[:], h_tile[:, i % 2, k, :], wr[:, k, :],
                                          start=(k == 0), stop=(k == KD - 1))
                mm.then_inc(s["lg_done"], 1)

            turn_o(0)
            for i in range(nt + 1):
                if i < nt:
                    products(i)
                if i + 1 < nt:
                    turn_o(i + 1)
                if i >= 1:
                    turn_h(i - 1)
                    if router:
                        route_tile(i - 1)


def max_blocks(nt):
    n = NE + 2 * nt
    return n + n % 2


def route(nc, e, layer, tiles, r):
    nt = len(tiles)
    nb = max_blocks(nt)
    with Phase(nc, f"route{layer}") as ph:
        before = ph.sb("before", [P, P])
        iota = ph.sb("iota", [P, P])
        rowid = ph.sb("rowid", [P, 3, NT])
        logits = r["logits"]
        gate_t = ph.sb("gate_t", [P, nt, NG])
        tg = ph.sb("tg", [P, nt, NG])
        hot_g = ph.sb("hot_g", [P, nt, NG])
        le = ph.sb("le", [P, nt, NE])
        te = ph.sb("te", [P, nt, NE])
        hot = ph.sb("hot", [P, 2, nt, NE])
        both = ph.sb("both", [P, nt + 1, NE])
        sums = ph.sb("sums", [P, nt + 1, NE])
        small = ph.sb("small", [P, 12, nt])
        place = ph.sb("place", [P, nt, NE])
        cnt = ph.sb("cnt", [P, NE])
        blocks = ph.sb("blocks", [P, NE])
        end = [ph.sb(f"end{i}", [P, NE]) for i in range(2)]
        dest = ph.sb("dest", [P, 2, nt])
        dest_i = ph.sb("dest_i", [P, 2, 2, nt], I32)
        dest_f = ph.sb("dest_f", [P, 2, 2, nt])
        lane = ph.sb("lane", [P, 2, nt, P])
        in_block = ph.sb("in_block", [P, 2, nt, nb])
        what = ph.sb("what", [P, 2, 2, nt, nb])
        past = ph.sb("past", [1, nb, NE])
        expert_f = ph.sb("expert_f", [1, nb])
        where, slots = ph.ps("where", [P, nt + 1, NE]), ph.ps("slots", [P, 2, nb])
        names = "const_in gexp_in gexp_done wexp_in wexp_done hot_done where_done tables_in slots_done step fill"
        s = {x: ph.sem(x) for x in names.split()}
        block = ph.block()

        @block.sync
        def _(sp):
            loads = [
                (before[:], e["c_before"]), (iota[:], e["c_iota"]), (rowid[:], e["c_rowid"]),
            ]
            for dst, src in loads:
                sp.dma_start(dst, src).then_inc(s["const_in"], 16)

        @block.tensor
        def _(pe):
            pe.wait_ge(s["const_in"], 16 * 3)
            pe.wait_ge(s["hot_done"], nt + 3)
            nc.tensor.matmul(where[:], before[:], both[:], start=True, stop=False)
            nc.tensor.matmul(where[:], e["ones"][:], sums[:], start=False, stop=True).then_inc(
                s["where_done"], 1)
            pe.wait_ge(s["tables_in"], 1)
            for j in range(2 * nt):
                a, i = j // nt, j % nt
                mm = nc.tensor.matmul(slots[:], lane[:, a, i, :], what[:, :, a, i, :],
                                      start=(j == 0), stop=(j == 2 * nt - 1))
            mm.then_inc(s["slots_done"], 1)

        @block.scalar
        def _(act):
            act.wait_ge(s["gexp_in"], 1)
            nc.scalar.activation(tg[:], tg[:], ACT.Exp).then_inc(s["gexp_done"], 1)
            act.wait_ge(s["wexp_in"], 1)
            nc.scalar.activation(small[:, 5, :], small[:, 5, :], ACT.Exp).then_inc(s["wexp_done"], 1)

        @block.vector
        def _(dve):
            v = nc.vector
            link = Chain(dve, s["step"])
            dve.wait_ge(s["const_in"], 16 * 3)
            row = lambda j: small[:, j, :]

            def first_max(hot_out, values, scratch, n, best):
                link(v.tensor_reduce(best, values, AX.X, ALU.max))
                link(v.tensor_tensor(scratch, values, inner(best, n), ALU.is_equal))
                link(v.scalar_tensor_tensor(scratch, middle(iota[:, 0:n], nt), float(n), scratch,
                                            ALU.subtract, ALU.mult))
                link(v.tensor_reduce(row(9), scratch, AX.X, ALU.min))
                link(v.tensor_scalar(row(9), row(9), float(n), None, ALU.add))
                link(v.tensor_tensor(hot_out, middle(iota[:, 0:n], nt), inner(row(9), n),
                                     ALU.is_equal))

            lg, lge = logits[:, :, 0:NG], logits[:, :, NG:]
            first_max(hot_g[:], lg, gate_t[:], NG, row(0))
            v.tensor_tensor(tg[:], lg, inner(row(0), NG), ALU.subtract).then_inc(s["gexp_in"], 1)
            dve.wait_ge(s["gexp_done"], 1)
            link(v.tensor_reduce(row(1), tg[:], AX.X, ALU.add))
            link(v.reciprocal(row(1), row(1)))
            for g in range(NG):
                sl = slice(g * EPG, (g + 1) * EPG)
                oh = hot_g[:, :, g]
                link(v.tensor_tensor(le[:, :, sl], lge[:, :, sl], inner(oh, EPG), ALU.mult))
                link(v.tensor_scalar(row(2), oh, -1.0, -NEG, ALU.add, ALU.mult))
                link(v.tensor_tensor(le[:, :, sl], le[:, :, sl], inner(row(2), EPG), ALU.add))
            first_max(hot[:, 0, :, :], le[:], te[:], NE, row(3))
            link(v.scalar_tensor_tensor(le[:], hot[:, 0, :, :], 2 * NEG, le[:], ALU.mult, ALU.add))
            first_max(hot[:, 1, :, :], le[:], te[:], NE, row(4))
            v.tensor_tensor(row(5), row(4), row(3), ALU.subtract).then_inc(s["wexp_in"], 1)
            v.tensor_tensor(both[:, 0:nt, :], hot[:, 0, :, :], hot[:, 1, :, :], ALU.add).then_inc(
                s["hot_done"], 1)
            v.memset(both[:, nt, :], 0.0).then_inc(s["hot_done"], 1)
            v.memset(sums[:, 0, :], 0.0).then_inc(s["hot_done"], 1)
            for i in range(nt):
                dve.wait_ge(s["hot_done"], 3 + i)
                v.tensor_tensor(sums[:, i + 1, :], sums[:, i, :], both[:, i, :], ALU.add).then_inc(
                    s["hot_done"], 1)
            dve.wait_ge(s["wexp_done"], 1)
            link(v.tensor_scalar(row(6), row(5), 1.0, None, ALU.add))
            link(v.reciprocal(row(6), row(6)))
            link(v.tensor_tensor(r["weight"][:, 0, 0:nt], row(6), row(1), ALU.mult))
            link(v.tensor_tensor(r["weight"][:, 1, 0:nt], r["weight"][:, 0, 0:nt], row(5), ALU.mult))
            dve.wait_ge(s["where_done"], 1)
            link(v.tensor_copy(cnt[:], where[:, nt, :]))
            link(v.tensor_scalar(blocks[:], cnt[:], 0.0, None, ALU.is_gt))
            for k in range(1, nt):
                link(v.scalar_tensor_tensor(blocks[:], cnt[:], float(k * P), blocks[:], ALU.is_gt,
                                            ALU.add))
            link(v.tensor_copy(end[0][:], blocks[:]))
            a = 0
            for k in (1, 2, 4, 8, 16):
                link(v.tensor_copy(end[1 - a][:, 0:k], end[a][:, 0:k]))
                link(v.tensor_tensor(end[1 - a][:, k:], end[a][:, k:], end[a][:, 0:NE - k], ALU.add))
                a = 1 - a
            last = end[a]
            link(v.tensor_tensor(cnt[:], last[:], blocks[:], ALU.subtract))
            link(v.tensor_scalar(cnt[:], cnt[:], float(P), None, ALU.mult))
            link(v.tensor_tensor(place[:], where[:, 0:nt, :], middle(cnt[:], nt), ALU.add))
            for a in range(2):
                link(v.tensor_tensor(te[:], place[:], hot[:, a, :, :], ALU.mult))
                link(v.tensor_reduce(dest[:, a, :], te[:], AX.X, ALU.add))
            link(v.tensor_copy(dest_i[:, 0, :, :], dest[:]))
            link(v.tensor_copy(dest_i[:, 1, :, :], dest[:]))
            link(v.tensor_single_scalar(dest_i[:, 0, :, :], dest_i[:, 0, :, :], P - 1,
                                        ALU.bitwise_and))
            link(v.tensor_single_scalar(dest_i[:, 1, :, :], dest_i[:, 1, :, :], 7,
                                        ALU.arith_shift_right))
            link(v.tensor_copy(dest_f[:], dest_i[:]))
            v.tensor_tensor(lane[:], iota[:].unsqueeze(1).unsqueeze(1).broadcast_to([P, 2, nt, P]),
                            over(dest_f[:, 0], P), ALU.is_equal).then_inc(s["fill"], 1)
            link(v.tensor_tensor(in_block[:],
                                 iota[:, 0:nb].unsqueeze(1).unsqueeze(1).broadcast_to([P, 2, nt, nb]),
                                 over(dest_f[:, 1], nb), ALU.is_equal))
            for z in range(2):
                ids = rowid[:, z:z + 2, tiles[0]:tiles[0] + nt]
                v.tensor_tensor(what[:, z], in_block[:], over(ids, nb), ALU.mult).then_inc(
                    s["fill"], 1)
            dve.wait_ge(s["fill"], 3)
            dve.sem_inc(s["tables_in"], 1)
            link(v.tensor_tensor(past[:], middle(last[0:1, :], nb), inner(iota[0:1, 0:nb], NE),
                                 ALU.is_le))
            link(v.tensor_reduce(expert_f[:], past[:], AX.X, ALU.add))
            link(v.tensor_scalar(expert_f[:], expert_f[:], float(NE - 1), None, ALU.min))
            link(v.tensor_copy(r["expert"][:, 0:nb], expert_f[:]))
            link(v.tensor_copy(r["count"][:], last[0:1, NE - 1:NE]))
            dve.wait_ge(s["slots_done"], 1)
            link(v.tensor_scalar(r["index"][:, :, 0:nb], slots[:], BIG, None, ALU.add))
            link(v.memset(r["index"][:, :, nb:], int(BIG)))


def experts(nc, e, layer, nt, r):
    nb = max_blocks(nt)
    with Phase(nc, f"moe{layer}") as ph:
        wg = [ph.sb(f"wg{b}", [P, KD, FE]) for b in range(2)]
        wu = [ph.sb(f"wu{b}", [P, KD, FE]) for b in range(2)]
        wd = [ph.sb(f"wd{b}", [P, FE // P, D]) for b in range(2)]
        xg = [ph.sb(f"xg{b}", [P, D]) for b in range(2)]
        xg_t = [ph.sb(f"xg_t{b}", [P, KD, P]) for b in range(2)]
        x_idx = [ph.sb(f"x_idx{b}", [P, 1], I32) for b in range(2)]
        y_idx = [ph.sb(f"y_idx{b}", [P, 1], I32) for b in range(2)]
        sig = ph.sb("sig", [P, FE])
        hid = ph.sb("hid", [P, FE])
        hid_t = ph.sb("hid_t", [P, FE // P, P])
        y = [ph.sb(f"y{b}", [P, D]) for b in range(2)]
        tp = [ph.ps(f"tp{i}", [P, 4, P]) for i in range(2)]
        HF = FE // 2
        gate = [ph.ps(f"gate{f}", [P, HF]) for f in range(2)]
        up = [ph.ps(f"up{f}", [P, HF]) for f in range(2)]
        down = [ph.ps(f"down{i}", [P, NCHUNK]) for i in range(2)]
        names = ("y_free cleared idx_done turned_x read_x gated upped expd hid_done issue indexed landed fetched "
                 "turned_h read_h downed y_done step")
        s = {x: ph.sem(x) for x in names.split()}
        gu_in = [ph.sem(f"gu_in{b}") for b in range(2)]
        d_in = [ph.sem(f"d_in{b}") for b in range(2)]
        x_in = [nc.alloc_semaphore(f"moe{layer}_x_in{b}") for b in range(2)]
        y_out = [nc.alloc_semaphore(f"moe{layer}_y_out{b}") for b in range(2)]
        block = ph.block()
        view_g = e["moe_w_gate"][layer].rearrange("x (p k) n -> x p k n", k=KD)
        view_u = e["moe_w_up"][layer].rearrange("x (p k) n -> x p k n", k=KD)
        view_d = e["moe_w_down"][layer].rearrange("x (k p) n -> x p k n", p=P)

        def count_of(eng):
            return eng.value_load(r["count"][0:1, 0:1], min_val=0, max_val=nb)

        @block.sync
        def _(sp):
            n = count_of(sp)
            with sp.Fori(0, nb // 2) as i2:
                for b in range(2):
                    i = 2 * i2 + b
                    with sp.If(i < n):
                        x = sp.value_load(r["expert"][0:1, bass.ds(i, 1)], min_val=0, max_val=NE - 1)
                        sp.wait_ge(s["upped"], 2 * i + 2)
                        sp.sem_inc(s["issue"], 1)
                        sp.wait_ge(s["fetched"], 1)
                        sp.dma_start(wg[b][:], view_g[bass.ds(x, 1)].rearrange(
                            "o p k n -> (o p) k n")).then_inc(gu_in[b], 16)
                        sp.dma_start(wu[b][:], view_u[bass.ds(x, 1)].rearrange(
                            "o p k n -> (o p) k n")).then_inc(gu_in[b], 16)
                        sp.wait_ge(s["downed"], i + 1)
                        sp.sem_inc(s["issue"], 1)
                        sp.dma_start(wd[b][:], view_d[bass.ds(x, 1)].rearrange(
                            "o p k n -> (o p) k n")).then_inc(d_in[b], 16)

        @block.gpsimd
        def _(pool):
            n = count_of(pool)
            last_token = pool.to_reg(NT * P - 1)
            last_result = pool.to_reg(2 * NT * P - 1)

            def fetch(b, i):
                nc.gpsimd.tensor_copy(x_idx[b][:], r["index"][:, 0, bass.ds(i, 1)]).then_inc(
                    s["idx_done"], 1)

            def gather(b):
                nc.gpsimd.indirect_dma_start(
                    xg[b][:], None, e["h_dram"],
                    bass.IndirectOffsetOnAxis(ap=x_idx[b][:], axis=0),
                    bounds_check=last_token, oob_is_err=False).then_inc(x_in[b], 16)

            for b in range(2):
                nc.gpsimd.memset(xg[b][:], 0.0).then_inc(s["cleared"], 1)
                pool.wait_ge(s["cleared"], b + 1)
                fetch(b, b)
                pool.wait_ge(s["idx_done"], b + 1)
                pool.sem_inc(s["indexed"], 1)
                gather(b)
                pool.sem_inc(s["fetched"], 1)
            with pool.Fori(0, nb // 2) as i2:
                for b in range(2):
                    i = 2 * i2 + b
                    with pool.If(i < n):
                        pool.wait_ge(s["turned_x"], 2 * i + 2)
                        fetch(b, i + 2)
                        pool.wait_ge(s["idx_done"], 2 * i + 3)
                        pool.sem_inc(s["indexed"], 1)
                        gather(b)
                        nc.gpsimd.tensor_copy(y_idx[b][:], r["index"][:, 1, bass.ds(i, 1)]).then_inc(
                            s["idx_done"], 1)
                        pool.wait_ge(s["idx_done"], 2 * i + 4)
                        pool.wait_ge(s["y_done"], 2 * i + 3)
                        pool.sem_inc(s["indexed"], 1)
                        nc.gpsimd.indirect_dma_start(
                            e["y_dram"], bass.IndirectOffsetOnAxis(ap=y_idx[b][:], axis=0),
                            y[b][:], None, bounds_check=last_result,
                            oob_is_err=False).then_inc(y_out[b], 16)
                        if b == 0:
                            with pool.If(i2 > 0):
                                pool.wait_ge(y_out[1], 16 * i2)
                                pool.sem_inc(s["landed"], 1)
                        else:
                            pool.wait_ge(y_out[0], 16 * (i2 + 1))
                        pool.sem_inc(s["y_free"], 1)
            pool.wait_ge(y_out[0], 16 * ((n + 1) // 2))
            pool.sem_inc(s["landed"], 1)
            with pool.If(n > 1):
                pool.wait_ge(y_out[1], 16 * (n // 2))
                pool.sem_inc(s["landed"], 1)
            pool.wait_ge(x_in[0], 16 * ((n + 1) // 2) + 16)
            pool.wait_ge(x_in[1], 16 * (n // 2) + 16)
            pool.sem_inc(s["landed"], 1)

        @block.tensor
        def _(pe):
            n = count_of(pe)
            pe.sem_inc(s["downed"], 2)
            pe.sem_inc(s["upped"], 4)

            def turn_x(b, half):
                for q in range(4):
                    tr = nc.tensor.transpose(tp[half][:, q, :], xg[b][:, 4 * half + q:D:KD],
                                             e["ident"][:])
                tr.then_inc(s["turned_x"], 1)

            pe.wait_ge(x_in[0], 16)
            turn_x(0, 0)
            turn_x(0, 1)
            with pe.Fori(0, nb // 2) as i2:
                for b in range(2):
                    i = 2 * i2 + b
                    with pe.If(i < n):
                        pe.wait_ge(gu_in[b], 32 * (i2 + 1))
                        pe.wait_ge(s["read_x"], 2 * i + 2)
                        pe.wait_ge(s["hid_done"], 2 * i + 1)

                        def up_or_gate(acc, w, f, done):
                            for k in range(KD):
                                mm = nc.tensor.matmul(acc[f][:], xg_t[b][:, k, :],
                                                      w[b][:, k, f * HF:(f + 1) * HF],
                                                      start=(k == 0), stop=(k == KD - 1))
                            mm.then_inc(done, 1)

                        def turn_hidden(f):
                            pe.wait_ge(s["hid_done"], 2 * i + f + 2)
                            for k in (2 * f, 2 * f + 1):
                                tr = nc.tensor.transpose(tp[f][:, k % 2, :],
                                                         hid[:, k * P:(k + 1) * P], e["ident"][:])
                            tr.then_inc(s["turned_h"], 1)

                        def down_half(f):
                            for c in range(2):
                                for k in (2 * f, 2 * f + 1):
                                    mm = nc.tensor.matmul(
                                        down[c][:], hid_t[:, k, :],
                                        wd[b][:, k, c * NCHUNK:(c + 1) * NCHUNK],
                                        start=(k == 0), stop=(k == 3), skip_group_check=True)
                            return mm

                        up_or_gate(gate, wg, 0, s["gated"])
                        up_or_gate(up, wu, 0, s["upped"])
                        up_or_gate(gate, wg, 1, s["gated"])
                        turn_hidden(0)
                        up_or_gate(up, wu, 1, s["upped"])
                        pe.wait_ge(d_in[b], 16 * (i2 + 1))
                        pe.wait_ge(s["y_done"], 2 * i + 1)
                        pe.wait_ge(s["read_h"], 2 * i + 1)
                        down_half(0)
                        turn_hidden(1)
                        pe.wait_ge(x_in[1 - b], 16 * (i2 + 1 + b))
                        turn_x(1 - b, 0)
                        pe.wait_ge(s["read_h"], 2 * i + 2)
                        turn_x(1 - b, 1)
                        down_half(1).then_inc(s["downed"], 1)

        @block.scalar
        def _(act):
            n = count_of(act)

            def read_x(b, i):
                for half in range(2):
                    act.wait_ge(s["turned_x"], 2 * i + 1 + half)
                    nc.scalar.copy(xg_t[b][:, 4 * half:4 * half + 4, :], tp[half][:]).then_inc(
                        s["read_x"], 1)

            read_x(0, 0)
            with act.Fori(0, nb // 2) as i2:
                for b in range(2):
                    i = 2 * i2 + b
                    with act.If(i < n):
                        act.wait_ge(s["hid_done"], 2 * i + 1)
                        for f in range(2):
                            act.wait_ge(s["gated"], 2 * i + f + 1)
                            nc.scalar.activation(sig[:, f * HF:(f + 1) * HF], gate[f][:], ACT.Exp,
                                                 scale=-1.0).then_inc(s["expd"], 1)
                            act.wait_ge(s["turned_h"], 2 * i + f + 1)
                            nc.scalar.copy(hid_t[:, 2 * f:2 * f + 2, :],
                                           tp[f][:, 0:2, :]).then_inc(s["read_h"], 1)
                        read_x(1 - b, i + 1)

        @block.vector
        def _(dve):
            n = count_of(dve)
            dve.sem_inc(s["y_free"], 1)
            dve.sem_inc(s["hid_done"], 1)
            dve.sem_inc(s["y_done"], 1)
            with dve.Fori(0, nb // 2) as i2:
                for b in range(2):
                    i = 2 * i2 + b
                    with dve.If(i < n):
                        for f in range(2):
                            half = sig[:, f * HF:(f + 1) * HF]
                            at = 6 * i + 3 * f
                            dve.wait_ge(s["expd"], 2 * i + f + 1)
                            nc.vector.tensor_scalar(half, half, 1.0, None, ALU.add).then_inc(
                                s["step"], 1)
                            dve.wait_ge(s["step"], at + 1)
                            nc.vector.reciprocal(half, half).then_inc(s["step"], 1)
                            dve.wait_ge(s["step"], at + 2)
                            nc.vector.tensor_tensor(half, half, gate[f][:], ALU.mult).then_inc(
                                s["step"], 1)
                            dve.wait_ge(s["step"], at + 3)
                            dve.wait_ge(s["upped"], 2 * i + f + 5)
                            nc.vector.tensor_tensor(hid[:, f * HF:(f + 1) * HF], half, up[f][:],
                                                    ALU.mult).then_inc(s["hid_done"], 1)
                        dve.wait_ge(s["downed"], i + 3)
                        dve.wait_ge(s["y_free"], i + 1)
                        for c in range(2):
                            nc.vector.tensor_copy(y[b][:, c * NCHUNK:(c + 1) * NCHUNK],
                                                  down[c][:]).then_inc(s["y_done"], 1)


def combine_experts(nc, e, layer, tiles, r, gate):
    nt = len(tiles)
    vecs = sorted({0 if t >= TC else 1 for t in tiles})
    with Phase(nc, f"comb{layer}") as ph:
        ys = ph.sb("ys", [P, 4, 2, D])
        gates = ph.sb("gates", [P, 2, D])
        vec_in, step, used = ph.sem("vec_in"), ph.sem("step"), ph.sem("used")
        y_in = [ph.sem(f"y_in{i}") for i in range(4)]
        block = ph.block()

        @block.sync
        def _(sp):
            for v in vecs:
                sp.dma_start(gates[:, v, :], bcast_rows(gate(v))).then_inc(vec_in, 16)
            src = e["y_dram"].rearrange("(a t p) d -> t p a d", a=2, p=P)
            for i, t in enumerate(tiles):
                if i >= 4:
                    sp.wait_ge(used, i - 3)
                sp.dma_start(ys[:, i % 4, :, :], src[t]).then_inc(y_in[i % 4], 16)

        @block.vector
        def _(dve):
            link = Chain(dve, step)
            dve.wait_ge(vec_in, 16 * len(vecs))
            for i, t in enumerate(tiles):
                v = 0 if t >= TC else 1
                a, b = ys[:, i % 4, 0, :], ys[:, i % 4, 1, :]
                dve.wait_ge(y_in[i % 4], 16 * (i // 4 + 1))
                link(nc.vector.tensor_scalar(a, a, r["weight"][:, 0, i:i + 1], None, ALU.mult))
                link(nc.vector.scalar_tensor_tensor(a, b, r["weight"][:, 1, i:i + 1], a, ALU.mult,
                                                    ALU.add))
                link(nc.vector.tensor_tensor(a, a, gates[:, v, :], ALU.mult))
                nc.vector.tensor_tensor(e["res"][:, t, :], e["res"][:, t, :], a, ALU.add).then_inc(used, 1)


def mod_part(e, layer, part):
    return lambda v: e["mod_dram"][v, (layer * 6 + part) * D:(layer * 6 + part + 1) * D]


def norm_vectors(e, layer, part):
    return lambda v: (mod_part(e, layer, part)(v), mod_part(e, layer, part + 1)(v))


def routing_tables(nc, stack, layer, nt):
    nb = max_blocks(nt)
    new = lambda name, shape, dt: stack.enter_context(nc.sbuf_tensor(f"r_{name}{layer}", shape, dt))
    return dict(index=new("index", [P, 2, nb + 2], I32), expert=new("expert", [1, nb], I32),
                count=new("count", [1, 1], I32), weight=new("weight", [P, 2, NT], F32),
                logits=new("logits", [P, nt, NG + NE], F32))


def moe_layer(nc, e, layer, tiles, r):
    route(nc, e, layer, tiles, r)
    experts(nc, e, layer, len(tiles), r)
    combine_experts(nc, e, layer, tiles, r, mod_part(e, layer, 5))


def layer_0(nc, e, stack):
    tiles = list(range(NT))
    sb = nc.sbuf_tensor
    r = routing_tables(nc, stack, 0, NT)
    with sb("a_buffer", [P, NT * D], F32) as buffer:
        h_t = buffer[:].rearrange("p (k n) -> p k n", k=KD)
        o = buffer[:].rearrange("p (t d) -> p t d", t=NT)
        normalise(nc, e, "norm1_0", tiles, e["norm1_g"][0], norm_vectors(e, 0, 0), h_t)
        with sb("a_q", [P, 8, NT * P], F32) as q_t, sb("a_k", [P, 2, 8, NT * P], F32) as k_t, \
                sb("a_v", [P, NT, D], F32) as v:

            def stores(c, t):
                if c >= 4:
                    return v[:, t, (c - 4) * NCHUNK:(c - 3) * NCHUNK]
                slots, cols = slice(4 * (c % 2), 4 * (c % 2) + 4), slice(t * P, (t + 1) * P)
                if c < 2:
                    return [(slice(0, P), q_t[:, slots, cols])], 0.125
                return [(rows, k_t[rows, side, slots, cols]) for side, rows in enumerate(HALVES)], 1.0

            items = [(c, t, "value" if c >= 4 else "rope" if t >= TC else "plain")
                     for c in range(6) for t in tiles]
            project_heads(nc, e, "qkv0", h_t, e["a_w_qkv"][0], items, stores, k_t)
            diff_attention(nc, e, q_t, k_t, v, o)
        project_out(nc, e, "out0", o, tiles, 8, e["a_subln_g"][0], 1.0 - LAM_INIT, e["a_w_o"][0],
                    mod_part(e, 0, 2), e["norm2_g"][0], norm_vectors(e, 0, 3), store=e["h_dram"],
                    router=(0, r["logits"]))
    moe_layer(nc, e, 0, tiles, r)


def layer_1(nc, e, stack):
    stream = list(range(TC, NT))
    sb = nc.sbuf_tensor
    r = routing_tables(nc, stack, 1, TX)
    with sb("b_buffer", [P, NT * D], F32) as buffer:
        h_t = buffer[:].rearrange("p (k n) -> p k n", k=KD)
        o = buffer[:, 0:TX * D].rearrange("p (t d) -> p t d", t=TX)
        normalise(nc, e, "norm1_1", list(range(NT)), e["norm1_g"][1], norm_vectors(e, 1, 0), h_t)
        with sb("b_q", [P, 8, NT * P], F32) as q_t, sb("b_k", [P, 2, 4, NT * P], F32) as k_t, \
                sb("b_v", [P, NT, 4 * HD], F32) as v:

            def stores(c, t):
                cols = slice(t * P, (t + 1) * P)
                if c == 2:
                    return [(rows, k_t[rows, side, :, cols]) for side, rows in enumerate(HALVES)], 1.0
                return [(slice(0, P), q_t[:, 4 * c:4 * c + 4, cols])], 0.125

            items = [(c, t, "rope") for c in range(2) for t in stream]
            items += [(2, t, "shared") for t in range(NT)]
            project_heads(nc, e, "qkv1", h_t, e["b_w_qkv"][0], items, stores, k_t,
                          lambda t: v[:, t, :])

            units = []
            for b in range(TX):
                lo, hi = max(0, b - 1), min(TX, b + 2)
                tiles = [*range(TC), *range(TC + lo, TC + hi)]
                for head in range(NH):
                    kv = head // 4
                    keys = []
                    for j0 in range(0, len(tiles), 4):
                        j = j0
                        while j < min(j0 + 4, len(tiles)):
                            k = j
                            while k + 1 < min(j0 + 4, len(tiles)) and tiles[k + 1] == tiles[k] + 1:
                                k += 1
                            keys.append((j * P, k_t[:, head % 2, kv, tiles[j] * P:(tiles[k] + 1) * P],
                                         (k - j + 1) * P))
                            j = k + 1
                    units.append(dict(
                        q=q_t[:, head // 2, (TC + b) * P:(TC + b + 1) * P], keys=keys,
                        width=len(tiles) * P, mask=b, mask0=0, head=head,
                        values=[v[:, j, kv * HD:(kv + 1) * HD] for j in tiles]))
            masked_attention(
                nc, e, "swa", units, [TX, 640], e["c_band"].rearrange("b p n -> p b n"),
                [(0, e["b_sink"][0])],
                lambda g: o[:, g // 2, (g % 2) * NCHUNK:(g % 2 + 1) * NCHUNK].rearrange(
                    "p (h d) -> p h d", d=HD))
        project_out(nc, e, "out1", o, stream, None, None, 1.0, e["b_w_o"][0], mod_part(e, 1, 2),
                    e["norm2_g"][1], norm_vectors(e, 1, 3), store=e["h_dram"],
                    router=(1, r["logits"]))
    moe_layer(nc, e, 1, stream, r)


def project_in(nc, e, h_t, hh):
    chunks = [(n0, min(NCHUNK, QKV2 - n0)) for n0 in range(0, QKV2, NCHUNK)]
    with Phase(nc, "in2") as ph:
        w = ph.sb("w", [P, 3, KD, NCHUNK])
        acc = [ph.ps(f"acc{i}", [P, NCHUNK]) for i in range(4)]
        loaded = [ph.sem(f"loaded{i}") for i in range(3)]
        mm_done, read = ph.sem("mm_done"), ph.sem("read")
        block = ph.block()

        @block.sync
        def _(sp):
            stream_weights(sp, w, e["w_in_2"][0].rearrange("(k p) n -> p k n", p=P), chunks, loaded,
                           mm_done, TX)

        @block.tensor
        def _(pe):
            for j in range(len(chunks) * TX):
                c, t = j // TX, j % TX
                width = chunks[c][1]
                if t == 0:
                    pe.wait_ge(loaded[c % 3], 16 * (c // 3 + 1))
                if j >= 4:
                    pe.wait_ge(read, j - 3)
                for k in range(KD):
                    mm = nc.tensor.matmul(acc[j % 4][:, 0:width], h_t[:, k, t * P:(t + 1) * P],
                                          w[:, c % 3, k, 0:width], start=(k == 0),
                                          stop=(k == KD - 1))
                mm.then_inc(mm_done, 1)

        @block.scalar
        def _(act):
            for j in range(len(chunks) * TX):
                n0, width = chunks[j // TX]
                act.wait_ge(mm_done, j + 1)
                nc.scalar.copy(hh[:, j % TX, n0:n0 + width], acc[j % 4][:, 0:width]).then_inc(read, 1)


RUNS2 = [(0, 8), (1184, 8), (1952, 6)]
GAINS2 = [("moba_q_g_2", 0, 4), ("moba_k_g_2", 256, 4), ("dil_q_g_2", 1184, 4),
          ("dil_k_g_2", 1440, 4), ("swa_q_g_2", 1952, 4), ("swa_k_g_2", 2208, 2)]
LATENTS = [("mla_qlat_g_2", 768, 256), ("mla_kvlat_g_2", 1024, 128)]
ROPE_COLS = (1152, 32)
VALUES2 = (512, 1696, 2336)
QK = 96


def heads_of(ap, width):
    return ap.rearrange("p t (h d) -> p t h d", d=width)


def over(ap, n):
    return ap.unsqueeze(3).broadcast_to([*ap.shape, n])


def gain_over(ap, t, h):
    return ap.unsqueeze(1).unsqueeze(1).broadcast_to([ap.shape[0], t, h, ap.shape[1]])


def prepare_heads(nc, e, hh, mq, mk, mv):
    with Phase(nc, "prep2") as ph:
        sq = ph.sb("sq", [P, TX, QKV2])
        ss, std, rstd, tmp = (ph.sb(x, [P, TX, 22]) for x in ("ss", "std", "rstd", "tmp"))
        sl, stl, rsl, tml = (ph.sb(x, [P, 2, TX]) for x in ("sl", "stl", "rsl", "tml"))
        gains = ph.sb("gains", [P, 6, HD])
        lat_g = ph.sb("lat_g", [P, 384])
        eps = ph.sb("eps", [P, 1])
        w_uq = ph.sb("w_uq", [P, 2, 4 * QK])
        w_ukv = ph.sb("w_ukv", [P, 4 * P])
        lat_t = ph.sb("lat_t", [P, TX, 3, P])
        tp = [ph.ps(f"tp{i}", [P, 3, P]) for i in range(2)]
        pq = [ph.ps(f"pq{i}", [P, 4 * QK]) for i in range(2)]
        pkv = [ph.ps(f"pkv{i}", [P, 4 * P]) for i in range(2)]
        names = "const_in w_in sq_done eps_done summed std_done lat_done tp_done tp_read q_done kv_done q_read kv_read step"
        s = {x: ph.sem(x) for x in names.split()}
        block = ph.block()

        @block.sync
        def _(sp):
            for j, (name, _, _) in enumerate(GAINS2):
                sp.dma_start(gains[:, j, :], bcast_rows(e["small"][name])).then_inc(s["const_in"], 16)
            for name, c0, width in LATENTS:
                sp.dma_start(lat_g[:, c0 - 768:c0 - 768 + width],
                             bcast_rows(e["small"][name])).then_inc(s["const_in"], 16)
            sp.dma_start(w_uq[:], e["mla_w_uq_2"][0].rearrange("(k p) n -> p k n", p=P)).then_inc(
                s["w_in"], 16)
            sp.dma_start(w_ukv[:], e["mla_w_ukv_2"][0]).then_inc(s["w_in"], 16)

        @block.scalar
        def _(act):
            for t in range(TX):
                nc.scalar.activation(sq[:, t, :], hh[:, t, :], ACT.Square).then_inc(s["sq_done"], 1)
            act.wait_ge(s["eps_done"], 1)
            act.wait_ge(s["summed"], 5)
            nc.scalar.activation(std[:], ss[:], ACT.Sqrt, scale=1.0 / HD, bias=eps[:]).then_inc(
                s["std_done"], 1)
            for j, (_, _, width) in enumerate(LATENTS):
                nc.scalar.activation(stl[:, j, :], sl[:, j, :], ACT.Sqrt, scale=1.0 / width,
                                     bias=eps[:]).then_inc(s["std_done"], 1)
            for t in range(TX):
                act.wait_ge(s["tp_done"], t + 1)
                nc.scalar.copy(lat_t[:, t, :, :], tp[t % 2][:]).then_inc(s["tp_read"], 1)
            for t in range(TX):
                act.wait_ge(s["q_done"], t + 1)
                nc.scalar.copy(mq[:, t, :, :].rearrange("p h d -> p (h d)"), pq[t % 2][:]).then_inc(
                    s["q_read"], 1)

        @block.vector
        def _(dve):
            v = nc.vector
            link = Chain(dve, s["step"])
            v.memset(eps[:], EPS).then_inc(s["eps_done"], 1)
            dve.wait_ge(s["sq_done"], TX)
            h0 = 0
            for c0, n in RUNS2:
                v.tensor_reduce(ss[:, :, h0:h0 + n], heads_of(sq[:, :, c0:c0 + n * HD], HD), AX.X,
                                ALU.add).then_inc(s["summed"], 1)
                h0 += n
            for j, (_, c0, width) in enumerate(LATENTS):
                v.tensor_reduce(sl[:, j, :], sq[:, :, c0:c0 + width], AX.X, ALU.add).then_inc(
                    s["summed"], 1)
            dve.wait_ge(s["std_done"], 3)
            dve.wait_ge(s["const_in"], 16 * 8)
            for j, (_, _, width) in enumerate(LATENTS):
                rsqrt_mean(v, link, rsl[:, j, :], stl[:, j, :], sl[:, j, :], tml[:, j, :], 1.0 / width)
            for j, (_, c0, width) in enumerate(LATENTS):
                x = hh[:, :, c0:c0 + width]
                link(v.tensor_tensor(x, x, inner(rsl[:, j, :], width), ALU.mult))
                v.tensor_tensor(x, x, middle(lat_g[:, c0 - 768:c0 - 768 + width], TX),
                                ALU.mult).then_inc(s["lat_done"], 1)
            rsqrt_mean(v, link, rstd[:], std[:], ss[:], tmp[:], 1.0 / HD)
            h0 = 0
            for c0, n in RUNS2:
                x = heads_of(hh[:, :, c0:c0 + n * HD], HD)
                link(v.tensor_tensor(x, x, over(rstd[:, :, h0:h0 + n], HD), ALU.mult))
                h0 += n
            for j, (_, c0, n) in enumerate(GAINS2):
                x = heads_of(hh[:, :, c0:c0 + n * HD], HD)
                link(v.tensor_tensor(x, x, gain_over(gains[:, j, :], TX, n), ALU.mult))
            for t in range(TX):
                dve.wait_ge(s["kv_done"], t + 1)
                both = pkv[t % 2][:].rearrange("p (h d) -> p h d", d=P)
                link(v.tensor_copy(mk[:, t, :, 0:HD], both[:, :, 0:HD]))
                link(v.tensor_copy(mk[:, t, :, HD:QK],
                                   middle(hh[:, t, ROPE_COLS[0]:sum(ROPE_COLS)], 4)))
                v.tensor_copy(mv[:, t, :, :], both[:, :, HD:P]).then_inc(s["kv_read"], 1)

        @block.tensor
        def _(pe):
            pe.wait_ge(s["lat_done"], 2)
            pe.wait_ge(s["w_in"], 32)
            for t in range(TX):
                if t >= 2:
                    pe.wait_ge(s["tp_read"], t - 1)
                for k in range(3):
                    tr = nc.tensor.transpose(tp[t % 2][:, k, :],
                                             hh[:, t, 768 + k * P:768 + (k + 1) * P], e["ident"][:])
                tr.then_inc(s["tp_done"], 1)
            for t in range(TX):
                pe.wait_ge(s["tp_read"], t + 1)
                if t >= 2:
                    pe.wait_ge(s["q_read"], t - 1)
                    pe.wait_ge(s["kv_read"], t - 1)
                for k in range(2):
                    mm = nc.tensor.matmul(pq[t % 2][:], lat_t[:, t, k, :], w_uq[:, k, :],
                                          start=(k == 0), stop=(k == 1))
                mm.then_inc(s["q_done"], 1)
                nc.tensor.matmul(pkv[t % 2][:], lat_t[:, t, 2, :], w_ukv[:], start=True,
                                 stop=True).then_inc(s["kv_done"], 1)


def key_slot(slot, side):
    return slot if side == 0 else {0: 10, 1: 11, 6: 12, 7: 13, 8: 14, 9: 15}[slot]


def turn_heads(nc, e, hh, mq, mk, q_t, k_t):
    with Phase(nc, "turn2") as ph:
        sq = ph.sb("sq", [P, 2, TX, 4, QK])
        ss, std, rstd, tms = (ph.sb(x, [P, 2, TX, 4]) for x in ("ss", "std", "rstd", "tms"))
        tmp = ph.sb("tmp", [P, TX, 4, 32])
        gains = ph.sb("gains", [P, 2, QK])
        line = ph.sb("line", [P, 2, TX, 32])
        dk = ph.sb("dk", [P, TX, 4, HD])
        eps = ph.sb("eps", [P, 1])
        tp = [ph.ps(f"tp{i}", [P, TX, P]) for i in range(4)]
        names = "const_in sq_done summed std_done eps_done ready dk_done tp_done tp_read zeroed step"
        s = {x: ph.sem(x) for x in names.split()}
        block = ph.block()
        pair = lambda c0, t: hh[:, t, c0:c0 + P]
        jobs = []
        for which, (a, c, d) in enumerate([(0, 1184, 1952), (256, 1440, None)]):
            sc = (1.0, 0.125)[which == 0]
            for j in range(2):
                jobs.append((lambda t, x=a + j * P: pair(x, t), P, which, j, sc))
                jobs.append((lambda t, x=c + j * P: pair(x, t), P, which, 6 + j, sc))
                if d is not None:
                    jobs.append((lambda t, x=d + j * P: pair(x, t), P, which, 8 + j, sc))
                else:
                    jobs.append((lambda t, j=j: dk[:, t, 2 * j:2 * j + 2, :].rearrange(
                        "p h d -> p (h d)"), P, which, 8 + j, sc))
        early = len(jobs)
        zero = [q_t[QK:P, 2:6, :], k_t[QK:P, 2:6, :], k_t[HALVES[1], 0:2, :], k_t[HALVES[1], 6:10, :],
                k_t[HALVES[0], 10:16, :]]
        for which, m in enumerate([mq, mk]):
            for h in range(4):
                jobs.append((lambda t, m=m, h=h: m[:, t, h, :], QK, which, 2 + h,
                             QK ** -0.5 if which == 0 else 1.0))

        @block.sync
        def _(sp):
            sp.dma_start(gains[:, 0, :], bcast_rows(e["small"]["mla_q_g_2"])).then_inc(s["const_in"], 16)
            sp.dma_start(gains[:, 1, :], bcast_rows(e["small"]["mla_k_g_2"])).then_inc(s["const_in"], 16)
            sp.dma_start(line[:], e["c_line"].rearrange("s (t p) d -> p s t d", p=P)).then_inc(
                s["const_in"], 16)

        copies = []
        for _, rows, which, slot, _ in jobs:
            if rows == QK or which == 0:
                copies.append([(slice(0, rows), (q_t, k_t)[which][0:rows, slot, :])])
            else:
                copies.append([(half, k_t[half, key_slot(slot, side), :])
                               for side, half in enumerate(HALVES)])
        reads = [sum(len(c) for c in copies[:j]) for j in range(len(jobs) + 1)]

        @block.gpsimd
        def _(pool):
            for i, dst in enumerate(zero):
                nc.gpsimd.memset(dst, 0.0).then_inc(s["zeroed"], 1)
                pool.wait_ge(s["zeroed"], i + 1)

        @block.scalar
        def _(act):
            for j, m in enumerate([mq, mk]):
                nc.scalar.activation(sq[:, j], m[:], ACT.Square).then_inc(s["sq_done"], 1)
            act.wait_ge(s["eps_done"], 1)
            act.wait_ge(s["summed"], 2)
            nc.scalar.activation(std[:], ss[:], ACT.Sqrt, scale=1.0 / QK, bias=eps[:]).then_inc(
                s["std_done"], 1)
            for j, (_, _, _, _, scale) in enumerate(jobs):
                act.wait_ge(s["tp_done"], j + 1)
                for rows, dst in copies[j]:
                    nc.scalar.activation(dst.rearrange("p (t n) -> p t n", n=P), tp[j % 4][rows],
                                         ACT.Copy, scale=scale).then_inc(s["tp_read"], 1)

        @block.vector
        def _(dve):
            v = nc.vector
            link = Chain(dve, s["step"])
            v.memset(eps[:], EPS).then_inc(s["eps_done"], 1)
            for c in range(2):
                v.tensor_copy(dk[:, :, c:4:2, :], heads_of(hh[:, :, 2208:2336], HD)).then_inc(
                    s["dk_done"], 1)
            for j in range(2):
                dve.wait_ge(s["sq_done"], j + 1)
                v.tensor_reduce(ss[:, j], sq[:, j], AX.X, ALU.add).then_inc(s["summed"], 1)
            dve.wait_ge(s["const_in"], 48)
            dve.wait_ge(s["std_done"], 1)
            rsqrt_mean(v, link, rstd[:], std[:], ss[:], tms[:], 1.0 / QK)
            for j, m in enumerate([mq, mk]):
                link(v.tensor_tensor(m[:], m[:], over(rstd[:, j], QK), ALU.mult))
                link(v.tensor_tensor(m[:], m[:], gain_over(gains[:, j, :], TX, 4), ALU.mult))
                x = m[:, :, :, HD:QK]
                wide = lambda ap: ap.unsqueeze(2).broadcast_to([P, TX, 4, ap.shape[2]])
                link(v.tensor_tensor(tmp[:, :, :, 0:16], x[:, :, :, 16:32],
                                     wide(line[:, 1, :, 0:16]), ALU.mult))
                link(v.tensor_tensor(tmp[:, :, :, 16:32], x[:, :, :, 0:16],
                                     wide(line[:, 1, :, 16:32]), ALU.mult))
                link(v.tensor_tensor(x, x, wide(line[:, 0]), ALU.mult))
                last = v.tensor_tensor(x, x, tmp[:], ALU.add)
                if j == 0:
                    link(last)
                else:
                    last.then_inc(s["ready"], 1)

        @block.tensor
        def _(pe):
            pe.wait_ge(s["dk_done"], 2)
            for j, (src, rows, _, _, _) in enumerate(jobs):
                if j == early:
                    pe.wait_ge(s["ready"], 1)
                if j >= 4:
                    pe.wait_ge(s["tp_read"], reads[j - 3])
                for t in range(TX):
                    tr = nc.tensor.transpose(tp[j % 4][0:rows, t, :], src(t), e["ident"][:])
                tr.then_inc(s["tp_done"], 1)


def mlp(nc, e, h_t):
    with Phase(nc, "mlp") as ph:
        ring, groups = 4, FF // NCHUNK
        w = ph.sb("w", [P, ring, 4096])
        u_t = ph.sb("u_t", [P, FF // P, SEQ])
        acc = [ph.ps(f"acc{i}", [P, NCHUNK]) for i in range(8)]
        loaded = [ph.sem(f"loaded{i}") for i in range(ring)]
        group_used, up_done, up_read = ph.sem("group_used"), ph.sem("up_done"), ph.sem("up_read")
        squared = ph.sem("squared")
        down_done, added, stored = ph.sem("down_done"), ph.sem("added"), ph.sem("stored")
        block = ph.block()
        up_view = e["w_up_2"][0].rearrange("(k p) n -> p k n", p=P)
        down_view = e["w_down_2"][0].rearrange("(k p) n -> p k n", p=P)

        @block.sync
        def _(sp):
            for j in range(2 * groups):
                g = j % groups
                if j >= ring:
                    sp.wait_ge(group_used, j - ring + 1)
                if j < groups:
                    dst = w[:, j % ring, :].rearrange("p (k n) -> p k n", k=KD)
                    src = up_view[:, :, g * NCHUNK:(g + 1) * NCHUNK]
                else:
                    dst = w[:, j % ring, :].rearrange("p (k n) -> p k n", k=4)
                    src = down_view[:, 4 * g:4 * g + 4, :]
                sp.dma_start(dst, src).then_inc(loaded[j % ring], 16)
            rows = e["out"][0].rearrange("(t p) d -> p t d", p=P)
            for t in range(TX):
                sp.wait_ge(added, 2 * t + 2)
                sp.dma_start(rows[:, t, :], e["res"][:, TC + t, :]).then_inc(stored, 16)
            sp.wait_ge(stored, 16 * TX)

        @block.tensor
        def _(pe):
            for j in range(groups):
                pe.wait_ge(loaded[j % ring], 16 * (j // ring + 1))
                wj = w[:, j % ring, :].rearrange("p (k n) -> p k n", k=KD)
                for q in range(4):
                    i = 4 * j + q
                    if i >= 8:
                        pe.wait_ge(up_read, i - 7)
                    for k in range(KD):
                        mm = nc.tensor.matmul(acc[i % 8][:], wj[:, k, q * P:(q + 1) * P],
                                              h_t[:, k, :], start=(k == 0), stop=(k == KD - 1))
                    mm.then_inc(up_done, 1)
                pe.wait_ge(up_done, 4 * j + 4)
                pe.sem_inc(group_used, 1)
            pe.wait_ge(squared, 4 * groups)
            for j in range(groups):
                b = (groups + j) % ring
                pe.wait_ge(loaded[b], 16 * ((groups + j) // ring + 1))
                wj = w[:, b, :].rearrange("p (k n) -> p k n", k=4)
                for q in range(4):
                    f = 4 * j + q
                    for t in range(TX):
                        for c in range(2):
                            mm = nc.tensor.matmul(acc[2 * t + c][:],
                                                  u_t[:, f, t * P:(t + 1) * P],
                                                  wj[:, q, c * NCHUNK:(c + 1) * NCHUNK],
                                                  start=(f == 0), stop=(f == FF // P - 1),
                                                  skip_group_check=True)
                            if f == FF // P - 1:
                                mm.then_inc(down_done, 1)
                            elif q == 3 and (t, c) == (TX - 1, 1):
                                mm.then_inc(group_used, 1)

        @block.scalar
        def _(act):
            for i in range(4 * groups):
                act.wait_ge(up_done, i + 1)
                nc.scalar.activation(u_t[:, i, :], acc[i % 8][:], ACT.Relu).then_inc(up_read, 1)

        @block.vector
        def _(dve):
            for i in range(4 * groups):
                dve.wait_ge(up_read, i + 1)
                nc.vector.tensor_tensor(u_t[:, i, :], u_t[:, i, :], u_t[:, i, :],
                                        ALU.mult).then_inc(squared, 1)
            for i in range(2 * TX):
                t, c = i // 2, i % 2
                dst = e["res"][:, TC + t, c * NCHUNK:(c + 1) * NCHUNK]
                dve.wait_ge(down_done, i + 1)
                nc.vector.tensor_tensor(dst, dst, acc[i][:], ALU.add).then_inc(added, 1)


def block_2(nc, e):
    stream = list(range(TC, NT))
    sb = nc.sbuf_tensor
    with sb("c_buffer", [P, TX * D], F32) as buffer:
        h_t = buffer[:].rearrange("p (k n) -> p k n", k=KD)
        o = buffer[:].rearrange("p (t d) -> p t d", t=TX)
        normalise(nc, e, "norm_in2", stream, e["attn_norm_g_2"][0], None, h_t, final=e["final_g"])
        with sb("c_hh", [P, TX, QKV2], F32) as hh, sb("c_mv", [P, TX, 4, HD], F32) as mv, \
                sb("c_q", [P, 10, SEQ], F32) as q_t, sb("c_k", [P, 16, SEQ], F32) as k_t:
            project_in(nc, e, h_t, hh)
            with sb("c_mq", [P, TX, 4, QK], F32) as mq, sb("c_mk", [P, TX, 4, QK], F32) as mk:
                prepare_heads(nc, e, hh, mq, mk, mv)
                turn_heads(nc, e, hh, mq, mk, q_t, k_t)
            units = []
            for b in range(TX):
                for head in range(NH):
                    kind, h = head // 4, head % 4
                    slot = {0: h // 2, 1: 2 + h, 2: 6 + h // 2, 3: 8 + h // 2}[kind]
                    k_slot = 2 + h if kind == 1 else key_slot(slot, h % 2)
                    first = max(0, b - 1) if kind == 3 else 0
                    width = (b + 1 - first) * P
                    if kind == 1:
                        values = [mv[:, j, h, :] for j in range(first, b + 1)]
                    else:
                        c0 = {0: VALUES2[0] + h * HD, 2: VALUES2[1] + h * HD,
                              3: VALUES2[2] + h // 2 * HD}[kind]
                        values = [hh[:, j, c0:c0 + HD] for j in range(first, b + 1)]
                    units.append(dict(
                        q=q_t[:, slot, b * P:(b + 1) * P],
                        keys=[(0, k_t[:, k_slot, first * P:(b + 1) * P], width)],
                        width=width, mask=(h, 4, 5 + h, 9 + h)[kind], mask0=512 - width,
                        head=head, values=values))
            masked_attention(
                nc, e, "att2", units, [13, 512], e["c_bias2"].rearrange("h p n -> p h n"),
                [(0, e["c_neg"]), (12, e["small"]["swa_sinks_2"])],
                lambda g: o[:, g // 2, (g % 2) * NCHUNK:(g % 2 + 1) * NCHUNK].rearrange(
                    "p (h d) -> p h d", d=HD))
        with sb("m_h", [P, KD, SEQ], F32) as m_h:
            project_out(nc, e, "out2", o, stream, 4, e["group_out_g_2"][0].rearrange("a d -> (a d)"),
                        1.0, e["w_o_2"][0], None, e["mlp_norm_g_2"][0], None, h_t=m_h)
            mlp(nc, e, m_h)


def build(nc, e, upto=3):
    e["res"] = nc.alloc_sbuf_tensor("res", [P, NT, D], F32).ap()
    e["ident"] = nc.alloc_sbuf_tensor("ident_sb", [P, P], F32).ap()
    e["ones"] = nc.alloc_sbuf_tensor("ones_sb", [P, P], F32).ap()
    load_constants(nc, e)
    modulation(nc, e)
    if upto >= 1:
        with ExitStack() as stack:
            layer_0(nc, e, stack)
    if upto >= 2:
        with ExitStack() as stack:
            layer_1(nc, e, stack)
    if upto >= 3:
        block_2(nc, e)



_INS = ["x", "c", "ctx", "c_ctx", "mod_w", "mod_b", "norm1_g", "norm2_g", "a_w_qkv", "a_w_o",
        "a_lam", "a_subln_g", "b_w_qkv", "b_w_o", "b_sink", "moe_router_g", "moe_router_g_b",
        "moe_router_e", "moe_router_e_b", "moe_w_gate", "moe_w_up", "moe_w_down", "final_g",
        "attn_norm_g_2", "w_in_2", "mla_w_uq_2", "mla_w_ukv_2", "group_out_g_2", "w_o_2",
        "mlp_norm_g_2", "w_up_2", "w_down_2"]
_SMALL = ["moba_q_g_2", "moba_k_g_2", "mla_qlat_g_2", "mla_kvlat_g_2", "mla_q_g_2", "mla_k_g_2",
          "dil_q_g_2", "dil_k_g_2", "swa_q_g_2", "swa_k_g_2", "swa_sinks_2"]


def kernel(**inputs):
    import concourse.bacc as bacc
    from concourse.bass_utils import run_bass_kernel_spmd

    nc = bacc.Bacc("TRN2", target_bir_lowering=False, num_devices=1)
    arrays, e = {}, {"small": {}}

    def give(name, a):
        arrays[name] = np.ascontiguousarray(a)
        return nc.dram_tensor(name, a.shape, F32, kind="ExternalInput").ap()

    for name in _INS:
        e[name] = give(f"in_{name}", inputs[name])
    for name in _SMALL:
        e["small"][name] = give(f"in_{name}", inputs[name])[0]
    for name, a in constants().items():
        e[f"c_{name}"] = give(f"const_{name}", a)
    e["out"] = nc.dram_tensor("result", (1, SEQ, D), F32, kind="ExternalOutput").ap()
    e["mod_dram"] = nc.dram_tensor("mod_scratch", (2, LAYERS * 6 * D), F32, kind="Internal").ap()
    e["h_dram"] = nc.dram_tensor("moe_tokens", (NT * P, D), F32, kind="Internal").ap()
    e["y_dram"] = nc.dram_tensor("moe_results", (2 * NT * P, D), F32, kind="Internal").ap()
    build(nc, e)
    r = run_bass_kernel_spmd(nc, [arrays], core_ids=[0])
    return r.results[0]["result"]
```

```python
import math
from contextlib import ExitStack

import numpy as np

import concourse.bass as bass
from concourse import mybir

F32 = mybir.dt.float32
I32 = mybir.dt.int32
ALU = mybir.AluOpType
ACT = mybir.ActivationFunctionType
AX = mybir.AxisListType

P = 128
D = 1024
KD = D // P
SEQ, CTX = 512, 256
TX, TC = SEQ // P, CTX // P
NT = TX + TC
HD = 64
NH = D // HD
HALVES = (slice(0, HD), slice(HD, P))
NCHUNK = 512
EPS = 1e-6
NEG = -1e30
LAYERS = 2
NE, NG, EPG = 32, 4, 8
FE = 512
BIG = 8192.0
FF = 4096
QKV2 = 2464
LOG2E = 1.4426950408889634
LN2_HI, LN2_LO = 0.693359375, -2.12194440054690583e-4
ROUND = 1.5 * 2.0 ** 23 + 127.0
LAM_INIT = 0.8 - 0.6 * math.exp(0.0)



def rope_table(angles, copies):
    cos, sin = np.cos(angles), np.sin(angles)
    both = np.stack([np.concatenate([cos, cos], -1), np.concatenate([-sin, sin], -1)])
    return both.reshape(2, angles.shape[0], copies * 2 * angles.shape[-1]).astype(np.float32)


def constants():
    f = np.float32
    out = {"ident": np.eye(P, dtype=f)}
    t = np.arange(SEQ)
    inv = (1.0 / (f(10000.0) ** (np.arange(16, dtype=f) / f(16)))).astype(f)
    pos = np.stack([t // 64, t % 64], -1).astype(f)
    out["axial"] = rope_table((pos[:, :, None] * inv).astype(f), 2)
    inv = (1.0 / (f(10000.0) ** (np.arange(0, 32, 2, dtype=f) / f(32)))).astype(f)
    out["line"] = rope_table((t.astype(f)[:, None] * inv).astype(f), 1)
    q = np.arange(P)[:, None]
    band = np.zeros((TX, P, 640), f)
    for b in range(TX):
        k = np.arange(max(0, b - 1) * P, min(TX, b + 2) * P)[None, :]
        band[b, :, CTX:CTX + k.shape[1]] = np.where(np.abs(k - b * P - q) <= 128, 0, NEG)
    out["band"] = band
    slopes = np.exp2(-8.0 * np.arange(1, 13, dtype=f).reshape(4, 3) / 12).astype(f)
    dist = q + 384 - np.arange(512)[None, :]
    tables = []
    for h in range(4):
        tables.append(np.where(dist >= 0, -slopes[h, 0] * dist.astype(f), NEG))
    tables.append(np.where(dist >= 0, 0, NEG))
    n = ((dist >= 0) & (dist <= 128)).astype(int) + ((dist >= 0) & (dist % 4 == 0)) + (
        (dist >= 0) & (dist % 16 == 0))
    for h in range(4):
        tables.append(np.where(n > 0, -slopes[h, 1] * dist.astype(f) + np.log(np.maximum(n, 1)), NEG))
    for h in range(4):
        tables.append(np.where((dist >= 0) & (dist < 128), -slopes[h, 2] * dist.astype(f), NEG))
    out["bias2"] = np.stack(tables).astype(f)
    out["before"] = np.triu(np.ones((P, P), f), 1)
    out["ones"] = np.ones((P, P), f)
    out["iota"] = np.broadcast_to(np.arange(P, dtype=f), (P, P)).copy()
    rows = np.arange(NT * P).reshape(NT, P).T
    out["neg"] = np.full((12,), NEG, f)
    out["rowid"] = (np.stack([rows, rows, rows + NT * P], 1) - BIG).astype(f)
    return out



class Phase:

    def __init__(self, nc, name):
        self.nc, self.name, self.stack, self.sems = nc, name, ExitStack(), []

    def sb(self, name, shape, dt=F32):
        return self.stack.enter_context(self.nc.sbuf_tensor(f"{self.name}_{name}", shape, dt))

    def ps(self, name, shape):
        return self.stack.enter_context(self.nc.psum_tensor(f"{self.name}_{name}", shape, F32))

    def sem(self, name):
        self.sems.append(self.nc.alloc_semaphore(f"{self.name}_{name}"))
        return self.sems[-1]

    def block(self):
        return self.stack.enter_context(self.nc.Block())

    def __enter__(self):
        return self

    def __exit__(self, *e):
        self.stack.close()
        numbers = sorted(sem.num for sem in self.sems)
        while numbers:
            n = next((i for i, x in enumerate(numbers) if x != numbers[0] + i), len(numbers))
            self.nc.gpsimd.sem_clear(range(numbers[0], numbers[0] + n))
            numbers = numbers[n:]
        for sem in self.sems:
            self.nc.release_semaphore(sem)


class Chain:

    def __init__(self, eng, sem):
        self.eng, self.sem, self.n = eng, sem, 0

    def __call__(self, ins):
        self.n += 1
        ins.then_inc(self.sem, 1)
        self.eng.wait_ge(self.sem, self.n)


def rsqrt_mean(v, link, out, std, ss, tmp, scale):
    link(v.reciprocal(out, std))
    link(v.tensor_scalar(tmp, ss, scale, EPS, ALU.mult, ALU.add))
    link(v.tensor_tensor(tmp, tmp, out, ALU.mult))
    link(v.tensor_tensor(tmp, tmp, out, ALU.mult))
    link(v.tensor_scalar(tmp, tmp, -0.5, 1.5, ALU.mult, ALU.add))
    link(v.tensor_tensor(out, out, tmp, ALU.mult))


def bcast_rows(vec):
    return vec.partition_broadcast(P)


def inner(ap, n):
    return ap.unsqueeze(2).broadcast_to([ap.shape[0], ap.shape[1], n])


def middle(ap, n):
    return ap.unsqueeze(1).broadcast_to([ap.shape[0], n, ap.shape[1]])



def modulation(nc, e):
    per_layer = 6 * D // NCHUNK
    chunks = LAYERS * per_layer
    ring = 3
    with Phase(nc, "mod") as ph:
        vec = ph.sb("vec", [P, 2, KD])
        expn, whole, rest = (ph.sb(x, [P, 2, KD]) for x in ("expn", "whole", "rest"))
        act = ph.sb("act", [P, KD, 2])
        w = ph.sb("w", [P, ring, KD, NCHUNK])
        bias = ph.sb("bias", [2, LAYERS * 6 * D])
        rows = ph.sb("rows", [2, LAYERS * 6 * D])
        acc = [ph.ps(f"acc{i}", [P, NCHUNK]) for i in range(4)]
        vec_in, bias_in, stored = ph.sem("vec_in"), ph.sem("bias_in"), ph.sem("stored")
        exp_done, act_done, step = ph.sem("exp_done"), ph.sem("act_done"), ph.sem("step")
        rest_done, arrived = ph.sem("rest_done"), ph.sem("arrived")
        sq = ph.sb("sq", [P, D])
        runs, eps = ph.sb("runs", [P, 32]), ph.sb("eps", [P, 1])
        ss, std, tmp = (ph.sb(x, [P, NT]) for x in ("ss", "std", "tmp"))
        sq_done, summed, std_done = ph.sem("sq_done"), ph.sem("summed"), ph.sem("std_done")
        eps_done = ph.sem("eps_done")
        loaded = [ph.sem(f"loaded{i}") for i in range(ring)]
        mm_done, rows_done = ph.sem("mm_done"), ph.sem("rows_done")
        block = ph.block()

        @block.sync
        def _(sp):
            sp.dma_start(vec[:, 0, :], e["c"][0].rearrange("(p k) -> p k", k=KD)).then_inc(vec_in, 16)
            sp.dma_start(vec[:, 1, :], e["c_ctx"].rearrange("(p k) -> p k", k=KD)).then_inc(vec_in, 16)
            sp.dma_start(bias[:], e["mod_b"].rearrange("l n -> (l n)").partition_broadcast(2)).then_inc(
                bias_in, 16)
            for j in range(chunks):
                if j >= ring:
                    sp.wait_ge(mm_done, j - ring + 1)
                layer, n0 = j // per_layer, j % per_layer * NCHUNK
                src = e["mod_w"][layer].rearrange("(p k) n -> p k n", k=KD)
                sp.dma_start(w[:, j % ring, :, :], src[:, :, n0:n0 + NCHUNK]).then_inc(
                    loaded[j % ring], 16)
                if j == ring - 1:
                    sp.dma_start(e["res"][:, TC:NT, :],
                                 e["x"][0].rearrange("(t p) d -> p t d", p=P)).then_inc(arrived, 16)
                    sp.dma_start(e["res"][:, 0:TC, :],
                                 e["ctx"][0].rearrange("(t p) d -> p t d", p=P)).then_inc(arrived, 16)
                    sp.dma_start(e["ident"][:], e["c_ident"]).then_inc(arrived, 16)
                    sp.dma_start(e["ones"][:], e["c_ones"]).then_inc(arrived, 16)
            sp.wait_ge(arrived, 16 * 4)
            sp.wait_ge(rows_done, chunks)
            sp.dma_start(e["mod_dram"], rows[:]).then_inc(stored, 16)
            sp.wait_ge(stored, 16)

        @block.scalar
        def _(act_eng):
            act_eng.wait_ge(rest_done, 1)
            nc.scalar.activation(expn[:], rest[:], ACT.Exp, scale=0.25).then_inc(exp_done, 1)
            act_eng.wait_ge(arrived, 16 * 4)
            for t in range(NT):
                if t >= 1:
                    act_eng.wait_ge(summed, t)
                nc.scalar.activation(sq[:], e["res"][:, t, :], ACT.Square).then_inc(sq_done, 1)
            act_eng.wait_ge(summed, NT)
            act_eng.wait_ge(eps_done, 1)
            nc.scalar.activation(std[:], ss[:], ACT.Sqrt, scale=1.0 / D, bias=eps[:]).then_inc(
                std_done, 1)

        @block.vector
        def _(dve):
            link = Chain(dve, step)
            v = nc.vector
            dve.wait_ge(vec_in, 32)
            link(v.tensor_scalar(rest[:], vec[:], -1.0, None, ALU.mult))
            link(v.tensor_scalar(rest[:], rest[:], 80.0, -80.0, ALU.min, ALU.max))
            link(v.tensor_scalar(whole[:], rest[:], LOG2E, ROUND, ALU.mult, ALU.add))
            link(v.tensor_scalar(expn[:], whole[:], ROUND, None, ALU.subtract))
            link(v.scalar_tensor_tensor(rest[:], expn[:], -LN2_HI, rest[:], ALU.mult, ALU.add))
            v.scalar_tensor_tensor(rest[:], expn[:], -LN2_LO, rest[:], ALU.mult, ALU.add).then_inc(
                rest_done, 1)
            link(v.tensor_single_scalar(whole[:].bitcast(I32), whole[:].bitcast(I32), 23,
                                        ALU.logical_shift_left))
            dve.wait_ge(exp_done, 1)
            link(v.tensor_tensor(expn[:], expn[:], expn[:], ALU.mult))
            link(v.tensor_tensor(expn[:], expn[:], expn[:], ALU.mult))
            link(v.tensor_tensor(expn[:], expn[:], whole[:], ALU.mult))
            link(nc.vector.tensor_scalar(expn[:], expn[:], 1.0, None, ALU.add))
            link(nc.vector.reciprocal(expn[:], expn[:]))
            nc.vector.tensor_tensor(act[:].rearrange("p k v -> p v k"), vec[:], expn[:],
                                    ALU.mult).then_inc(act_done, 1)
            v.memset(eps[:], EPS).then_inc(eps_done, 1)
            dve.wait_ge(bias_in, 16)
            for j in range(chunks):
                if 6 <= j < 6 + NT:
                    t = j - 6
                    dve.wait_ge(sq_done, t + 1)
                    link(v.tensor_reduce(runs[:], sq[:].rearrange("p (a b) -> p a b", b=32), AX.X,
                                         ALU.add))
                    v.tensor_reduce(ss[:, t:t + 1], runs[:], AX.X, ALU.add).then_inc(summed, 1)
                    dve.wait_ge(summed, t + 1)
                if j == 6 + NT:
                    dve.wait_ge(std_done, 1)
                    rsqrt_mean(v, link, e["rstd"], std[:], ss[:], tmp[:], 1.0 / D)
                n0 = j * NCHUNK
                dve.wait_ge(mm_done, j + 1)
                nc.vector.tensor_tensor(rows[:, n0:n0 + NCHUNK], acc[j % 4][0:2, :],
                                        bias[:, n0:n0 + NCHUNK], ALU.add).then_inc(rows_done, 1)

        @block.tensor
        def _(pe):
            pe.wait_ge(act_done, 1)
            for j in range(chunks):
                pe.wait_ge(loaded[j % ring], 16 * (j // ring + 1))
                if j >= 4:
                    pe.wait_ge(rows_done, j - 3)
                for k in range(KD):
                    mm = nc.tensor.matmul(acc[j % 4][0:2, :], act[:, k, :], w[:, j % ring, k, :],
                                          start=(k == 0), stop=(k == KD - 1))
                mm.then_inc(mm_done, 1)


def normalise_first(nc, e, name, tiles, gain, shift_scale, rstd, h_t):
    vecs = sorted({0 if t >= TC else 1 for t in tiles})
    nt = len(tiles)
    with Phase(nc, name) as ph:
        g = ph.sb("g", [P, D])
        mul, add, h = (ph.sb(x, [P, 2, D]) for x in ("mul", "add", "h"))
        tp = [ph.ps(f"tp{i}", [P, 4, P]) for i in range(4)]
        vec_in = ph.sem("vec_in")
        step, h_done, tp_done, tp_read = (ph.sem(s) for s in ("step", "h_done", "tp_done", "tp_read"))
        block = ph.block()

        @block.sync
        def _(sp):
            sp.dma_start(g[:], bcast_rows(gain)).then_inc(vec_in, 16)
            for v in vecs:
                shift, scale = shift_scale(v)
                sp.dma_start(mul[:, v, :], bcast_rows(scale)).then_inc(vec_in, 16)
                sp.dma_start(add[:, v, :], bcast_rows(shift)).then_inc(vec_in, 16)

        @block.scalar
        def _(act):
            for j in range(2 * nt):
                i, half = j // 2, j % 2
                act.wait_ge(tp_done, j + 1)
                nc.scalar.copy(h_t[:, 4 * half:4 * half + 4, i * P:(i + 1) * P],
                               tp[j % 4][:]).then_inc(tp_read, 1)

        @block.vector
        def _(dve):
            link = Chain(dve, step)
            dve.wait_ge(vec_in, 16 * (1 + 2 * len(vecs)))
            for v in vecs:
                link(nc.vector.scalar_tensor_tensor(mul[:, v, :], mul[:, v, :], 1.0, g[:],
                                                    ALU.add, ALU.mult))
            for i, t in enumerate(tiles):
                v = 0 if t >= TC else 1
                if i >= 2:
                    dve.wait_ge(tp_done, 2 * (i - 1))
                out = h[:, i % 2, :]
                link(nc.vector.scalar_tensor_tensor(out, e["res"][:, t, :], rstd[:, t:t + 1],
                                                    mul[:, v, :], ALU.mult, ALU.mult))
                nc.vector.tensor_tensor(out, out, add[:, v, :], ALU.add).then_inc(h_done, 1)

        @block.tensor
        def _(pe):
            for j in range(2 * nt):
                i, half = j // 2, j % 2
                pe.wait_ge(h_done, i + 1)
                if j >= 4:
                    pe.wait_ge(tp_read, j - 3)
                for q in range(4):
                    k = 4 * half + q
                    tr = nc.tensor.transpose(tp[j % 4][:, q, :], h[:, i % 2, k * P:(k + 1) * P],
                                             e["ident"][:])
                tr.then_inc(tp_done, 1)


def rope_heads(dve, nc, link, out, src, tmp, cos, sin, half):
    heads, width = src.shape[1], src.shape[2]
    pairs = width // (2 * half)
    link(nc.vector.tensor_tensor(out, src, middle(cos, heads), ALU.mult))
    for side in range(2):
        for a in range(pairs):
            lo, other = (2 * a + side) * half, (2 * a + 1 - side) * half
            op = nc.vector.tensor_tensor(tmp[:, :, lo:lo + half], src[:, :, other:other + half],
                                         middle(sin[:, lo:lo + half], heads), ALU.mult)
            if (side, a) != (1, pairs - 1):
                op.then_inc(link.sem, 1)
                link.n += 1
            else:
                link(op)
    return nc.vector.tensor_tensor(out, out, tmp, ALU.add)


def project_heads(nc, e, name, h_t, w_dram, items, stores, keys):
    chunks = sorted({c for c, _, _ in items})
    ends = [max(i for i, it in enumerate(items) if it[0] == c) + 1 for c in chunks]
    ring, stages = 3, 3
    with Phase(nc, name) as ph:
        w = ph.sb("w", [P, ring, KD, NCHUNK])
        rope = ph.sb("rope", [P, 2, TX, HD])
        stage = ph.sb("stage", [P, stages, 8, HD])
        tmp = ph.sb("tmp", [P, 8, HD])
        acc = [ph.ps(f"acc{i}", [P, NCHUNK]) for i in range(4)]
        tp = [ph.ps(f"tp{i}", [P, 4, P]) for i in range(2)]
        loaded = [ph.sem(f"loaded{i}") for i in range(ring)]
        rope_in, mm_done, acc_read = ph.sem("rope_in"), ph.sem("mm_done"), ph.sem("acc_read")
        zeroed = ph.sem("zeroed")
        tp_done, tp_read, step = ph.sem("tp_done"), ph.sem("tp_read"), ph.sem("step")
        block = ph.block()
        turned = [i for i, it in enumerate(items) if it[2] != "value"]
        reads = [0]
        for i in turned:
            reads.append(reads[-1] + len(stores(items[i][0], items[i][1])[0]))

        @block.gpsimd
        def _(pool):
            for side in range(2):
                other = slice(HD * (1 - side), HD * (2 - side))
                nc.gpsimd.memset(keys[other, side], 0.0).then_inc(zeroed, 1)
                pool.wait_ge(zeroed, side + 1)

        @block.sync
        def _(sp):
            view = w_dram.rearrange("(k p) n -> p k n", p=P)
            for j, c in enumerate(chunks):
                if j >= ring:
                    sp.wait_ge(mm_done, ends[j - ring])
                sp.dma_start(w[:, j % ring, :, :],
                             view[:, :, c * NCHUNK:(c + 1) * NCHUNK]).then_inc(loaded[j % ring], 16)
                if j == 0:
                    sp.dma_start(rope[:], e["c_axial"].rearrange("s (t p) d -> p s t d", p=P)).then_inc(
                        rope_in, 16)

        @block.tensor
        def _(pe):
            def turn(j):
                i = turned[j]
                pe.wait_ge(acc_read, i + 1)
                if j >= 2:
                    pe.wait_ge(tp_read, reads[j - 1])
                for q in range(4):
                    tr = nc.tensor.transpose(
                        tp[j % 2][:, q, :],
                        stage[:, j % stages, 2 * q:2 * q + 2, :].rearrange("p a d -> p (a d)"),
                        e["ident"][:])
                tr.then_inc(tp_done, 1)

            last, j = None, 0
            for i, (c, t, kind) in enumerate(items):
                b = chunks.index(c)
                if c != last:
                    pe.wait_ge(loaded[b % ring], 16 * (b // ring + 1))
                    last = c
                if i >= 4:
                    pe.wait_ge(acc_read, i - 3)
                for k in range(KD):
                    mm = nc.tensor.matmul(acc[i % 4][:], h_t[:, k, t * P:(t + 1) * P],
                                          w[:, b % ring, k, :], start=(k == 0), stop=(k == KD - 1))
                mm.then_inc(mm_done, 1)
                if j < len(turned) and turned[j] <= i - 1:
                    turn(j)
                    j += 1
            while j < len(turned):
                turn(j)
                j += 1

        @block.vector
        def _(dve):
            link = Chain(dve, step)
            dve.wait_ge(rope_in, 16)
            j = 0
            for i, (c, t, kind) in enumerate(items):
                dve.wait_ge(mm_done, i + 1)
                if kind == "value":
                    nc.vector.tensor_copy(stores(c, t), acc[i % 4][:]).then_inc(acc_read, 1)
                    continue
                if j >= stages:
                    dve.wait_ge(tp_done, j - stages + 1)
                dst = stage[:, j % stages, :, :]
                src = acc[i % 4][:].rearrange("p (h d) -> p h d", d=HD)
                j += 1
                if kind == "plain":
                    nc.vector.tensor_copy(dst, src).then_inc(acc_read, 1)
                elif kind == "rope":
                    rope_heads(dve, nc, link, dst, src, tmp[:], rope[:, 0, t - TC, :],
                               rope[:, 1, t - TC, :], 16).then_inc(acc_read, 1)

        @block.scalar
        def _(act):
            for j, i in enumerate(turned):
                c, t, kind = items[i]
                act.wait_ge(tp_done, j + 1)
                parts, scale = stores(c, t)
                for rows, dst in parts:
                    nc.scalar.activation(dst, tp[j % 2][rows], ACT.Copy, scale=scale).then_inc(
                        tp_read, 1)


def diff_attention(nc, e, q_t, k_t, v, o):
    pairs = [(t, h) for t in [*range(TC, NT), *range(TC)] for h in range(8)]
    n = len(pairs)
    keys = lambda t: NT if t >= TC else TC
    with Phase(nc, "dif") as ph:
        lam_v = ph.sb("lam_v", [P, 4, HD])
        lam_p = ph.sb("lam_p", [P, 2, HD])
        lam = ph.sb("lam", [P, 4])
        prob = ph.sb("prob", [P, 2, 2, NT * P])
        prob_t = ph.sb("prob_t", [P, 2, NT, P])
        neg_max = ph.sb("neg_max", [P, 2, 2])
        total = ph.sb("total", [P, 2, 2])
        score = [ph.ps(f"score{i}", [P, 1024]) for i in range(2)]
        tp_a, tp_b = ph.ps("tp_a", [P, 4, P]), ph.ps("tp_b", [P, 4, P])
        out = [ph.ps(f"out{i}", [P, NCHUNK]) for i in range(2)]
        names = "lam_in lam_exp lam_done scored maxed exped combined turned read_a read_b weighed out_read step"
        s = {x: ph.sem(x) for x in names.split()}
        block = ph.block()

        @block.sync
        def _(sp):
            sp.dma_start(lam_v[:].rearrange("p a d -> p (a d)"),
                         e["a_lam"][0].rearrange("a d -> (a d)").partition_broadcast(P)).then_inc(
                             s["lam_in"], 16)

        @block.tensor
        def _(pe):
            def scores(g, m):
                t, h = pairs[g]
                if g >= 1:
                    pe.wait_ge(s["exped"], 2 * g + m - 1)
                width = keys(t) * P
                for n0 in range(0, width, NCHUNK):
                    w = min(NCHUNK, width - n0)
                    mm = nc.tensor.matmul(score[m][:, n0:n0 + w],
                                          q_t[:, h, t * P:(t + 1) * P],
                                          k_t[:, m, h, n0:n0 + w], start=True, stop=True)
                mm.then_inc(s["scored"], 1)

            def turn(g):
                t, h = pairs[g]
                pe.wait_ge(s["combined"], g + 1)
                if g >= 1:
                    pe.wait_ge(s["read_a"], g)
                    pe.wait_ge(s["read_b"], g)
                for k in range(keys(t)):
                    bank = tp_a if k < 4 else tp_b
                    tr = nc.tensor.transpose(bank[:, k % 4, :], prob[:, g % 2, 0, k * P:(k + 1) * P],
                                             e["ident"][:])
                tr.then_inc(s["turned"], 1)

            def weigh(g):
                t, h = pairs[g]
                if g >= 2:
                    pe.wait_ge(s["out_read"], g - 1)
                pe.wait_ge(s["read_a"], g + 1)
                pe.wait_ge(s["read_b"], g + 1)
                for k in range(keys(t)):
                    mm = nc.tensor.matmul(out[g % 2][:, 0:P], prob_t[:, g % 2, k, :],
                                          v[:, k, h * P:(h + 1) * P], start=(k == 0),
                                          stop=(k == keys(t) - 1))
                mm.then_inc(s["weighed"], 1)

            scores(0, 0)
            for g in range(n + 1):
                if g < n:
                    scores(g, 1)
                if g >= 1:
                    turn(g - 1)
                if g + 1 < n:
                    scores(g + 1, 0)
                if g >= 1:
                    weigh(g - 1)

        @block.vector
        def _(dve):
            link = Chain(dve, s["step"])
            dve.wait_ge(s["lam_in"], 16)
            link(nc.vector.tensor_tensor(lam_p[:], lam_v[:, 0:4:2, :], lam_v[:, 1:4:2, :], ALU.mult))
            nc.vector.tensor_reduce(lam[:, 0:2], lam_p[:], AX.X, ALU.add).then_inc(s["lam_done"], 1)
            dve.wait_ge(s["lam_exp"], 1)
            link(nc.vector.tensor_tensor(lam[:, 3:4], lam[:, 1:2], lam[:, 0:1], ALU.subtract))
            link(nc.vector.tensor_scalar(lam[:, 3:4], lam[:, 3:4], -LAM_INIT, None, ALU.add))

            def maximum(g, m):
                t, _ = pairs[g]
                dve.wait_ge(s["scored"], 2 * g + m + 1)
                if g >= 2:
                    dve.wait_ge(s["exped"], 2 * (g - 2) + m + 1)
                nc.vector.tensor_reduce(neg_max[:, g % 2, m:m + 1], score[m][:, 0:keys(t) * P],
                                        AX.X, ALU.max, negate=True).then_inc(s["maxed"], 1)

            def combine(g):
                t, _ = pairs[g]
                width = keys(t) * P
                dve.wait_ge(s["exped"], 2 * g + 2)
                tot = total[:, g % 2, :]
                link(nc.vector.reciprocal(tot, tot))
                link(nc.vector.tensor_tensor(tot[:, 1:2], tot[:, 1:2], lam[:, 3:4], ALU.mult))
                a, b = prob[:, g % 2, 0, 0:width], prob[:, g % 2, 1, 0:width]
                link(nc.vector.tensor_scalar(a, a, tot[:, 0:1], None, ALU.mult))
                nc.vector.scalar_tensor_tensor(a, b, tot[:, 1:2], a, ALU.mult, ALU.add).then_inc(
                    s["combined"], 1)

            def read_b(g):
                t, _ = pairs[g]
                dve.wait_ge(s["turned"], g + 1)
                if g >= 2:
                    dve.wait_ge(s["weighed"], g - 1)
                if keys(t) > 4:
                    nc.vector.tensor_copy(prob_t[:, g % 2, 4:keys(t), :],
                                          tp_b[:, 0:keys(t) - 4, :]).then_inc(s["read_b"], 1)
                else:
                    dve.sem_inc(s["read_b"], 1)

            def read_out(g):
                t, h = pairs[g]
                dve.wait_ge(s["weighed"], g + 1)
                nc.vector.tensor_copy(o[:, t, h * P:(h + 1) * P], out[g % 2][:, 0:P]).then_inc(
                    s["out_read"], 1)

            maximum(0, 0)
            for g in range(n + 1):
                if g < n:
                    maximum(g, 1)
                if g >= 1:
                    read_b(g - 1)
                if g + 1 < n:
                    maximum(g + 1, 0)
                if g < n:
                    combine(g)
                if g >= 1:
                    read_out(g - 1)

        @block.scalar
        def _(act):
            act.wait_ge(s["lam_done"], 1)
            nc.scalar.activation(lam[:, 0:2], lam[:, 0:2], ACT.Exp).then_inc(s["lam_exp"], 1)

            def exponential(g, m):
                t, _ = pairs[g]
                width = keys(t) * P
                if m == 0 and g >= 2:
                    act.wait_ge(s["combined"], g - 1)
                    act.wait_ge(s["turned"], g - 1)
                act.wait_ge(s["maxed"], 2 * g + m + 1)
                nc.scalar.activation(prob[:, g % 2, m, 0:width], score[m][:, 0:width],
                                     ACT.Exp, bias=neg_max[:, g % 2, m:m + 1],
                                     accum_out=total[:, g % 2, m:m + 1]).then_inc(s["exped"], 1)

            exponential(0, 0)
            for g in range(n + 1):
                if g < n:
                    exponential(g, 1)
                if g >= 1:
                    act.wait_ge(s["turned"], g)
                    if g >= 3:
                        act.wait_ge(s["weighed"], g - 2)
                    k = min(4, keys(pairs[g - 1][0]))
                    nc.scalar.copy(prob_t[:, (g - 1) % 2, 0:k, :], tp_a[:, 0:k, :]).then_inc(
                        s["read_a"], 1)
                if g + 1 < n:
                    exponential(g + 1, 0)


def masked_attention(nc, e, name, units, mask, mask_src, sink_src, o):
    n = len(units)
    groups = n // 8
    with Phase(nc, name) as ph:
        masks = ph.sb("masks", [P, *mask])
        sinks = ph.sb("sinks", [P, NH])
        masked = ph.sb("masked", [P, 2, 640])
        prob = ph.sb("prob", [P, 2, 640])
        prob_t = ph.sb("prob_t", [P, 2, 5, P])
        top = ph.sb("top", [P, 2, 8])
        neg_top = ph.sb("neg_top", [P, 2, 8])
        total = ph.sb("total", [P, 2, 8])
        sink_e = ph.sb("sink_e", [P, 2, 8])
        score = [ph.ps(f"score{i}", [P, 1024]) for i in range(2)]
        tp_a, tp_b = ph.ps("tp_a", [P, 4, P]), ph.ps("tp_b", [P, 4, P])
        out = [ph.ps(f"out{i}", [P, 8, HD]) for i in range(2)]
        names = ("const_in scored masked topped exped turned read_a read_b weighed sink_d sink_x "
                 "out_read step")
        s = {x: ph.sem(x) for x in names.split()}
        block = ph.block()
        n_sink = len(sink_src)

        @block.sync
        def _(sp):
            sp.dma_start(masks[:], mask_src).then_inc(s["const_in"], 16)
            for dst0, src in sink_src:
                sp.dma_start(sinks[:, dst0:dst0 + src.shape[0]], bcast_rows(src)).then_inc(
                    s["const_in"], 16)

        @block.tensor
        def _(pe):
            def scores(u):
                unit = units[u]
                if u >= 2:
                    pe.wait_ge(s["masked"], u - 1)
                for col, rhs, w in unit["keys"]:
                    mm = nc.tensor.matmul(score[u % 2][:, col:col + w], unit["q"], rhs,
                                          start=True, stop=True)
                mm.then_inc(s["scored"], 1)

            def turn(u):
                kt = units[u]["width"] // P
                pe.wait_ge(s["exped"], u + 1)
                if u >= 1:
                    pe.wait_ge(s["read_a"], u)
                    pe.wait_ge(s["read_b"], u)
                for k in range(kt):
                    bank = tp_a if k < 4 else tp_b
                    tr = nc.tensor.transpose(bank[:, k % 4, :], prob[:, u % 2, k * P:(k + 1) * P],
                                             e["ident"][:])
                tr.then_inc(s["turned"], 1)

            def weigh(u):
                unit, g = units[u], u // 8
                kt = unit["width"] // P
                if u % 8 == 0 and g >= 2:
                    pe.wait_ge(s["out_read"], g - 1)
                pe.wait_ge(s["read_a"], u + 1)
                pe.wait_ge(s["read_b"], u + 1)
                for k in range(kt):
                    mm = nc.tensor.matmul(out[g % 2][:, u % 8, :], prob_t[:, u % 2, k, :],
                                          unit["values"][k], start=(k == 0), stop=(k == kt - 1))
                mm.then_inc(s["weighed"], 1)

            scores(0)
            scores(1)
            for u in range(n):
                turn(u)
                if u + 2 < n:
                    scores(u + 2)
                weigh(u)

        @block.vector
        def _(dve):
            link = Chain(dve, s["step"])
            dve.wait_ge(s["const_in"], 16 * (1 + n_sink))

            def mask_and_max(u):
                unit, g = units[u], u // 8
                dve.wait_ge(s["scored"], u + 1)
                if u >= 2:
                    dve.wait_ge(s["exped"], u - 1)
                if u % 8 == 0 and g >= 2:
                    dve.wait_ge(s["sink_x"], g - 1)
                col = top[:, g % 2, u % 8:u % 8 + 1]
                nc.vector.tensor_tensor_reduce(
                    masked[:, u % 2, 0:unit["width"]], score[u % 2][:, 0:unit["width"]],
                    masks[:, unit["mask"], unit["mask0"]:unit["mask0"] + unit["width"]], 1.0,
                    sinks[:, unit["head"]:unit["head"] + 1], ALU.add, ALU.max, col).then_inc(s["masked"], 1)
                dve.wait_ge(s["masked"], u + 1)
                nc.vector.tensor_scalar(neg_top[:, g % 2, u % 8:u % 8 + 1], col, -1.0, None,
                                        ALU.mult).then_inc(s["topped"], 1)

            def read_b(u):
                unit = units[u]
                dve.wait_ge(s["turned"], u + 1)
                if u >= 2:
                    dve.wait_ge(s["weighed"], u - 1)
                if unit["width"] > 4 * P:
                    nc.vector.tensor_copy(prob_t[:, u % 2, 4:5, :], tp_b[:, 0:1, :]).then_inc(
                        s["read_b"], 1)
                else:
                    dve.sem_inc(s["read_b"], 1)

            def finish(g):
                head = units[8 * g]["head"]
                dve.wait_ge(s["topped"], 8 * g + 8)
                if g >= 2:
                    dve.wait_ge(s["sink_x"], g - 1)
                nc.vector.tensor_tensor(sink_e[:, g % 2, :], sinks[:, head:head + 8],
                                        top[:, g % 2, :], ALU.subtract).then_inc(s["sink_d"], 1)
                dve.wait_ge(s["sink_x"], g + 1)
                dve.wait_ge(s["exped"], 8 * g + 8)
                tot = total[:, g % 2, :]
                link(nc.vector.tensor_tensor(tot, tot, sink_e[:, g % 2, :], ALU.add))
                link(nc.vector.reciprocal(tot, tot))
                dve.wait_ge(s["weighed"], 8 * g + 8)
                nc.vector.tensor_tensor(o(g), out[g % 2][:], inner(tot, HD), ALU.mult).then_inc(
                    s["out_read"], 1)

            mask_and_max(0)
            mask_and_max(1)
            for u in range(n + 1):
                if u < n:
                    read_b(u)
                if u + 2 < n:
                    mask_and_max(u + 2)
                if u >= 8 and u % 8 == 0:
                    finish(u // 8 - 1)

        @block.scalar
        def _(act):
            def exponential(u):
                unit, g = units[u], u // 8
                if u >= 2:
                    act.wait_ge(s["turned"], u - 1)
                if u % 8 == 0 and g >= 2:
                    act.wait_ge(s["out_read"], g - 1)
                act.wait_ge(s["topped"], u + 1)
                nc.scalar.activation(prob[:, u % 2, 0:unit["width"]],
                                     masked[:, u % 2, 0:unit["width"]], ACT.Exp,
                                     bias=neg_top[:, g % 2, u % 8:u % 8 + 1],
                                     accum_out=total[:, g % 2, u % 8:u % 8 + 1]).then_inc(
                                         s["exped"], 1)

            exponential(0)
            exponential(1)
            for u in range(n + 1):
                if u < n:
                    k = min(4, units[u]["width"] // P)
                    act.wait_ge(s["turned"], u + 1)
                    if u >= 2:
                        act.wait_ge(s["weighed"], u - 1)
                    nc.scalar.copy(prob_t[:, u % 2, 0:k, :], tp_a[:, 0:k, :]).then_inc(
                        s["read_a"], 1)
                if u + 2 < n:
                    exponential(u + 2)
                if u >= 8 and u % 8 == 0:
                    g = u // 8 - 1
                    act.wait_ge(s["sink_d"], g + 1)
                    nc.scalar.activation(sink_e[:, g % 2, :], sink_e[:, g % 2, :],
                                         ACT.Exp).then_inc(s["sink_x"], 1)


def project_out(nc, e, name, o, tiles, heads, gain, gain_scale, w_dram, gate, norm_gain, shift_scale,
                h_t=None, store=None, router=None):
    nt = len(tiles)
    vecs = sorted({0 if t >= TC else 1 for t in tiles}) if gate else []
    with Phase(nc, name) as ph:
        w = ph.sb("w", [P, 2, KD, NCHUNK])
        o_t = ph.sb("o_t", [P, 2, KD, P])
        gates = ph.sb("gates", [P, 2, D])
        g = ph.sb("g", [P, D])
        sq = ph.sb("sq", [P, D])
        n_sq = ph.sb("n_sq", [P, D])
        hh = heads or 1
        ss, std, rstd, tmp = (ph.sb(x, [P, nt, hh]) for x in ("ss", "std", "rstd", "tmp"))
        n_ss, n_std, n_rstd, n_tmp = (ph.sb(x, [P, nt]) for x in ("n_ss", "n_std", "n_rstd", "n_tmp"))
        runs = ph.sb("runs", [P, 32])
        part = ph.sb("part", [P, NCHUNK])
        n_g = ph.sb("n_g", [P, D])
        mul, add = ph.sb("mul", [P, 2, D]), ph.sb("add", [P, 2, D])
        h = ph.sb("h", [P, 2, D])
        eps = ph.sb("eps", [P, 1])
        if router:
            layer, logits = router
            h_tile = ph.sb("h_tile", [P, 2, KD, P])
            wr = ph.sb("wr", [P, KD, NG + NE])
            bias = ph.sb("bias", [P, NG + NE])
            lg = ph.ps("lg", [P, NG + NE])
        tp = [ph.ps(f"tp{i}", [P, 4, P]) for i in range(2)]
        n_tp = [ph.ps(f"n_tp{i}", [P, 4, P]) for i in range(2)]
        acc = [ph.ps(f"acc{i}", [P, NCHUNK]) for i in range(3)]
        names = ("vec_in g_in sq_done summed std_done eps_done o_done tp_done tp_read mm_done added n_vec_in "
                 "n_sq_done n_summed n_std_done h_done n_tp_done n_tp_read lg_done lg_read step")
        s = {x: ph.sem(x) for x in names.split()}
        loaded = [ph.sem(f"loaded{i}") for i in range(4)]
        stored = [ph.sem(f"stored{i}") for i in range(2)]
        block = ph.block()
        n_norm = 1 + 2 * len(vecs) + (4 if router else 0)
        side = lambda t: 0 if t >= TC else 1

        @block.sync
        def _(sp):
            if gain is not None:
                sp.dma_start(g[:, 0:gain.shape[0]], bcast_rows(gain)).then_inc(s["g_in"], 16)
            view = w_dram.rearrange("(k p) n -> p k n", p=P)
            for c in range(2):
                for half in range(2):
                    ks = slice(4 * half, 4 * half + 4)
                    sp.dma_start(w[:, c, ks, :], view[:, ks, c * NCHUNK:(c + 1) * NCHUNK]).then_inc(
                        loaded[2 * c + half], 16)
            for v in vecs:
                sp.dma_start(gates[:, v, :], bcast_rows(gate(v))).then_inc(s["vec_in"], 16)
            sp.dma_start(n_g[:], bcast_rows(norm_gain)).then_inc(s["n_vec_in"], 16)
            for v in vecs:
                shift, scale = shift_scale(v)
                sp.dma_start(add[:, v, :], bcast_rows(shift)).then_inc(s["n_vec_in"], 16)
                sp.dma_start(mul[:, v, :], bcast_rows(scale)).then_inc(s["n_vec_in"], 16)
            if router:
                for dst, src in [
                        (wr[:, :, 0:NG], e["moe_router_g"][layer].rearrange("(k p) n -> p k n", p=P)),
                        (wr[:, :, NG:], e["moe_router_e"][layer].rearrange("(k p) n -> p k n", p=P)),
                        (bias[:, 0:NG], bcast_rows(e["moe_router_g_b"][layer])),
                        (bias[:, NG:], bcast_rows(e["moe_router_e_b"][layer]))]:
                    sp.dma_start(dst, src).then_inc(s["n_vec_in"], 16)
            if store is not None:
                for i, t in enumerate(tiles):
                    sp.wait_ge(s["h_done"], i + 1)
                    sp.dma_start(store[t * P:(t + 1) * P, :], h[:, i % 2, :]).then_inc(
                        stored[i % 2], 16)
                for b in range(2):
                    sp.wait_ge(stored[b], 16 * (nt // 2))

        @block.scalar
        def _(act):
            def square_slices(i):
                if gain is None or i >= nt:
                    return
                if i >= 1:
                    act.wait_ge(s["summed"], i)
                nc.scalar.activation(sq[:], o[:, i, :], ACT.Square).then_inc(s["sq_done"], 1)

            def root_slices(i):
                if gain is None or i >= nt:
                    return
                act.wait_ge(s["eps_done"], 1)
                act.wait_ge(s["summed"], i + 1)
                nc.scalar.activation(std[:, i, :], ss[:, i, :], ACT.Sqrt, scale=heads / D,
                                     bias=eps[:]).then_inc(s["std_done"], 1)

            def copy_o(i):
                for half in range(2):
                    act.wait_ge(s["tp_done"], 2 * i + half + 1)
                    if i >= 2:
                        act.wait_ge(s["mm_done"], 2 * i - 2)
                    nc.scalar.copy(o_t[:, i % 2, 4 * half:4 * half + 4, :],
                                   tp[half][:]).then_inc(s["tp_read"], 1)

            def copy_h(i):
                for half in range(2):
                    act.wait_ge(s["n_tp_done"], 2 * i + half + 1)
                    if router:
                        if i >= 2:
                            act.wait_ge(s["lg_done"], i - 1)
                        dst = h_tile[:, i % 2, 4 * half:4 * half + 4, :]
                    else:
                        dst = h_t[:, 4 * half:4 * half + 4, i * P:(i + 1) * P]
                    nc.scalar.copy(dst, n_tp[half][:]).then_inc(s["n_tp_read"], 1)

            def square_and_root(i):
                act.wait_ge(s["added"], 2 * i + 2)
                if i >= 1:
                    act.wait_ge(s["n_summed"], i)
                nc.scalar.activation(n_sq[:], e["res"][:, tiles[i], :], ACT.Square).then_inc(
                    s["n_sq_done"], 1)
                act.wait_ge(s["eps_done"], 1)
                act.wait_ge(s["n_summed"], i + 1)
                nc.scalar.activation(n_std[:, i:i + 1], n_ss[:, i:i + 1], ACT.Sqrt, scale=1.0 / D,
                                     bias=eps[:]).then_inc(s["n_std_done"], 1)

            square_slices(0)
            root_slices(0)
            square_slices(1)
            copy_o(0)
            root_slices(1)
            square_slices(2)
            root_slices(2)
            for i in range(nt + 1):
                if i + 1 < nt:
                    copy_o(i + 1)
                if i >= 1:
                    copy_h(i - 1)
                if i < nt:
                    square_and_root(i)
                    square_slices(i + 3)
                    root_slices(i + 3)

        @block.vector
        def _(dve):
            link = Chain(dve, s["step"])
            v = nc.vector
            v.memset(eps[:], EPS).then_inc(s["eps_done"], 1)

            def scale_slices(i):
                if gain is None or i >= nt:
                    return
                width = D // heads
                dve.wait_ge(s["sq_done"], i + 1)
                v.tensor_reduce(ss[:, i, :], sq[:].rearrange("p (h d) -> p h d", h=heads), AX.X,
                                ALU.add).then_inc(s["summed"], 1)
                dve.wait_ge(s["summed"], i + 1)
                dve.wait_ge(s["std_done"], i + 1)
                rsqrt_mean(v, link, rstd[:, i, :], std[:, i, :], ss[:, i, :], tmp[:, i, :], heads / D)
                if gain_scale != 1.0:
                    link(v.tensor_scalar(rstd[:, i, :], rstd[:, i, :], gain_scale, None, ALU.mult))
                slices = o[:, i, :].rearrange("p (h d) -> p h d", h=heads)
                link(v.tensor_tensor(slices, slices, inner(rstd[:, i, :], width), ALU.mult))
                if gain.shape[0] == width:
                    op = v.tensor_tensor(slices, slices, middle(g[:, 0:width], heads), ALU.mult)
                else:
                    op = v.tensor_tensor(o[:, i, :], o[:, i, :], g[:], ALU.mult)
                op.then_inc(s["o_done"], 1)

            def add_products(i):
                for c in range(2):
                    j = 2 * i + c
                    cols = slice(c * NCHUNK, (c + 1) * NCHUNK)
                    dst = e["res"][:, tiles[i], cols]
                    dve.wait_ge(s["mm_done"], j + 1)
                    if not gate:
                        v.tensor_tensor(dst, dst, acc[j % 3][:], ALU.add).then_inc(s["added"], 1)
                        continue
                    link(v.tensor_tensor(part[:], acc[j % 3][:], gates[:, side(tiles[i]), cols],
                                         ALU.mult))
                    v.tensor_tensor(dst, dst, part[:], ALU.add).then_inc(s["added"], 1)
                    dve.wait_ge(s["added"], j + 1)

            def normalise_tile(i):
                t = tiles[i]
                dve.wait_ge(s["n_sq_done"], i + 1)
                link(v.tensor_reduce(runs[:], n_sq[:].rearrange("p (a b) -> p a b", b=32), AX.X,
                                     ALU.add))
                v.tensor_reduce(n_ss[:, i:i + 1], runs[:], AX.X, ALU.add).then_inc(s["n_summed"], 1)
                dve.wait_ge(s["n_summed"], i + 1)
                dve.wait_ge(s["n_std_done"], i + 1)
                one = slice(i, i + 1)
                rsqrt_mean(v, link, n_rstd[:, one], n_std[:, one], n_ss[:, one], n_tmp[:, one], 1.0 / D)
                if i >= 2:
                    dve.wait_ge(s["n_tp_done"], 2 * (i - 1))
                    if store is not None:
                        dve.wait_ge(stored[i % 2], 16 * (i // 2))
                out = h[:, i % 2, :]
                if not vecs:
                    v.scalar_tensor_tensor(out, e["res"][:, t, :], n_rstd[:, one], n_g[:], ALU.mult,
                                           ALU.mult).then_inc(s["h_done"], 1)
                    return
                link(v.scalar_tensor_tensor(out, e["res"][:, t, :], n_rstd[:, one],
                                            mul[:, side(t), :], ALU.mult, ALU.mult))
                v.tensor_tensor(out, out, add[:, side(t), :], ALU.add).then_inc(s["h_done"], 1)

            def read_logits(i):
                dve.wait_ge(s["lg_done"], i + 1)
                v.tensor_tensor(logits[:, i, :], lg[:], bias[:], ALU.add).then_inc(s["lg_read"], 1)

            if gain is not None:
                dve.wait_ge(s["g_in"], 16)
            for i in range(3):
                scale_slices(i)
            if vecs:
                dve.wait_ge(s["vec_in"], 16 * len(vecs))
            dve.wait_ge(s["n_vec_in"], 16 * n_norm)
            for x in vecs:
                link(v.scalar_tensor_tensor(mul[:, x, :], mul[:, x, :], 1.0, n_g[:], ALU.add,
                                            ALU.mult))
            for i in range(nt + 1):
                if i < nt:
                    add_products(i)
                    normalise_tile(i)
                if i >= 1 and router:
                    read_logits(i - 1)
                scale_slices(i + 3)

        @block.tensor
        def _(pe):
            def turn_o(i):
                if gain is not None:
                    pe.wait_ge(s["o_done"], i + 1)
                for half in range(2):
                    if i >= 1:
                        pe.wait_ge(s["tp_read"], 2 * i - 1 + half)
                    for q in range(4):
                        k = 4 * half + q
                        tr = nc.tensor.transpose(tp[half][:, q, :], o[:, i, k * P:(k + 1) * P],
                                                 e["ident"][:])
                    tr.then_inc(s["tp_done"], 1)

            def products(i):
                pe.wait_ge(s["tp_read"], 2 * i + 2)
                for c in range(2):
                    j = 2 * i + c
                    if j >= 3:
                        pe.wait_ge(s["added"], j - 2)
                    for k in range(KD):
                        if i == 0 and k % 4 == 0:
                            pe.wait_ge(loaded[2 * c + k // 4], 16)
                        mm = nc.tensor.matmul(acc[j % 3][:], o_t[:, i % 2, k, :], w[:, c, k, :],
                                              start=(k == 0), stop=(k == KD - 1))
                    mm.then_inc(s["mm_done"], 1)

            def turn_h(i):
                pe.wait_ge(s["h_done"], i + 1)
                for half in range(2):
                    if i >= 1:
                        pe.wait_ge(s["n_tp_read"], 2 * i - 1 + half)
                    for q in range(4):
                        k = 4 * half + q
                        tr = nc.tensor.transpose(n_tp[half][:, q, :], h[:, i % 2, k * P:(k + 1) * P],
                                                 e["ident"][:])
                    tr.then_inc(s["n_tp_done"], 1)

            def route_tile(i):
                if i == 0:
                    pe.wait_ge(s["n_vec_in"], 16 * n_norm)
                else:
                    pe.wait_ge(s["lg_read"], i)
                pe.wait_ge(s["n_tp_read"], 2 * i + 2)
                for k in range(KD):
                    mm = nc.tensor.matmul(lg[:], h_tile[:, i % 2, k, :], wr[:, k, :],
                                          start=(k == 0), stop=(k == KD - 1))
                mm.then_inc(s["lg_done"], 1)

            turn_o(0)
            for i in range(nt + 1):
                if i < nt:
                    products(i)
                if i + 1 < nt:
                    turn_o(i + 1)
                if i >= 1:
                    turn_h(i - 1)
                    if router:
                        route_tile(i - 1)


def max_blocks(nt):
    n = NE + 2 * nt
    return n + n % 2


def route(nc, e, layer, tiles, logits, r):
    nt = len(tiles)
    nb = max_blocks(nt)
    with Phase(nc, f"route{layer}") as ph:
        before = ph.sb("before", [P, P])
        iota = ph.sb("iota", [P, P])
        rowid = ph.sb("rowid", [P, 3, NT])
        gate_t = ph.sb("gate_t", [P, nt, NG])
        tg = ph.sb("tg", [P, nt, NG])
        hot_g = ph.sb("hot_g", [P, nt, NG])
        le = ph.sb("le", [P, nt, NE])
        te = ph.sb("te", [P, nt, NE])
        hot = ph.sb("hot", [P, 2, nt, NE])
        both = ph.sb("both", [P, nt + 1, NE])
        sums = ph.sb("sums", [P, nt + 1, NE])
        small = ph.sb("small", [P, 12, nt])
        place = ph.sb("place", [P, nt, NE])
        cnt = ph.sb("cnt", [P, NE])
        blocks = ph.sb("blocks", [P, NE])
        end = [ph.sb(f"end{i}", [P, NE]) for i in range(2)]
        dest = ph.sb("dest", [P, 2, nt])
        dest_i = ph.sb("dest_i", [P, 2, 2, nt], I32)
        dest_f = ph.sb("dest_f", [P, 2, 2, nt])
        lane = ph.sb("lane", [P, 2, nt, P])
        in_block = ph.sb("in_block", [P, 2, nt, nb])
        what = ph.sb("what", [P, 2, 2, nt, nb])
        past = ph.sb("past", [1, nb, NE])
        expert_f = ph.sb("expert_f", [1, nb])
        where, slots = ph.ps("where", [P, nt + 1, NE]), ph.ps("slots", [P, 2, nb])
        names = "const_in gexp_in gexp_done wexp_in wexp_done hot_done where_done tables_in slots_done step fill"
        s = {x: ph.sem(x) for x in names.split()}
        block = ph.block()

        @block.sync
        def _(sp):
            loads = [
                (before[:], e["c_before"]), (iota[:], e["c_iota"]), (rowid[:], e["c_rowid"]),
            ]
            for dst, src in loads:
                sp.dma_start(dst, src).then_inc(s["const_in"], 16)

        @block.tensor
        def _(pe):
            pe.wait_ge(s["const_in"], 16 * 3)
            pe.wait_ge(s["hot_done"], nt + 3)
            nc.tensor.matmul(where[:], before[:], both[:], start=True, stop=False)
            nc.tensor.matmul(where[:], e["ones"][:], sums[:], start=False, stop=True).then_inc(
                s["where_done"], 1)
            pe.wait_ge(s["tables_in"], 1)
            for j in range(2 * nt):
                a, i = j // nt, j % nt
                mm = nc.tensor.matmul(slots[:], lane[:, a, i, :], what[:, :, a, i, :],
                                      start=(j == 0), stop=(j == 2 * nt - 1))
            mm.then_inc(s["slots_done"], 1)

        @block.scalar
        def _(act):
            act.wait_ge(s["gexp_in"], 1)
            nc.scalar.activation(tg[:], tg[:], ACT.Exp).then_inc(s["gexp_done"], 1)
            act.wait_ge(s["wexp_in"], 1)
            nc.scalar.activation(small[:, 5, :], small[:, 5, :], ACT.Exp).then_inc(s["wexp_done"], 1)

        @block.vector
        def _(dve):
            v = nc.vector
            link = Chain(dve, s["step"])
            dve.wait_ge(s["const_in"], 16 * 3)
            row = lambda j: small[:, j, :]

            def first_max(hot_out, values, scratch, n, best):
                link(v.tensor_reduce(best, values, AX.X, ALU.max))
                link(v.tensor_tensor(scratch, values, inner(best, n), ALU.is_equal))
                link(v.scalar_tensor_tensor(scratch, middle(iota[:, 0:n], nt), float(n), scratch,
                                            ALU.subtract, ALU.mult))
                link(v.tensor_reduce(row(9), scratch, AX.X, ALU.min))
                link(v.tensor_scalar(row(9), row(9), float(n), None, ALU.add))
                link(v.tensor_tensor(hot_out, middle(iota[:, 0:n], nt), inner(row(9), n),
                                     ALU.is_equal))

            lg, lge = logits[:, :, 0:NG], logits[:, :, NG:]
            first_max(hot_g[:], lg, gate_t[:], NG, row(0))
            v.tensor_tensor(tg[:], lg, inner(row(0), NG), ALU.subtract).then_inc(s["gexp_in"], 1)
            dve.wait_ge(s["gexp_done"], 1)
            link(v.tensor_reduce(row(1), tg[:], AX.X, ALU.add))
            link(v.reciprocal(row(1), row(1)))
            for g in range(NG):
                sl = slice(g * EPG, (g + 1) * EPG)
                oh = hot_g[:, :, g]
                link(v.tensor_tensor(le[:, :, sl], lge[:, :, sl], inner(oh, EPG), ALU.mult))
                link(v.tensor_scalar(row(2), oh, -1.0, -NEG, ALU.add, ALU.mult))
                link(v.tensor_tensor(le[:, :, sl], le[:, :, sl], inner(row(2), EPG), ALU.add))
            first_max(hot[:, 0, :, :], le[:], te[:], NE, row(3))
            link(v.scalar_tensor_tensor(le[:], hot[:, 0, :, :], 2 * NEG, le[:], ALU.mult, ALU.add))
            first_max(hot[:, 1, :, :], le[:], te[:], NE, row(4))
            v.tensor_tensor(row(5), row(4), row(3), ALU.subtract).then_inc(s["wexp_in"], 1)
            v.tensor_tensor(both[:, 0:nt, :], hot[:, 0, :, :], hot[:, 1, :, :], ALU.add).then_inc(
                s["hot_done"], 1)
            v.memset(both[:, nt, :], 0.0).then_inc(s["hot_done"], 1)
            v.memset(sums[:, 0, :], 0.0).then_inc(s["hot_done"], 1)
            for i in range(nt):
                dve.wait_ge(s["hot_done"], 3 + i)
                v.tensor_tensor(sums[:, i + 1, :], sums[:, i, :], both[:, i, :], ALU.add).then_inc(
                    s["hot_done"], 1)
            dve.wait_ge(s["wexp_done"], 1)
            link(v.tensor_scalar(row(6), row(5), 1.0, None, ALU.add))
            link(v.reciprocal(row(6), row(6)))
            link(v.tensor_tensor(r["weight"][:, 0, 0:nt], row(6), row(1), ALU.mult))
            link(v.tensor_tensor(r["weight"][:, 1, 0:nt], r["weight"][:, 0, 0:nt], row(5), ALU.mult))
            dve.wait_ge(s["where_done"], 1)
            link(v.tensor_copy(cnt[:], where[:, nt, :]))
            link(v.tensor_scalar(blocks[:], cnt[:], 0.0, None, ALU.is_gt))
            for k in range(1, nt):
                link(v.scalar_tensor_tensor(blocks[:], cnt[:], float(k * P), blocks[:], ALU.is_gt,
                                            ALU.add))
            link(v.tensor_copy(end[0][:], blocks[:]))
            a = 0
            for k in (1, 2, 4, 8, 16):
                link(v.tensor_copy(end[1 - a][:, 0:k], end[a][:, 0:k]))
                link(v.tensor_tensor(end[1 - a][:, k:], end[a][:, k:], end[a][:, 0:NE - k], ALU.add))
                a = 1 - a
            last = end[a]
            link(v.tensor_tensor(cnt[:], last[:], blocks[:], ALU.subtract))
            link(v.tensor_scalar(cnt[:], cnt[:], float(P), None, ALU.mult))
            link(v.tensor_tensor(place[:], where[:, 0:nt, :], middle(cnt[:], nt), ALU.add))
            for a in range(2):
                link(v.tensor_tensor(te[:], place[:], hot[:, a, :, :], ALU.mult))
                link(v.tensor_reduce(dest[:, a, :], te[:], AX.X, ALU.add))
            link(v.tensor_copy(dest_i[:, 0, :, :], dest[:]))
            link(v.tensor_copy(dest_i[:, 1, :, :], dest[:]))
            link(v.tensor_single_scalar(dest_i[:, 0, :, :], dest_i[:, 0, :, :], P - 1,
                                        ALU.bitwise_and))
            link(v.tensor_single_scalar(dest_i[:, 1, :, :], dest_i[:, 1, :, :], 7,
                                        ALU.arith_shift_right))
            link(v.tensor_copy(dest_f[:], dest_i[:]))
            v.tensor_tensor(lane[:], iota[:].unsqueeze(1).unsqueeze(1).broadcast_to([P, 2, nt, P]),
                            over(dest_f[:, 0], P), ALU.is_equal).then_inc(s["fill"], 1)
            link(v.tensor_tensor(in_block[:],
                                 iota[:, 0:nb].unsqueeze(1).unsqueeze(1).broadcast_to([P, 2, nt, nb]),
                                 over(dest_f[:, 1], nb), ALU.is_equal))
            for z in range(2):
                ids = rowid[:, z:z + 2, tiles[0]:tiles[0] + nt]
                v.tensor_tensor(what[:, z], in_block[:], over(ids, nb), ALU.mult).then_inc(
                    s["fill"], 1)
            dve.wait_ge(s["fill"], 3)
            dve.sem_inc(s["tables_in"], 1)
            link(v.tensor_tensor(past[:], middle(last[0:1, :], nb), inner(iota[0:1, 0:nb], NE),
                                 ALU.is_le))
            link(v.tensor_reduce(expert_f[:], past[:], AX.X, ALU.add))
            link(v.tensor_scalar(expert_f[:], expert_f[:], float(NE - 1), None, ALU.min))
            link(v.tensor_copy(r["expert"][:, 0:nb], expert_f[:]))
            link(v.tensor_copy(r["count"][:], last[0:1, NE - 1:NE]))
            dve.wait_ge(s["slots_done"], 1)
            link(v.tensor_scalar(r["index"][:, :, 0:nb], slots[:], BIG, None, ALU.add))
            link(v.memset(r["index"][:, :, nb:], int(BIG)))


def experts(nc, e, layer, nt, r):
    nb = max_blocks(nt)
    with Phase(nc, f"moe{layer}") as ph:
        wg = [ph.sb(f"wg{b}", [P, KD, FE]) for b in range(2)]
        wu = [ph.sb(f"wu{b}", [P, KD, FE]) for b in range(2)]
        wd = [ph.sb(f"wd{b}", [P, FE // P, D]) for b in range(2)]
        xg = [ph.sb(f"xg{b}", [P, D]) for b in range(2)]
        xg_t = [ph.sb(f"xg_t{b}", [P, KD, P]) for b in range(2)]
        x_idx = [ph.sb(f"x_idx{b}", [P, 1], I32) for b in range(2)]
        y_idx = [ph.sb(f"y_idx{b}", [P, 1], I32) for b in range(2)]
        sig = ph.sb("sig", [P, FE])
        hid = ph.sb("hid", [P, FE])
        hid_t = ph.sb("hid_t", [P, FE // P, P])
        y = [ph.sb(f"y{b}", [P, D]) for b in range(2)]
        tp = [ph.ps(f"tp{i}", [P, 4, P]) for i in range(2)]
        HF = FE // 2
        gate = [ph.ps(f"gate{f}", [P, HF]) for f in range(2)]
        up = [ph.ps(f"up{f}", [P, HF]) for f in range(2)]
        down = [ph.ps(f"down{i}", [P, NCHUNK]) for i in range(2)]
        names = ("y_free cleared idx_done turned_x read_x gated upped expd hid_done issue indexed landed fetched "
                 "turned_h read_h downed y_done step")
        s = {x: ph.sem(x) for x in names.split()}
        gu_in = [ph.sem(f"gu_in{b}") for b in range(2)]
        d_in = [ph.sem(f"d_in{b}") for b in range(2)]
        x_in = [nc.alloc_semaphore(f"moe{layer}_x_in{b}") for b in range(2)]
        y_out = [nc.alloc_semaphore(f"moe{layer}_y_out{b}") for b in range(2)]
        block = ph.block()
        view_g = e["moe_w_gate"][layer].rearrange("x (p k) n -> x p k n", k=KD)
        view_u = e["moe_w_up"][layer].rearrange("x (p k) n -> x p k n", k=KD)
        view_d = e["moe_w_down"][layer].rearrange("x (k p) n -> x p k n", p=P)

        def count_of(eng):
            return eng.value_load(r["count"][0:1, 0:1], min_val=0, max_val=nb)

        @block.sync
        def _(sp):
            n = count_of(sp)
            with sp.Fori(0, nb // 2) as i2:
                for b in range(2):
                    i = 2 * i2 + b
                    with sp.If(i < n):
                        x = sp.value_load(r["expert"][0:1, bass.ds(i, 1)], min_val=0, max_val=NE - 1)
                        sp.wait_ge(s["upped"], 2 * i + 2)
                        sp.sem_inc(s["issue"], 1)
                        sp.wait_ge(s["fetched"], 1)
                        sp.dma_start(wg[b][:], view_g[bass.ds(x, 1)].rearrange(
                            "o p k n -> (o p) k n")).then_inc(gu_in[b], 16)
                        sp.dma_start(wu[b][:], view_u[bass.ds(x, 1)].rearrange(
                            "o p k n -> (o p) k n")).then_inc(gu_in[b], 16)
                        sp.wait_ge(s["downed"], i + 1)
                        sp.sem_inc(s["issue"], 1)
                        sp.dma_start(wd[b][:], view_d[bass.ds(x, 1)].rearrange(
                            "o p k n -> (o p) k n")).then_inc(d_in[b], 16)

        @block.gpsimd
        def _(pool):
            n = count_of(pool)
            last_token = pool.to_reg(NT * P - 1)
            last_result = pool.to_reg(2 * NT * P - 1)

            def fetch(b, i):
                nc.gpsimd.tensor_copy(x_idx[b][:], r["index"][:, 0, bass.ds(i, 1)]).then_inc(
                    s["idx_done"], 1)

            def gather(b):
                nc.gpsimd.indirect_dma_start(
                    xg[b][:], None, e["h_dram"],
                    bass.IndirectOffsetOnAxis(ap=x_idx[b][:], axis=0),
                    bounds_check=last_token, oob_is_err=False).then_inc(x_in[b], 16)

            for b in range(2):
                nc.gpsimd.memset(xg[b][:], 0.0).then_inc(s["cleared"], 1)
                pool.wait_ge(s["cleared"], b + 1)
                fetch(b, b)
                pool.wait_ge(s["idx_done"], b + 1)
                pool.sem_inc(s["indexed"], 1)
                gather(b)
                pool.sem_inc(s["fetched"], 1)
            with pool.Fori(0, nb // 2) as i2:
                for b in range(2):
                    i = 2 * i2 + b
                    with pool.If(i < n):
                        pool.wait_ge(s["turned_x"], 2 * i + 2)
                        fetch(b, i + 2)
                        pool.wait_ge(s["idx_done"], 2 * i + 3)
                        pool.sem_inc(s["indexed"], 1)
                        gather(b)
                        nc.gpsimd.tensor_copy(y_idx[b][:], r["index"][:, 1, bass.ds(i, 1)]).then_inc(
                            s["idx_done"], 1)
                        pool.wait_ge(s["idx_done"], 2 * i + 4)
                        pool.wait_ge(s["y_done"], 2 * i + 3)
                        pool.sem_inc(s["indexed"], 1)
                        nc.gpsimd.indirect_dma_start(
                            e["y_dram"], bass.IndirectOffsetOnAxis(ap=y_idx[b][:], axis=0),
                            y[b][:], None, bounds_check=last_result,
                            oob_is_err=False).then_inc(y_out[b], 16)
                        if b == 0:
                            with pool.If(i2 > 0):
                                pool.wait_ge(y_out[1], 16 * i2)
                                pool.sem_inc(s["landed"], 1)
                        else:
                            pool.wait_ge(y_out[0], 16 * (i2 + 1))
                        pool.sem_inc(s["y_free"], 1)
            pool.wait_ge(y_out[0], 16 * ((n + 1) // 2))
            pool.sem_inc(s["landed"], 1)
            with pool.If(n > 1):
                pool.wait_ge(y_out[1], 16 * (n // 2))
                pool.sem_inc(s["landed"], 1)
            pool.wait_ge(x_in[0], 16 * ((n + 1) // 2) + 16)
            pool.wait_ge(x_in[1], 16 * (n // 2) + 16)
            pool.sem_inc(s["landed"], 1)

        @block.tensor
        def _(pe):
            n = count_of(pe)
            pe.sem_inc(s["downed"], 2)
            pe.sem_inc(s["upped"], 4)

            def turn_x(b, half):
                for q in range(4):
                    tr = nc.tensor.transpose(tp[half][:, q, :], xg[b][:, 4 * half + q:D:KD],
                                             e["ident"][:])
                tr.then_inc(s["turned_x"], 1)

            pe.wait_ge(x_in[0], 16)
            turn_x(0, 0)
            turn_x(0, 1)
            with pe.Fori(0, nb // 2) as i2:
                for b in range(2):
                    i = 2 * i2 + b
                    with pe.If(i < n):
                        pe.wait_ge(gu_in[b], 32 * (i2 + 1))
                        pe.wait_ge(s["read_x"], 2 * i + 2)
                        pe.wait_ge(s["hid_done"], 2 * i + 1)

                        def up_or_gate(acc, w, f, done):
                            for k in range(KD):
                                mm = nc.tensor.matmul(acc[f][:], xg_t[b][:, k, :],
                                                      w[b][:, k, f * HF:(f + 1) * HF],
                                                      start=(k == 0), stop=(k == KD - 1))
                            mm.then_inc(done, 1)

                        def turn_hidden(f):
                            pe.wait_ge(s["hid_done"], 2 * i + f + 2)
                            for k in (2 * f, 2 * f + 1):
                                tr = nc.tensor.transpose(tp[f][:, k % 2, :],
                                                         hid[:, k * P:(k + 1) * P], e["ident"][:])
                            tr.then_inc(s["turned_h"], 1)

                        def down_half(f):
                            for c in range(2):
                                for k in (2 * f, 2 * f + 1):
                                    mm = nc.tensor.matmul(
                                        down[c][:], hid_t[:, k, :],
                                        wd[b][:, k, c * NCHUNK:(c + 1) * NCHUNK],
                                        start=(k == 0), stop=(k == 3), skip_group_check=True)
                            return mm

                        up_or_gate(gate, wg, 0, s["gated"])
                        up_or_gate(up, wu, 0, s["upped"])
                        up_or_gate(gate, wg, 1, s["gated"])
                        turn_hidden(0)
                        up_or_gate(up, wu, 1, s["upped"])
                        pe.wait_ge(d_in[b], 16 * (i2 + 1))
                        pe.wait_ge(s["y_done"], 2 * i + 1)
                        pe.wait_ge(s["read_h"], 2 * i + 1)
                        down_half(0)
                        turn_hidden(1)
                        pe.wait_ge(x_in[1 - b], 16 * (i2 + 1 + b))
                        turn_x(1 - b, 0)
                        pe.wait_ge(s["read_h"], 2 * i + 2)
                        turn_x(1 - b, 1)
                        down_half(1).then_inc(s["downed"], 1)

        @block.scalar
        def _(act):
            n = count_of(act)

            def read_x(b, i):
                for half in range(2):
                    act.wait_ge(s["turned_x"], 2 * i + 1 + half)
                    nc.scalar.copy(xg_t[b][:, 4 * half:4 * half + 4, :], tp[half][:]).then_inc(
                        s["read_x"], 1)

            read_x(0, 0)
            with act.Fori(0, nb // 2) as i2:
                for b in range(2):
                    i = 2 * i2 + b
                    with act.If(i < n):
                        act.wait_ge(s["hid_done"], 2 * i + 1)
                        for f in range(2):
                            act.wait_ge(s["gated"], 2 * i + f + 1)
                            nc.scalar.activation(sig[:, f * HF:(f + 1) * HF], gate[f][:], ACT.Exp,
                                                 scale=-1.0).then_inc(s["expd"], 1)
                            act.wait_ge(s["turned_h"], 2 * i + f + 1)
                            nc.scalar.copy(hid_t[:, 2 * f:2 * f + 2, :],
                                           tp[f][:, 0:2, :]).then_inc(s["read_h"], 1)
                        read_x(1 - b, i + 1)

        @block.vector
        def _(dve):
            n = count_of(dve)
            dve.sem_inc(s["y_free"], 1)
            dve.sem_inc(s["hid_done"], 1)
            dve.sem_inc(s["y_done"], 1)
            with dve.Fori(0, nb // 2) as i2:
                for b in range(2):
                    i = 2 * i2 + b
                    with dve.If(i < n):
                        for f in range(2):
                            half = sig[:, f * HF:(f + 1) * HF]
                            at = 6 * i + 3 * f
                            dve.wait_ge(s["expd"], 2 * i + f + 1)
                            nc.vector.tensor_scalar(half, half, 1.0, None, ALU.add).then_inc(
                                s["step"], 1)
                            dve.wait_ge(s["step"], at + 1)
                            nc.vector.reciprocal(half, half).then_inc(s["step"], 1)
                            dve.wait_ge(s["step"], at + 2)
                            nc.vector.tensor_tensor(half, half, gate[f][:], ALU.mult).then_inc(
                                s["step"], 1)
                            dve.wait_ge(s["step"], at + 3)
                            dve.wait_ge(s["upped"], 2 * i + f + 5)
                            nc.vector.tensor_tensor(hid[:, f * HF:(f + 1) * HF], half, up[f][:],
                                                    ALU.mult).then_inc(s["hid_done"], 1)
                        dve.wait_ge(s["downed"], i + 3)
                        dve.wait_ge(s["y_free"], i + 1)
                        for c in range(2):
                            nc.vector.tensor_copy(y[b][:, c * NCHUNK:(c + 1) * NCHUNK],
                                                  down[c][:]).then_inc(s["y_done"], 1)


def mod_part(e, layer, part):
    return lambda v: e["mod_dram"][v, (layer * 6 + part) * D:(layer * 6 + part + 1) * D]


def norm_vectors(e, layer, part):
    return lambda v: (mod_part(e, layer, part)(v), mod_part(e, layer, part + 1)(v))


def routing_tables(nc, stack, layer, nt):
    nb = max_blocks(nt)
    new = lambda name, shape, dt: stack.enter_context(nc.sbuf_tensor(f"r_{name}{layer}", shape, dt))
    return dict(index=new("index", [P, 2, nb + 2], I32), expert=new("expert", [1, nb], I32),
                count=new("count", [1, 1], I32), weight=new("weight", [P, 2, NT], F32))


def layer_0(nc, e, stack):
    tiles = list(range(NT))
    sb = nc.sbuf_tensor
    r, logits_scope = routing_tables(nc, stack, 0, NT), ExitStack()
    logits = logits_scope.enter_context(sb("a_logits", [P, NT, NG + NE], F32))
    with sb("a_buffer", [P, NT * D], F32) as buffer:
        h_t = buffer[:].rearrange("p (k n) -> p k n", k=KD)
        o = buffer[:].rearrange("p (t d) -> p t d", t=NT)
        normalise_first(nc, e, "norm1_0", tiles, e["norm1_g"][0], norm_vectors(e, 0, 0), e["rstd"], h_t)
        with sb("a_q", [P, 8, NT * P], F32) as q_t, sb("a_k", [P, 2, 8, NT * P], F32) as k_t, \
                sb("a_v", [P, NT, D], F32) as v:

            def stores(c, t):
                if c >= 4:
                    return v[:, t, (c - 4) * NCHUNK:(c - 3) * NCHUNK]
                slots, cols = slice(4 * (c % 2), 4 * (c % 2) + 4), slice(t * P, (t + 1) * P)
                if c < 2:
                    return [(slice(0, P), q_t[:, slots, cols])], 0.125
                return [(rows, k_t[rows, side, slots, cols]) for side, rows in enumerate(HALVES)], 1.0

            items = [(c, t, "value" if c >= 4 else "rope" if t >= TC else "plain")
                     for c in range(6) for t in tiles]
            project_heads(nc, e, "qkv0", h_t, e["a_w_qkv"][0], items, stores, k_t)
            diff_attention(nc, e, q_t, k_t, v, o)
        project_out(nc, e, "out0", o, tiles, 8, e["a_subln_g"][0], 1.0 - LAM_INIT, e["a_w_o"][0],
                    mod_part(e, 0, 2), e["norm2_g"][0], norm_vectors(e, 0, 3), store=e["h_dram"],
                    router=(0, logits))
    route(nc, e, 0, tiles, logits, r)
    logits_scope.close()
    experts(nc, e, 0, NT, r)
    return r


def enter_layer_1(nc, e, r, h_t, q_t, k_t, v_t):
    tiles = [*range(TC, NT), *range(TC)]
    items = [(i, c) for i, t in enumerate(tiles) for c in ([0, 1, 2] if t >= TC else [2])]
    first = [next(j for j, it in enumerate(items) if it[0] == i) for i in range(NT)] + [len(items)]
    side = lambda t: 0 if t >= TC else 1
    reads = [0]
    for _, c in items:
        reads.append(reads[-1] + (2 if c == 2 else 1))
    with Phase(nc, "qkv1") as ph:
        w = ph.sb("w", [P, 3, KD, NCHUNK])
        rope = ph.sb("rope", [P, 2, TX, HD])
        stage = ph.sb("stage", [P, 3, 8, HD])
        rope_tmp = ph.sb("rope_tmp", [P, 8, HD])
        ys = ph.sb("ys", [P, 2, D])
        gates, mul, add = (ph.sb(x, [P, 2, D]) for x in ("gates", "mul", "add"))
        g, h, sq = (ph.sb(x, [P, D]) for x in ("g", "h", "sq"))
        runs, eps = ph.sb("runs", [P, 32]), ph.sb("eps", [P, 1])
        ss, std, rstd, tmp = (ph.sb(x, [P, NT]) for x in ("ss", "std", "rstd", "tmp"))
        acc = [ph.ps(f"acc{i}", [P, NCHUNK]) for i in range(3)]
        tp = [ph.ps(f"tp{i}", [P, 4, P]) for i in range(2)]
        n_tp = [ph.ps(f"n_tp{i}", [P, 4, P]) for i in range(2)]
        names = ("gates_in vec_in rope_in y_in combined sq_done summed std_done eps_done h_done n_tp_done "
                 "n_tp_read mm_done acc_read tp_done tp_read zeroed step")
        s = {x: ph.sem(x) for x in names.split()}
        loaded = [ph.sem(f"loaded{i}") for i in range(3)]
        block = ph.block()

        @block.sync
        def _(sp):
            src = e["y_dram"].rearrange("(a t p) d -> t p a d", a=2, p=P)
            sp.dma_start(ys[:], src[tiles[0]]).then_inc(s["y_in"], 16)
            for x in range(2):
                sp.dma_start(gates[:, x, :], bcast_rows(mod_part(e, 0, 5)(x))).then_inc(
                    s["gates_in"], 16)
            sp.dma_start(g[:], bcast_rows(e["norm1_g"][1])).then_inc(s["vec_in"], 16)
            for x in range(2):
                shift, scale = norm_vectors(e, 1, 0)(x)
                sp.dma_start(add[:, x, :], bcast_rows(shift)).then_inc(s["vec_in"], 16)
                sp.dma_start(mul[:, x, :], bcast_rows(scale)).then_inc(s["vec_in"], 16)
            view = e["b_w_qkv"][0].rearrange("(k p) n -> p k n", p=P)
            for c in range(3):
                sp.dma_start(w[:, c], view[:, :, c * NCHUNK:(c + 1) * NCHUNK]).then_inc(loaded[c], 16)
            sp.dma_start(rope[:], e["c_axial"].rearrange("s (t p) d -> p s t d", p=P)).then_inc(
                s["rope_in"], 16)
            for i in range(1, NT):
                sp.wait_ge(s["combined"], i)
                sp.dma_start(ys[:], src[tiles[i]]).then_inc(s["y_in"], 16)

        @block.gpsimd
        def _(pool):
            for half in range(2):
                nc.gpsimd.memset(k_t[HALVES[1 - half], half], 0.0).then_inc(s["zeroed"], 1)
                pool.wait_ge(s["zeroed"], half + 1)

        @block.scalar
        def _(act):
            def square_and_root(i):
                act.wait_ge(s["combined"], i + 1)
                if i >= 1:
                    act.wait_ge(s["summed"], i)
                nc.scalar.activation(sq[:], e["res"][:, tiles[i], :], ACT.Square).then_inc(
                    s["sq_done"], 1)
                act.wait_ge(s["summed"], i + 1)
                nc.scalar.activation(std[:, i:i + 1], ss[:, i:i + 1], ACT.Sqrt, scale=1.0 / D,
                                     bias=eps[:]).then_inc(s["std_done"], 1)

            def copy_h(i):
                t = tiles[i]
                for half in range(2):
                    act.wait_ge(s["n_tp_done"], 2 * i + half + 1)
                    nc.scalar.copy(h_t[:, 4 * half:4 * half + 4, t * P:(t + 1) * P],
                                   n_tp[half][:]).then_inc(s["n_tp_read"], 1)

            def copy_heads(j):
                i, c = items[j]
                t = tiles[i]
                act.wait_ge(s["tp_done"], j + 1)
                if c == 2:
                    for half, rows in enumerate(HALVES):
                        nc.scalar.copy(k_t[rows, half, :, t * P:(t + 1) * P],
                                       tp[j % 2][rows]).then_inc(s["tp_read"], 1)
                else:
                    cols = slice((t - TC) * P, (t - TC + 1) * P)
                    nc.scalar.activation(q_t[:, 4 * c:4 * c + 4, cols], tp[j % 2][:], ACT.Copy,
                                         scale=0.125).then_inc(s["tp_read"], 1)

            act.wait_ge(s["eps_done"], 1)
            square_and_root(0)
            copy_h(0)
            for j in range(len(items) + 1):
                i = items[j][0] if j < len(items) else NT
                last = j < len(items) and j == first[i + 1] - 1
                if i + 1 < NT and j == min(first[i] + 1, first[i + 1] - 1):
                    square_and_root(i + 1)
                if last and i + 1 < NT:
                    copy_h(i + 1)
                if j >= 1:
                    copy_heads(j - 1)

        @block.vector
        def _(dve):
            v = nc.vector
            link = Chain(dve, s["step"])
            v.memset(eps[:], EPS).then_inc(s["eps_done"], 1)

            def combine(i):
                t = tiles[i]
                res, a, b = e["res"][:, t, :], ys[:, 0, :], ys[:, 1, :]
                dve.wait_ge(s["y_in"], 16 * (i + 1))
                link(v.tensor_scalar(a, a, r["weight"][:, 0, t:t + 1], None, ALU.mult))
                link(v.scalar_tensor_tensor(a, b, r["weight"][:, 1, t:t + 1], a, ALU.mult, ALU.add))
                link(v.tensor_tensor(a, a, gates[:, side(t), :], ALU.mult))
                v.tensor_tensor(res, res, a, ALU.add).then_inc(s["combined"], 1)

            def norm(i):
                t, one = tiles[i], slice(i, i + 1)
                dve.wait_ge(s["sq_done"], i + 1)
                link(v.tensor_reduce(runs[:], sq[:].rearrange("p (a b) -> p a b", b=32), AX.X,
                                     ALU.add))
                v.tensor_reduce(ss[:, one], runs[:], AX.X, ALU.add).then_inc(s["summed"], 1)
                dve.wait_ge(s["summed"], i + 1)
                dve.wait_ge(s["std_done"], i + 1)
                rsqrt_mean(v, link, rstd[:, one], std[:, one], ss[:, one], tmp[:, one], 1.0 / D)
                if i == 0:
                    dve.wait_ge(s["vec_in"], 16 * 5)
                    for x in range(2):
                        link(v.scalar_tensor_tensor(mul[:, x, :], mul[:, x, :], 1.0, g[:], ALU.add,
                                                    ALU.mult))
                else:
                    dve.wait_ge(s["n_tp_done"], 2 * i)
                link(v.scalar_tensor_tensor(h[:], e["res"][:, t, :], rstd[:, one],
                                            mul[:, side(t), :], ALU.mult, ALU.mult))
                v.tensor_tensor(h[:], h[:], add[:, side(t), :], ALU.add).then_inc(s["h_done"], 1)

            def rotate(j):
                i, c = items[j]
                t = tiles[i]
                dve.wait_ge(s["mm_done"], j + 1)
                if j >= 3:
                    dve.wait_ge(s["tp_done"], j - 2)
                dst = stage[:, j % 3, :, :]
                src = acc[j % 3][:].rearrange("p (h d) -> p h d", d=HD)
                if t >= TC:
                    cos, sin = rope[:, 0, t - TC, :], rope[:, 1, t - TC, :]
                if c < 2:
                    rope_heads(dve, nc, link, dst, src, rope_tmp[:], cos, sin, 16).then_inc(
                        s["acc_read"], 1)
                    return
                twice = dst.rearrange("p (g c) d -> p g c d", c=2)
                one, keys = twice[:, :, 0, :], src[:, 0:4, :]
                if t < TC:
                    link(v.tensor_copy(one, keys))
                else:
                    link(rope_heads(dve, nc, link, one, keys, rope_tmp[:, 0:4, :], cos, sin, 16))
                link(v.tensor_copy(twice[:, :, 1, :], one))
                v.tensor_copy(v_t[:, t, :], acc[j % 3][:, 4 * HD:8 * HD]).then_inc(s["acc_read"], 1)

            dve.wait_ge(s["gates_in"], 32)
            combine(0)
            norm(0)
            dve.wait_ge(s["rope_in"], 16)
            for i in range(NT):
                mine = list(range(first[i], first[i + 1]))
                if len(mine) > 1:
                    rotate(mine[0])
                if i + 1 < NT:
                    combine(i + 1)
                    norm(i + 1)
                for j in (mine[1:] if len(mine) > 1 else mine):
                    rotate(j)

        @block.tensor
        def _(pe):
            def turn_h(i):
                pe.wait_ge(s["h_done"], i + 1)
                for half in range(2):
                    if i >= 1:
                        pe.wait_ge(s["n_tp_read"], 2 * i - 1 + half)
                    for q in range(4):
                        k = 4 * half + q
                        tr = nc.tensor.transpose(n_tp[half][:, q, :], h[:, k * P:(k + 1) * P],
                                                 e["ident"][:])
                    tr.then_inc(s["n_tp_done"], 1)

            def turn_heads_of(j):
                pe.wait_ge(s["acc_read"], j + 1)
                if j >= 2:
                    pe.wait_ge(s["tp_read"], reads[j - 1])
                for q in range(4):
                    tr = nc.tensor.transpose(
                        tp[j % 2][:, q, :],
                        stage[:, j % 3, 2 * q:2 * q + 2, :].rearrange("p a d -> p (a d)"),
                        e["ident"][:])
                tr.then_inc(s["tp_done"], 1)

            turn_h(0)
            for j, (i, c) in enumerate(items):
                t = tiles[i]
                if i == 0:
                    pe.wait_ge(loaded[c], 16)
                if j == first[i]:
                    pe.wait_ge(s["n_tp_read"], 2 * i + 2)
                if j >= 3:
                    pe.wait_ge(s["acc_read"], j - 2)
                for k in range(KD):
                    mm = nc.tensor.matmul(acc[j % 3][:], h_t[:, k, t * P:(t + 1) * P], w[:, c, k, :],
                                          start=(k == 0), stop=(k == KD - 1))
                mm.then_inc(s["mm_done"], 1)
                if j == first[i + 1] - 1 and i + 1 < NT:
                    turn_h(i + 1)
                if j >= 1:
                    turn_heads_of(j - 1)
            turn_heads_of(len(items) - 1)


def layer_1(nc, e, stack, last_r):
    stream = list(range(TC, NT))
    sb = nc.sbuf_tensor
    r, logits_scope = routing_tables(nc, stack, 1, TX), ExitStack()
    logits = logits_scope.enter_context(sb("b_logits", [P, TX, NG + NE], F32))
    with sb("b_buffer", [P, NT * D], F32) as buffer:
        h_t = buffer[:].rearrange("p (k n) -> p k n", k=KD)
        o = buffer[:, 0:TX * D].rearrange("p (t d) -> p t d", t=TX)
        with sb("b_q", [P, 8, SEQ], F32) as q_t, sb("b_k", [P, 2, 4, NT * P], F32) as k_t, \
                sb("b_v", [P, NT, 4 * HD], F32) as v:
            enter_layer_1(nc, e, last_r, h_t, q_t, k_t, v)
            units = []
            for b in range(TX):
                lo, hi = max(0, b - 1), min(TX, b + 2)
                tiles = [*range(TC), *range(TC + lo, TC + hi)]
                for head in range(NH):
                    kv = head // 4
                    keys = []
                    for j0 in range(0, len(tiles), 4):
                        j = j0
                        while j < min(j0 + 4, len(tiles)):
                            k = j
                            while k + 1 < min(j0 + 4, len(tiles)) and tiles[k + 1] == tiles[k] + 1:
                                k += 1
                            keys.append((j * P, k_t[:, head % 2, kv, tiles[j] * P:(tiles[k] + 1) * P],
                                         (k - j + 1) * P))
                            j = k + 1
                    units.append(dict(
                        q=q_t[:, head // 2, b * P:(b + 1) * P], keys=keys,
                        width=len(tiles) * P, mask=b, mask0=0, head=head,
                        values=[v[:, j, kv * HD:(kv + 1) * HD] for j in tiles]))
            masked_attention(
                nc, e, "swa", units, [TX, 640], e["c_band"].rearrange("b p n -> p b n"),
                [(0, e["b_sink"][0])],
                lambda g: o[:, g // 2, (g % 2) * NCHUNK:(g % 2 + 1) * NCHUNK].rearrange(
                    "p (h d) -> p h d", d=HD))
        project_out(nc, e, "out1", o, stream, None, None, 1.0, e["b_w_o"][0], mod_part(e, 1, 2),
                    e["norm2_g"][1], norm_vectors(e, 1, 3), store=e["h_dram"],
                    router=(1, logits))
    route(nc, e, 1, stream, logits, r)
    logits_scope.close()
    experts(nc, e, 1, TX, r)
    return r


RUNS2 = [(0, 8), (1184, 8), (1952, 6)]
GAINS2 = [("moba_q_g_2", 0, 4), ("moba_k_g_2", 256, 4), ("dil_q_g_2", 1184, 4),
          ("dil_k_g_2", 1440, 4), ("swa_q_g_2", 1952, 4), ("swa_k_g_2", 2208, 2)]
LATENTS = [("mla_qlat_g_2", 768, 256), ("mla_kvlat_g_2", 1024, 128)]
ROPE_COLS = (1152, 32)
VALUES2 = (512, 1696, 2336)
QK = 96


def heads_of(ap, width):
    return ap.rearrange("p t (h d) -> p t h d", d=width)


def over(ap, n):
    return ap.unsqueeze(3).broadcast_to([*ap.shape, n])


def gain_over(ap, t, h):
    return ap.unsqueeze(1).unsqueeze(1).broadcast_to([ap.shape[0], t, h, ap.shape[1]])


def enter_block_2(nc, e, r, buffer, hh, mq, mk, mv):
    chunks = [(n0, min(NCHUNK, QKV2 - n0)) for n0 in range(0, QKV2, NCHUNK)]
    n_chunks = len(chunks)
    ys = buffer[:, 0:2 * D].rearrange("p (a d) -> p a d", a=2)
    h, gates = buffer[:, 2 * D:3 * D], buffer[:, 3 * D:4 * D]
    with Phase(nc, "in2") as ph:
        w = ph.sb("w", [P, KD, QKV2])
        gf, g = ph.sb("gf", [P, D]), ph.sb("g", [P, D])
        h_tile = ph.sb("h_tile", [P, KD, P])
        sq = ph.sb("sq", [P, QKV2])
        runs = ph.sb("runs", [P, 32])
        n_ss, n_std, n_rstd, n_tmp = (ph.sb(x, [P, 2, TX]) for x in ("n_ss", "n_std", "n_rstd", "n_tmp"))
        ss, std, rstd, tmp = (ph.sb(x, [P, TX, 24]) for x in ("ss", "std", "rstd", "tmp"))
        gains, lat_g = ph.sb("gains", [P, 6, HD]), ph.sb("lat_g", [P, 384])
        eps = ph.sb("eps", [P, 1])
        w_uq, w_ukv = ph.sb("w_uq", [P, 2, 4 * QK]), ph.sb("w_ukv", [P, 4 * P])
        lat_t = ph.sb("lat_t", [P, 3, P])
        tp = [ph.ps(f"tp{i}", [P, 4, P]) for i in range(2)]
        acc = [ph.ps(f"acc{i}", [P, NCHUNK]) for i in range(3)]
        lat_tp, pq, pkv = ph.ps("lat_tp", [P, 3, P]), ph.ps("pq", [P, 4 * QK]), ph.ps("pkv", [P, 4 * P])
        names = ("gates_in norm_in const_in latent_in y_in combined finaled h_done sq_done summed std_done "
                 "eps_done tp_done tp_read mm_done hh_read lat_done lat_tp_done lat_t_done q_done "
                 "kv_done q_read kv_read step")
        s = {x: ph.sem(x) for x in names.split()}
        loaded = [ph.sem(f"loaded{i}") for i in range(n_chunks)]
        block = ph.block()
        order = [("final", 0), ("norm", 0)]
        for i in range(TX + 1):
            if i >= 1:
                order.append(("heads", i - 1))
            if i + 1 < TX:
                order += [("final", i + 1), ("norm", i + 1)]
        place = {x: n for n, x in enumerate(order)}
        roots = {}
        count = 0
        for x in order:
            count += 3 if x[0] == "heads" else 1
            roots[x] = count

        @block.sync
        def _(sp):
            src = e["y_dram"].rearrange("(a t p) d -> t p a d", a=2, p=P)
            view = e["w_in_2"][0].rearrange("(k p) n -> p k n", p=P)
            sp.dma_start(ys, src[TC]).then_inc(s["y_in"], 16)
            sp.dma_start(gates, bcast_rows(mod_part(e, 1, 5)(0))).then_inc(s["gates_in"], 16)
            sp.dma_start(gf[:], bcast_rows(e["final_g"])).then_inc(s["norm_in"], 16)
            sp.dma_start(g[:], bcast_rows(e["attn_norm_g_2"][0])).then_inc(s["norm_in"], 16)
            for c, (n0, width) in enumerate(chunks):
                sp.dma_start(w[:, :, n0:n0 + width], view[:, :, n0:n0 + width]).then_inc(loaded[c], 16)
            for j, (name, _, _) in enumerate(GAINS2):
                sp.dma_start(gains[:, j, :], bcast_rows(e["small"][name])).then_inc(s["const_in"], 16)
            for name, c0, width in LATENTS:
                sp.dma_start(lat_g[:, c0 - 768:c0 - 768 + width],
                             bcast_rows(e["small"][name])).then_inc(s["const_in"], 16)
            sp.dma_start(w_uq[:], e["mla_w_uq_2"][0].rearrange("(k p) n -> p k n", p=P)).then_inc(
                s["latent_in"], 16)
            sp.dma_start(w_ukv[:], e["mla_w_ukv_2"][0]).then_inc(s["latent_in"], 16)
            for i in range(1, TX):
                sp.wait_ge(s["combined"], i)
                sp.dma_start(ys, src[TC + i]).then_inc(s["y_in"], 16)

        @block.scalar
        def _(act):
            def square(kind, i, src):
                n = place[kind, i]
                if n:
                    act.wait_ge(s["summed"], n)
                nc.scalar.activation(sq[:, 0:src.shape[1]], src, ACT.Square).then_inc(s["sq_done"], 1)

            def root(kind, i, dst, src, width):
                act.wait_ge(s["summed"], place[kind, i] + 1)
                nc.scalar.activation(dst, src, ACT.Sqrt, scale=1.0 / width, bias=eps[:]).then_inc(
                    s["std_done"], 1)

            def final(i):
                act.wait_ge(s["combined"], i + 1)
                square("final", i, e["res"][:, TC + i, :])
                root("final", i, n_std[:, 0, i:i + 1], n_ss[:, 0, i:i + 1], D)

            def norm(i):
                act.wait_ge(s["finaled"], i + 1)
                square("norm", i, e["res"][:, TC + i, :])
                root("norm", i, n_std[:, 1, i:i + 1], n_ss[:, 1, i:i + 1], D)

            def heads(i):
                act.wait_ge(s["hh_read"], n_chunks * (i + 1))
                square("heads", i, hh[:, i, :])
                root("heads", i, std[:, i, 0:22], ss[:, i, 0:22], HD)
                for j, (_, _, width) in enumerate(LATENTS):
                    root("heads", i, std[:, i, 22 + j:23 + j], ss[:, i, 22 + j:23 + j], width)

            def copy_h(i):
                for half in range(2):
                    act.wait_ge(s["tp_done"], 2 * i + half + 1)
                    if i >= 1:
                        act.wait_ge(s["mm_done"], n_chunks * i)
                    nc.scalar.copy(h_tile[:, 4 * half:4 * half + 4, :], tp[half][:]).then_inc(
                        s["tp_read"], 1)

            def copy_hh(i, c):
                n0, width = chunks[c]
                j = i * n_chunks + c
                act.wait_ge(s["mm_done"], j + 1)
                nc.scalar.copy(hh[:, i, n0:n0 + width], acc[j % 3][:, 0:width]).then_inc(s["hh_read"], 1)

            def copy_latents(i):
                act.wait_ge(s["lat_tp_done"], i + 1)
                if i >= 1:
                    act.wait_ge(s["kv_done"], i)
                nc.scalar.copy(lat_t[:], lat_tp[:]).then_inc(s["lat_t_done"], 1)

            def copy_mq(i):
                act.wait_ge(s["q_done"], i + 1)
                nc.scalar.copy(mq[:, i, :, :].rearrange("p h d -> p (h d)"), pq[:]).then_inc(
                    s["q_read"], 1)

            act.wait_ge(s["eps_done"], 1)
            final(0)
            norm(0)
            copy_h(0)
            for i in range(TX + 1):
                if i >= 1:
                    heads(i - 1)
                if i < TX:
                    copy_hh(i, 0)
                if i + 1 < TX:
                    final(i + 1)
                if i < TX:
                    copy_hh(i, 1)
                    copy_hh(i, 2)
                if i + 1 < TX:
                    norm(i + 1)
                if i >= 1:
                    copy_latents(i - 1)
                if i < TX:
                    copy_hh(i, 3)
                if i >= 1:
                    copy_mq(i - 1)
                if i < TX:
                    copy_hh(i, 4)
                if i + 1 < TX:
                    copy_h(i + 1)

        @block.vector
        def _(dve):
            v = nc.vector
            link = Chain(dve, s["step"])
            v.memset(eps[:], EPS).then_inc(s["eps_done"], 1)

            def combine(i):
                res = e["res"][:, TC + i, :]
                a, b = ys[:, 0, :], ys[:, 1, :]
                dve.wait_ge(s["y_in"], 16 * (i + 1))
                link(v.tensor_scalar(a, a, r["weight"][:, 0, i:i + 1], None, ALU.mult))
                link(v.scalar_tensor_tensor(a, b, r["weight"][:, 1, i:i + 1], a, ALU.mult, ALU.add))
                link(v.tensor_tensor(a, a, gates, ALU.mult))
                v.tensor_tensor(res, res, a, ALU.add).then_inc(s["combined"], 1)

            def inverse_root(kind, i):
                z, one = (0 if kind == "final" else 1), slice(i, i + 1)
                dve.wait_ge(s["sq_done"], place[kind, i] + 1)
                link(v.tensor_reduce(runs[:], sq[:, 0:D].rearrange("p (a b) -> p a b", b=32), AX.X,
                                     ALU.add))
                v.tensor_reduce(n_ss[:, z, one], runs[:], AX.X, ALU.add).then_inc(s["summed"], 1)
                dve.wait_ge(s["summed"], place[kind, i] + 1)
                dve.wait_ge(s["std_done"], roots[kind, i])
                rsqrt_mean(v, link, n_rstd[:, z, one], n_std[:, z, one], n_ss[:, z, one],
                           n_tmp[:, z, one], 1.0 / D)

            def norms(i):
                res, one = e["res"][:, TC + i, :], slice(i, i + 1)
                inverse_root("final", i)
                v.scalar_tensor_tensor(res, res, n_rstd[:, 0, one], gf[:], ALU.mult,
                                       ALU.mult).then_inc(s["finaled"], 1)
                inverse_root("norm", i)
                if i >= 1:
                    dve.wait_ge(s["tp_done"], 2 * i)
                v.scalar_tensor_tensor(h, res, n_rstd[:, 1, one], g[:], ALU.mult,
                                       ALU.mult).then_inc(s["h_done"], 1)

            def heads(i):
                dve.wait_ge(s["sq_done"], place["heads", i] + 1)
                h0 = 0
                for c0, n in RUNS2:
                    link(v.tensor_reduce(ss[:, i, h0:h0 + n],
                                         sq[:, c0:c0 + n * HD].rearrange("p (h d) -> p h d", d=HD),
                                         AX.X, ALU.add))
                    h0 += n
                link(v.tensor_reduce(ss[:, i, 22:23], sq[:, 768:1024], AX.X, ALU.add))
                v.tensor_reduce(ss[:, i, 23:24], sq[:, 1024:1152], AX.X, ALU.add).then_inc(
                    s["summed"], 1)
                dve.wait_ge(s["std_done"], roots["heads", i])
                for j, (_, c0, width) in enumerate(LATENTS):
                    col = slice(22 + j, 23 + j)
                    rsqrt_mean(v, link, rstd[:, i, col], std[:, i, col], ss[:, i, col], tmp[:, i, col],
                               1.0 / width)
                    x = hh[:, i, c0:c0 + width]
                    v.scalar_tensor_tensor(x, x, rstd[:, i, col],
                                           lat_g[:, c0 - 768:c0 - 768 + width], ALU.mult,
                                           ALU.mult).then_inc(s["lat_done"], 1)
                rsqrt_mean(v, link, rstd[:, i, 0:22], std[:, i, 0:22], ss[:, i, 0:22],
                           tmp[:, i, 0:22], 1.0 / HD)
                h0 = 0
                for c0, n in RUNS2:
                    x = hh[:, i, c0:c0 + n * HD].rearrange("p (h d) -> p h d", d=HD)
                    link(v.tensor_tensor(x, x, inner(rstd[:, i, h0:h0 + n], HD), ALU.mult))
                    h0 += n
                for j, (_, c0, n) in enumerate(GAINS2):
                    x = hh[:, i, c0:c0 + n * HD].rearrange("p (h d) -> p h d", d=HD)
                    link(v.tensor_tensor(x, x, middle(gains[:, j, :], n), ALU.mult))

            def keys_and_values(i):
                dve.wait_ge(s["kv_done"], i + 1)
                both = pkv[:].rearrange("p (h d) -> p h d", d=P)
                link(v.tensor_copy(mk[:, i, :, 0:HD], both[:, :, 0:HD]))
                link(v.tensor_copy(mk[:, i, :, HD:QK],
                                   middle(hh[:, i, ROPE_COLS[0]:sum(ROPE_COLS)], 4)))
                v.tensor_copy(mv[:, i, :, :], both[:, :, HD:P]).then_inc(s["kv_read"], 1)

            dve.wait_ge(s["gates_in"], 16)
            combine(0)
            dve.wait_ge(s["norm_in"], 32)
            norms(0)
            dve.wait_ge(s["const_in"], 16 * 8)
            for i in range(TX + 1):
                if i >= 1:
                    heads(i - 1)
                if i + 1 < TX:
                    combine(i + 1)
                    norms(i + 1)
                if i >= 1:
                    keys_and_values(i - 1)

        @block.tensor
        def _(pe):
            def turn_h(i):
                pe.wait_ge(s["h_done"], i + 1)
                for half in range(2):
                    if i >= 1:
                        pe.wait_ge(s["tp_read"], 2 * i - 1 + half)
                    for q in range(4):
                        k = 4 * half + q
                        tr = nc.tensor.transpose(tp[half][:, q, :], h[:, k * P:(k + 1) * P],
                                                 e["ident"][:])
                    tr.then_inc(s["tp_done"], 1)

            def products(i, c):
                n0, width = chunks[c]
                j = i * n_chunks + c
                if i == 0:
                    pe.wait_ge(loaded[c], 16)
                if c == 0:
                    pe.wait_ge(s["tp_read"], 2 * i + 2)
                if j >= 3:
                    pe.wait_ge(s["hh_read"], j - 2)
                for k in range(KD):
                    mm = nc.tensor.matmul(acc[j % 3][:, 0:width], h_tile[:, k, :],
                                          w[:, k, n0:n0 + width], start=(k == 0),
                                          stop=(k == KD - 1))
                mm.then_inc(s["mm_done"], 1)

            def turn_latents(i):
                pe.wait_ge(s["lat_done"], 2 * i + 2)
                if i >= 1:
                    pe.wait_ge(s["lat_t_done"], i)
                for k in range(3):
                    tr = nc.tensor.transpose(lat_tp[:, k, :], hh[:, i, 768 + k * P:768 + (k + 1) * P],
                                             e["ident"][:])
                tr.then_inc(s["lat_tp_done"], 1)

            def expand_latents(i):
                pe.wait_ge(s["lat_t_done"], i + 1)
                if i == 0:
                    pe.wait_ge(s["latent_in"], 32)
                else:
                    pe.wait_ge(s["q_read"], i)
                    pe.wait_ge(s["kv_read"], i)
                for k in range(2):
                    mm = nc.tensor.matmul(pq[:], lat_t[:, k, :], w_uq[:, k, :], start=(k == 0),
                                          stop=(k == 1))
                mm.then_inc(s["q_done"], 1)
                nc.tensor.matmul(pkv[:], lat_t[:, 2, :], w_ukv[:], start=True,
                                 stop=True).then_inc(s["kv_done"], 1)

            turn_h(0)
            for i in range(TX + 1):
                if i < TX:
                    for c in range(3):
                        products(i, c)
                if i >= 1:
                    turn_latents(i - 1)
                if i < TX:
                    products(i, 3)
                if i >= 1:
                    expand_latents(i - 1)
                if i < TX:
                    products(i, 4)
                if i + 1 < TX:
                    turn_h(i + 1)


def key_slot(slot, side):
    return slot if side == 0 else {0: 10, 1: 11, 6: 12, 7: 13, 8: 14, 9: 15}[slot]


def turn_heads(nc, e, hh, mq, mk, q_t, k_t):
    with Phase(nc, "turn2") as ph:
        sq = ph.sb("sq", [P, 2, TX, 4, QK])
        ss, std, rstd, tms = (ph.sb(x, [P, 2, TX, 4]) for x in ("ss", "std", "rstd", "tms"))
        tmp = ph.sb("tmp", [P, TX, 4, 32])
        gains = ph.sb("gains", [P, 2, QK])
        line = ph.sb("line", [P, 2, TX, 32])
        dk = ph.sb("dk", [P, TX, 4, HD])
        eps = ph.sb("eps", [P, 1])
        tp = [ph.ps(f"tp{i}", [P, TX, P]) for i in range(4)]
        names = "const_in sq_done summed std_done eps_done ready dk_done tp_done tp_read zeroed step"
        s = {x: ph.sem(x) for x in names.split()}
        block = ph.block()
        pair = lambda c0, t: hh[:, t, c0:c0 + P]
        jobs = []
        for which, (a, c, d) in enumerate([(0, 1184, 1952), (256, 1440, None)]):
            sc = (1.0, 0.125)[which == 0]
            for j in range(2):
                jobs.append((lambda t, x=a + j * P: pair(x, t), P, which, j, sc))
                jobs.append((lambda t, x=c + j * P: pair(x, t), P, which, 6 + j, sc))
                if d is not None:
                    jobs.append((lambda t, x=d + j * P: pair(x, t), P, which, 8 + j, sc))
                else:
                    jobs.append((lambda t, j=j: dk[:, t, 2 * j:2 * j + 2, :].rearrange(
                        "p h d -> p (h d)"), P, which, 8 + j, sc))
        early = len(jobs)
        zero = [q_t[QK:P, 2:6, :], k_t[QK:P, 2:6, :], k_t[HALVES[1], 0:2, :], k_t[HALVES[1], 6:10, :],
                k_t[HALVES[0], 10:16, :]]
        for which, m in enumerate([mq, mk]):
            for h in range(4):
                jobs.append((lambda t, m=m, h=h: m[:, t, h, :], QK, which, 2 + h,
                             QK ** -0.5 if which == 0 else 1.0))

        @block.sync
        def _(sp):
            sp.dma_start(gains[:, 0, :], bcast_rows(e["small"]["mla_q_g_2"])).then_inc(s["const_in"], 16)
            sp.dma_start(gains[:, 1, :], bcast_rows(e["small"]["mla_k_g_2"])).then_inc(s["const_in"], 16)
            sp.dma_start(line[:], e["c_line"].rearrange("s (t p) d -> p s t d", p=P)).then_inc(
                s["const_in"], 16)

        copies = []
        for _, rows, which, slot, _ in jobs:
            if rows == QK or which == 0:
                copies.append([(slice(0, rows), (q_t, k_t)[which][0:rows, slot, :])])
            else:
                copies.append([(half, k_t[half, key_slot(slot, side), :])
                               for side, half in enumerate(HALVES)])
        reads = [sum(len(c) for c in copies[:j]) for j in range(len(jobs) + 1)]

        @block.gpsimd
        def _(pool):
            for i, dst in enumerate(zero):
                nc.gpsimd.memset(dst, 0.0).then_inc(s["zeroed"], 1)
                pool.wait_ge(s["zeroed"], i + 1)

        @block.scalar
        def _(act):
            for j, m in enumerate([mq, mk]):
                nc.scalar.activation(sq[:, j], m[:], ACT.Square).then_inc(s["sq_done"], 1)
            act.wait_ge(s["eps_done"], 1)
            act.wait_ge(s["summed"], 2)
            nc.scalar.activation(std[:], ss[:], ACT.Sqrt, scale=1.0 / QK, bias=eps[:]).then_inc(
                s["std_done"], 1)
            for j, (_, _, _, _, scale) in enumerate(jobs):
                act.wait_ge(s["tp_done"], j + 1)
                for rows, dst in copies[j]:
                    nc.scalar.activation(dst.rearrange("p (t n) -> p t n", n=P), tp[j % 4][rows],
                                         ACT.Copy, scale=scale).then_inc(s["tp_read"], 1)

        @block.vector
        def _(dve):
            v = nc.vector
            link = Chain(dve, s["step"])
            v.memset(eps[:], EPS).then_inc(s["eps_done"], 1)
            for c in range(2):
                v.tensor_copy(dk[:, :, c:4:2, :], heads_of(hh[:, :, 2208:2336], HD)).then_inc(
                    s["dk_done"], 1)
            for j in range(2):
                dve.wait_ge(s["sq_done"], j + 1)
                v.tensor_reduce(ss[:, j], sq[:, j], AX.X, ALU.add).then_inc(s["summed"], 1)
            dve.wait_ge(s["const_in"], 48)
            dve.wait_ge(s["std_done"], 1)
            rsqrt_mean(v, link, rstd[:], std[:], ss[:], tms[:], 1.0 / QK)
            for j, m in enumerate([mq, mk]):
                link(v.tensor_tensor(m[:], m[:], over(rstd[:, j], QK), ALU.mult))
                link(v.tensor_tensor(m[:], m[:], gain_over(gains[:, j, :], TX, 4), ALU.mult))
                x = m[:, :, :, HD:QK]
                wide = lambda ap: ap.unsqueeze(2).broadcast_to([P, TX, 4, ap.shape[2]])
                link(v.tensor_tensor(tmp[:, :, :, 0:16], x[:, :, :, 16:32],
                                     wide(line[:, 1, :, 0:16]), ALU.mult))
                link(v.tensor_tensor(tmp[:, :, :, 16:32], x[:, :, :, 0:16],
                                     wide(line[:, 1, :, 16:32]), ALU.mult))
                link(v.tensor_tensor(x, x, wide(line[:, 0]), ALU.mult))
                last = v.tensor_tensor(x, x, tmp[:], ALU.add)
                if j == 0:
                    link(last)
                else:
                    last.then_inc(s["ready"], 1)

        @block.tensor
        def _(pe):
            pe.wait_ge(s["dk_done"], 2)
            for j, (src, rows, _, _, _) in enumerate(jobs):
                if j == early:
                    pe.wait_ge(s["ready"], 1)
                if j >= 4:
                    pe.wait_ge(s["tp_read"], reads[j - 3])
                for t in range(TX):
                    tr = nc.tensor.transpose(tp[j % 4][0:rows, t, :], src(t), e["ident"][:])
                tr.then_inc(s["tp_done"], 1)


def mlp(nc, e, h_t):
    with Phase(nc, "mlp") as ph:
        ring, groups = 4, FF // NCHUNK
        w = ph.sb("w", [P, ring, 4096])
        u_t = ph.sb("u_t", [P, FF // P, SEQ])
        acc = [ph.ps(f"acc{i}", [P, NCHUNK]) for i in range(8)]
        loaded = [ph.sem(f"loaded{i}") for i in range(ring)]
        group_used, up_done, up_read = ph.sem("group_used"), ph.sem("up_done"), ph.sem("up_read")
        squared = ph.sem("squared")
        down_done, added, stored = ph.sem("down_done"), ph.sem("added"), ph.sem("stored")
        block = ph.block()
        up_view = e["w_up_2"][0].rearrange("(k p) n -> p k n", p=P)
        down_view = e["w_down_2"][0].rearrange("(k p) n -> p k n", p=P)

        @block.sync
        def _(sp):
            for j in range(2 * groups):
                g = j % groups
                if j >= ring:
                    sp.wait_ge(group_used, j - ring + 1)
                if j < groups:
                    dst = w[:, j % ring, :].rearrange("p (k n) -> p k n", k=KD)
                    src = up_view[:, :, g * NCHUNK:(g + 1) * NCHUNK]
                else:
                    dst = w[:, j % ring, :].rearrange("p (k n) -> p k n", k=4)
                    src = down_view[:, 4 * g:4 * g + 4, :]
                sp.dma_start(dst, src).then_inc(loaded[j % ring], 16)
            rows = e["out"][0].rearrange("(t p) d -> p t d", p=P)
            for t in range(TX):
                sp.wait_ge(added, 2 * t + 2)
                sp.dma_start(rows[:, t, :], e["res"][:, TC + t, :]).then_inc(stored, 16)
            sp.wait_ge(stored, 16 * TX)

        @block.tensor
        def _(pe):
            for j in range(groups):
                pe.wait_ge(loaded[j % ring], 16 * (j // ring + 1))
                wj = w[:, j % ring, :].rearrange("p (k n) -> p k n", k=KD)
                for q in range(4):
                    i = 4 * j + q
                    if i >= 8:
                        pe.wait_ge(up_read, i - 7)
                    for k in range(KD):
                        mm = nc.tensor.matmul(acc[i % 8][:], wj[:, k, q * P:(q + 1) * P],
                                              h_t[:, k, :], start=(k == 0), stop=(k == KD - 1))
                    mm.then_inc(up_done, 1)
                pe.wait_ge(up_done, 4 * j + 4)
                pe.sem_inc(group_used, 1)
            pe.wait_ge(squared, 4 * groups)
            for j in range(groups):
                b = (groups + j) % ring
                pe.wait_ge(loaded[b], 16 * ((groups + j) // ring + 1))
                wj = w[:, b, :].rearrange("p (k n) -> p k n", k=4)
                for q in range(4):
                    f = 4 * j + q
                    for t in range(TX):
                        for c in range(2):
                            mm = nc.tensor.matmul(acc[2 * t + c][:],
                                                  u_t[:, f, t * P:(t + 1) * P],
                                                  wj[:, q, c * NCHUNK:(c + 1) * NCHUNK],
                                                  start=(f == 0), stop=(f == FF // P - 1),
                                                  skip_group_check=True)
                            if f == FF // P - 1:
                                mm.then_inc(down_done, 1)
                            elif q == 3 and (t, c) == (TX - 1, 1):
                                mm.then_inc(group_used, 1)

        @block.scalar
        def _(act):
            for i in range(4 * groups):
                act.wait_ge(up_done, i + 1)
                nc.scalar.activation(u_t[:, i, :], acc[i % 8][:], ACT.Relu).then_inc(up_read, 1)

        @block.vector
        def _(dve):
            for i in range(4 * groups):
                dve.wait_ge(up_read, i + 1)
                nc.vector.tensor_tensor(u_t[:, i, :], u_t[:, i, :], u_t[:, i, :],
                                        ALU.mult).then_inc(squared, 1)
            for i in range(2 * TX):
                t, c = i // 2, i % 2
                dst = e["res"][:, TC + t, c * NCHUNK:(c + 1) * NCHUNK]
                dve.wait_ge(down_done, i + 1)
                nc.vector.tensor_tensor(dst, dst, acc[i][:], ALU.add).then_inc(added, 1)


def block_2(nc, e, r):
    stream = list(range(TC, NT))
    sb = nc.sbuf_tensor
    with sb("c_buffer", [P, TX * D], F32) as buffer:
        o = buffer[:].rearrange("p (t d) -> p t d", t=TX)
        with sb("c_hh", [P, TX, QKV2], F32) as hh, sb("c_mv", [P, TX, 4, HD], F32) as mv, \
                sb("c_mq", [P, TX, 4, QK], F32) as mq, sb("c_mk", [P, TX, 4, QK], F32) as mk, \
                ExitStack() as stack:
            enter_block_2(nc, e, r, buffer, hh, mq, mk, mv)
            q_t = stack.enter_context(sb("c_q", [P, 10, SEQ], F32))
            k_t = stack.enter_context(sb("c_k", [P, 16, SEQ], F32))
            turn_heads(nc, e, hh, mq, mk, q_t, k_t)
            units = []
            for b in range(TX):
                for head in range(NH):
                    kind, h = head // 4, head % 4
                    slot = {0: h // 2, 1: 2 + h, 2: 6 + h // 2, 3: 8 + h // 2}[kind]
                    k_slot = 2 + h if kind == 1 else key_slot(slot, h % 2)
                    first = max(0, b - 1) if kind == 3 else 0
                    width = (b + 1 - first) * P
                    if kind == 1:
                        values = [mv[:, j, h, :] for j in range(first, b + 1)]
                    else:
                        c0 = {0: VALUES2[0] + h * HD, 2: VALUES2[1] + h * HD,
                              3: VALUES2[2] + h // 2 * HD}[kind]
                        values = [hh[:, j, c0:c0 + HD] for j in range(first, b + 1)]
                    units.append(dict(
                        q=q_t[:, slot, b * P:(b + 1) * P],
                        keys=[(0, k_t[:, k_slot, first * P:(b + 1) * P], width)],
                        width=width, mask=(h, 4, 5 + h, 9 + h)[kind], mask0=512 - width,
                        head=head, values=values))
            masked_attention(
                nc, e, "att2", units, [13, 512], e["c_bias2"].rearrange("h p n -> p h n"),
                [(0, e["c_neg"]), (12, e["small"]["swa_sinks_2"])],
                lambda g: o[:, g // 2, (g % 2) * NCHUNK:(g % 2 + 1) * NCHUNK].rearrange(
                    "p (h d) -> p h d", d=HD))
        with sb("m_h", [P, KD, SEQ], F32) as m_h:
            project_out(nc, e, "out2", o, stream, 4, e["group_out_g_2"][0].rearrange("a d -> (a d)"),
                        1.0, e["w_o_2"][0], None, e["mlp_norm_g_2"][0], None, h_t=m_h)
            mlp(nc, e, m_h)


def build(nc, e, upto=3):
    e["res"] = nc.alloc_sbuf_tensor("res", [P, NT, D], F32).ap()
    e["ident"] = nc.alloc_sbuf_tensor("ident_sb", [P, P], F32).ap()
    e["ones"] = nc.alloc_sbuf_tensor("ones_sb", [P, P], F32).ap()
    e["rstd"] = nc.alloc_sbuf_tensor("rstd", [P, NT], F32).ap()
    modulation(nc, e)
    if upto >= 1:
        with ExitStack() as stack:
            r = layer_0(nc, e, stack)
            if upto >= 2:
                r = layer_1(nc, e, stack, r)
            if upto >= 3:
                block_2(nc, e, r)



_INS = ["x", "c", "ctx", "c_ctx", "mod_w", "mod_b", "norm1_g", "norm2_g", "a_w_qkv", "a_w_o",
        "a_lam", "a_subln_g", "b_w_qkv", "b_w_o", "b_sink", "moe_router_g", "moe_router_g_b",
        "moe_router_e", "moe_router_e_b", "moe_w_gate", "moe_w_up", "moe_w_down", "final_g",
        "attn_norm_g_2", "w_in_2", "mla_w_uq_2", "mla_w_ukv_2", "group_out_g_2", "w_o_2",
        "mlp_norm_g_2", "w_up_2", "w_down_2"]
_SMALL = ["moba_q_g_2", "moba_k_g_2", "mla_qlat_g_2", "mla_kvlat_g_2", "mla_q_g_2", "mla_k_g_2",
          "dil_q_g_2", "dil_k_g_2", "swa_q_g_2", "swa_k_g_2", "swa_sinks_2"]


def kernel(**inputs):
    import concourse.bacc as bacc
    from concourse.bass_utils import run_bass_kernel_spmd

    nc = bacc.Bacc("TRN2", target_bir_lowering=False, num_devices=1)
    arrays, e = {}, {"small": {}}

    def give(name, a):
        arrays[name] = np.ascontiguousarray(a)
        return nc.dram_tensor(name, a.shape, F32, kind="ExternalInput").ap()

    for name in _INS:
        e[name] = give(f"in_{name}", inputs[name])
    for name in _SMALL:
        e["small"][name] = give(f"in_{name}", inputs[name])[0]
    for name, a in constants().items():
        e[f"c_{name}"] = give(f"const_{name}", a)
    e["out"] = nc.dram_tensor("result", (1, SEQ, D), F32, kind="ExternalOutput").ap()
    e["mod_dram"] = nc.dram_tensor("mod_scratch", (2, LAYERS * 6 * D), F32, kind="Internal").ap()
    e["h_dram"] = nc.dram_tensor("moe_tokens", (NT * P, D), F32, kind="Internal").ap()
    e["y_dram"] = nc.dram_tensor("moe_results", (2 * NT * P, D), F32, kind="Internal").ap()
    build(nc, e)
    r = run_bass_kernel_spmd(nc, [arrays], core_ids=[0])
    return r.results[0]["result"]
```
